# Optimizing a Trainium2 kernel written in Bass

```python
import math
import jax, jax.numpy as jnp
from jax import lax
import numpy as np

D_MODEL = 1024
BATCH = 1
SEQ = 256
DEPTH = 2

N_MIXERS = 2
HEAD_DIM = 64
N_HEADS = D_MODEL // HEAD_DIM
N_RWKV = (DEPTH + 1) // 2
N_MOBA = DEPTH // 2
DECAY_LORA = max(32, int(round(1.8 * D_MODEL ** 0.5 / 32)) * 32)
AAA_LORA = max(32, int(round(1.8 * D_MODEL ** 0.5 / 32)) * 32)
GATE_LORA = max(32, int(round(0.6 * D_MODEL ** 0.8 / 32)) * 32)
GN_EPS = HEAD_DIM * 1e-5
MOBA_BLOCK = 256
MOBA_TOPK = 3
Q_CHUNK = 128
ROPE_THETA = 10000.0
D_FF = -(-8 * D_MODEL // (3 * 256)) * 256
ALPHA = (2 * DEPTH) ** 0.25
BETA = (8 * DEPTH) ** -0.25
LN_EPS = 1e-5


def layer_norm(x, g, b):
    xf = x.astype(jnp.float32)
    mu = xf.mean(-1, keepdims=True)
    var = jnp.square(xf - mu).mean(-1, keepdims=True)
    return ((xf - mu) * lax.rsqrt(var + LN_EPS) * g + b).astype(x.dtype)

def swiglu_ffn(x, w_in, w_down):
    gate, up = jnp.split(x @ w_in, 2, axis=-1)
    return (jax.nn.silu(gate) * up) @ w_down

def time_shift(x):
    return jnp.pad(x, ((0, 0), (1, 0), (0, 0)))[:, :-1, :]

def rwkv7_time_mix(x, mu, w_rkv, w0, w1, w2, a0, a1, a2, g1, g2, k_k, k_a, r_k, gn_g, gn_b, w_o):
    B, T, C = x.shape
    H, N = N_HEADS, HEAD_DIM
    f32 = jnp.float32
    xx = time_shift(x) - x
    xr, xw, xk, xv, xa, xg = [x + xx * mu[n] for n in range(6)]
    r, k, v = jnp.einsum('nbtc,ncd->nbtd', jnp.stack([xr, xk, xv]), w_rkv)
    w = -jax.nn.softplus(-(w0 + jnp.tanh(xw @ w1) @ w2)) - 0.5
    a = jax.nn.sigmoid(a0 + (xa @ a1) @ a2)
    g = jax.nn.sigmoid(xg @ g1) @ g2
    heads = lambda t: t.reshape(B, T, H, N).astype(f32)
    kk = heads(k * k_k)
    kk = kk / jnp.maximum(jnp.sqrt(jnp.sum(kk * kk, -1, keepdims=True)), 1e-12)
    k = k * (1 + (a - 1) * k_a)
    rh, kh, vh, ah = heads(r), heads(k), heads(v), heads(a)
    decay = jnp.exp(-jnp.exp(heads(w)))

    def step(S, inp):
        r_t, w_t, k_t, v_t, kk_t, b_t = inp
        sa = jnp.einsum('bhvk,bhk->bhv', S, -kk_t)
        S = S * w_t[:, :, None, :] + sa[..., None] * b_t[:, :, None, :] + v_t[..., None] * k_t[:, :, None, :]
        return S, jnp.einsum('bhvk,bhk->bhv', S, r_t)

    to_time = lambda t: jnp.swapaxes(t, 0, 1)
    S0 = jnp.zeros((B, H, N, N), f32)
    _, y = lax.scan(step, S0, tuple(to_time(t) for t in (rh, decay, kh, vh, kk, kk * ah)))
    y = to_time(y)
    mean = y.mean(-1, keepdims=True)
    var = jnp.square(y - mean).mean(-1, keepdims=True)
    y = ((y - mean) * lax.rsqrt(var + GN_EPS)).reshape(B, T, C) * gn_g + gn_b
    bonus = jnp.sum(rh * kh * r_k, -1, keepdims=True) * vh
    y = (y + bonus.reshape(B, T, C)).astype(x.dtype)
    return (y * g) @ w_o

def rope_tables(T):
    inv = ROPE_THETA ** (-jnp.arange(0, HEAD_DIM, 2, dtype=jnp.float32) / HEAD_DIM)
    ang = jnp.arange(T, dtype=jnp.float32)[:, None] * inv[None, :]
    return jnp.cos(ang), jnp.sin(ang)

def apply_rope(t, cos, sin):
    t1, t2 = jnp.split(t, 2, axis=-1)
    return jnp.concatenate([t1 * cos - t2 * sin, t2 * cos + t1 * sin], axis=-1)

def moba_attention(x, w_qkv, w_o):
    B, T, C = x.shape
    H, Dh = N_HEADS, HEAD_DIM
    f32 = jnp.float32
    qkv = (x @ w_qkv).reshape(B, T, 3, H, Dh)
    q, k, v = [jnp.transpose(qkv[:, :, n], (0, 2, 1, 3)).astype(f32) for n in range(3)]
    cos, sin = rope_tables(T)
    q = apply_rope(q, cos, sin) * (Dh ** -0.5)
    k = apply_rope(k, cos, sin)
    NB = -(-T // MOBA_BLOCK)
    K = min(MOBA_TOPK, NB)
    pad = NB * MOBA_BLOCK - T
    kb = jnp.pad(k, ((0, 0), (0, 0), (0, pad), (0, 0))).reshape(B, H, NB, MOBA_BLOCK, Dh)
    vb = jnp.pad(v, ((0, 0), (0, 0), (0, pad), (0, 0))).reshape(B, H, NB, MOBA_BLOCK, Dh)
    k_mean = kb.mean(axis=3)
    bi = jnp.arange(B)[:, None, None, None]
    hi = jnp.arange(H)[None, :, None, None]
    blk_ids = jnp.arange(NB)
    key_off = jnp.arange(MOBA_BLOCK)
    q_off = jnp.arange(Q_CHUNK)

    def attend_chunk(c):
        q0 = c * Q_CHUNK
        own = q0 // MOBA_BLOCK
        q_c = lax.dynamic_slice_in_dim(q, q0, Q_CHUNK, axis=2)
        gate = jnp.einsum('bhqd,bhnd->bhqn', q_c, k_mean)
        gate = jnp.where(blk_ids < own, gate, -jnp.inf)
        _, sel = lax.top_k(gate, K)
        valid = sel < own
        k_sel = kb[bi, hi, sel]
        v_sel = vb[bi, hi, sel]
        s_sel = jnp.einsum('bhqd,bhqksd->bhqks', q_c, k_sel)
        s_sel = jnp.where(valid[..., None], s_sel, -jnp.inf).reshape(B, H, Q_CHUNK, K * MOBA_BLOCK)
        k_own = lax.dynamic_index_in_dim(kb, own, axis=2, keepdims=False)
        v_own = lax.dynamic_index_in_dim(vb, own, axis=2, keepdims=False)
        s_own = jnp.einsum('bhqd,bhsd->bhqs', q_c, k_own)
        causal = (own * MOBA_BLOCK + key_off)[None, :] <= (q0 + q_off)[:, None]
        s_own = jnp.where(causal, s_own, -jnp.inf)
        p = jax.nn.softmax(jnp.concatenate([s_sel, s_own], axis=-1), axis=-1)
        p_sel = p[..., :K * MOBA_BLOCK].reshape(B, H, Q_CHUNK, K, MOBA_BLOCK)
        p_own = p[..., K * MOBA_BLOCK:]
        return (jnp.einsum('bhqks,bhqksd->bhqd', p_sel, v_sel)
                + jnp.einsum('bhqs,bhsd->bhqd', p_own, v_own))

    out = lax.map(attend_chunk, jnp.arange(T // Q_CHUNK))
    out = jnp.transpose(out, (1, 0, 3, 2, 4)).reshape(B, T, C)
    return out.astype(x.dtype) @ w_o

def first_inputs(seed: int = 0) -> dict:
    key = jax.random.key(seed)
    ks = iter(jax.random.split(key, 32))
    C, H, N, F = D_MODEL, N_HEADS, HEAD_DIM, D_FF
    nrm = lambda shape, s: jax.random.normal(next(ks), shape, jnp.float32) * s
    return {
        'x': nrm((BATCH, SEQ, C), 1.0),
        'rwkv_mu': jax.random.uniform(next(ks), (N_RWKV, 6, C), jnp.float32),
        'rwkv_w_rkv': nrm((N_RWKV, 3, C, C), C ** -0.5),
        'rwkv_w0': jax.random.uniform(next(ks), (N_RWKV, C), jnp.float32, -5.0, 0.5),
        'rwkv_w1': nrm((N_RWKV, C, DECAY_LORA), C ** -0.5),
        'rwkv_w2': nrm((N_RWKV, DECAY_LORA, C), 0.5 * DECAY_LORA ** -0.5),
        'rwkv_a0': nrm((N_RWKV, C), 0.1),
        'rwkv_a1': nrm((N_RWKV, C, AAA_LORA), C ** -0.5),
        'rwkv_a2': nrm((N_RWKV, AAA_LORA, C), 0.5 * AAA_LORA ** -0.5),
        'rwkv_g1': nrm((N_RWKV, C, GATE_LORA), C ** -0.5),
        'rwkv_g2': nrm((N_RWKV, GATE_LORA, C), GATE_LORA ** -0.5),
        'rwkv_k_k': 0.85 + nrm((N_RWKV, C), 0.05),
        'rwkv_k_a': 1.0 + nrm((N_RWKV, C), 0.05),
        'rwkv_r_k': nrm((N_RWKV, H, N), 0.1),
        'rwkv_gn_g': 1.0 + nrm((N_RWKV, C), 0.05),
        'rwkv_gn_b': nrm((N_RWKV, C), 0.02),
        'rwkv_w_o': nrm((N_RWKV, C, C), BETA * C ** -0.5),
        'moba_w_qkv': nrm((N_MOBA, C, 3 * C), C ** -0.5),
        'moba_w_o': nrm((N_MOBA, C, C), BETA * C ** -0.5),
        'ffn_w_in': nrm((DEPTH, C, 2 * F), C ** -0.5),
        'ffn_w_down': nrm((DEPTH, F, C), BETA * F ** -0.5),
        'ln_mix_g': 1.0 + nrm((DEPTH, C), 0.05),
        'ln_mix_b': nrm((DEPTH, C), 0.02),
        'ln_ffn_g': 1.0 + nrm((DEPTH, C), 0.05),
        'ln_ffn_b': nrm((DEPTH, C), 0.02),
    }

def first_block(x, rwkv_mu, rwkv_w_rkv, rwkv_w0, rwkv_w1, rwkv_w2, rwkv_a0, rwkv_a1, rwkv_a2,
              rwkv_g1, rwkv_g2, rwkv_k_k, rwkv_k_a, rwkv_r_k, rwkv_gn_g, rwkv_gn_b, rwkv_w_o,
              moba_w_qkv, moba_w_o, ffn_w_in, ffn_w_down, ln_mix_g, ln_mix_b, ln_ffn_g, ln_ffn_b):
    for i in range(DEPTH):
        j = i // N_MIXERS
        if i % N_MIXERS == 0:
            h = rwkv7_time_mix(x, rwkv_mu[j], rwkv_w_rkv[j], rwkv_w0[j], rwkv_w1[j], rwkv_w2[j],
                               rwkv_a0[j], rwkv_a1[j], rwkv_a2[j], rwkv_g1[j], rwkv_g2[j],
                               rwkv_k_k[j], rwkv_k_a[j], rwkv_r_k[j], rwkv_gn_g[j], rwkv_gn_b[j],
                               rwkv_w_o[j])
        else:
            h = moba_attention(x, moba_w_qkv[j], moba_w_o[j])
        x = layer_norm(ALPHA * x + h, ln_mix_g[i], ln_mix_b[i])
        x = layer_norm(ALPHA * x + swiglu_ffn(x, ffn_w_in[i], ffn_w_down[i]), ln_ffn_g[i], ln_ffn_b[i])
    return x


DEPTH_2 = 1

N_MEM = 256
CONV_CH = D_MODEL
CONV_WIDTH = 31
N_HEADS_2 = 8
HEAD_DIM_2 = D_MODEL // N_HEADS_2
ATTN_W = N_HEADS_2 * HEAD_DIM_2
IDX_HEADS = 8
IDX_DIM = 64
TOPK_MAX = 256
Q_BLOCK = 128
X_HEADS = 4
X_HEAD_DIM = 128
X_W = X_HEADS * X_HEAD_DIM
D_FF_2 = 4 * D_MODEL
EPS = 1e-6

IN_SIZES = (CONV_CH, CONV_CH, ATTN_W, ATTN_W, ATTN_W, IDX_HEADS * IDX_DIM, IDX_DIM, IDX_HEADS, D_MODEL, D_MODEL)
IN_WIDTH = sum(IN_SIZES)


def _rmsnorm(x, g):
    x32 = x.astype(jnp.float32)
    y = x32 * lax.rsqrt(jnp.mean(x32 * x32, axis=-1, keepdims=True) + EPS)
    return y.astype(x.dtype) * g

def _layernorm(x, g, b):
    x32 = x.astype(jnp.float32)
    mu = jnp.mean(x32, axis=-1, keepdims=True)
    xc = x32 - mu
    var = jnp.mean(xc * xc, axis=-1, keepdims=True)
    return (xc * lax.rsqrt(var + EPS)).astype(x.dtype) * g + b

def _split_cols(z, sizes):
    offs = []
    acc = 0
    for s in sizes[:-1]:
        acc += s
        offs.append(acc)
    return jnp.split(z, offs, axis=-1)

def _conformer_conv(a, gate, conv_w, conv_b, ln_g, ln_b, w_out):
    u = a * jax.nn.sigmoid(gate)
    u = lax.conv_general_dilated(
        u, conv_w[:, None, :].astype(u.dtype), window_strides=(1,),
        padding=[(CONV_WIDTH - 1, 0)], dimension_numbers=('NWC', 'WIO', 'NWC'),
        feature_group_count=CONV_CH) + conv_b
    u = jax.nn.silu(_layernorm(u, ln_g, ln_b))
    return u @ w_out

def _dsa_attention(q, k, v, qi, ki, wi):
    B, L = q.shape[0], q.shape[1]
    k_top = min(TOPK_MAX, L // 4)
    nb = L // Q_BLOCK
    key_pos = jnp.arange(L)
    ki32 = ki.astype(jnp.float32)

    def to_blocks(a):
        return a.reshape((B, nb, Q_BLOCK) + a.shape[2:]).swapaxes(0, 1)

    def block(args):
        qb, qib, wb, bi = args
        q_pos = bi * Q_BLOCK + jnp.arange(Q_BLOCK)
        causal = key_pos[None, :] <= q_pos[:, None]
        logits = jnp.einsum('bqhd,bsd->bqhs', qib.astype(jnp.float32), ki32) * (IDX_DIM ** -0.5)
        score = jnp.einsum('bqh,bqhs->bqs', wb.astype(jnp.float32), jax.nn.relu(logits))
        score = jnp.where(causal[None], score, -jnp.inf)
        _, idx = lax.top_k(score, k_top)
        valid = idx <= q_pos[None, :, None]
        k_sel = jax.vmap(lambda kb, ib: kb[ib])(k, idx)
        v_sel = jax.vmap(lambda vb, ib: vb[ib])(v, idx)
        s = jnp.einsum('bqhd,bqkhd->bhqk', qb.astype(jnp.float32), k_sel.astype(jnp.float32)) * (HEAD_DIM_2 ** -0.5)
        s = jnp.where(valid[:, None], s, -jnp.inf)
        p = jax.nn.softmax(s, axis=-1)
        return jnp.einsum('bhqk,bqkhd->bqhd', p.astype(v.dtype), v_sel)

    out = lax.map(block, (to_blocks(q), to_blocks(qi), to_blocks(wi), jnp.arange(nb)))
    return out.swapaxes(0, 1).reshape(B, L, ATTN_W)

def _cross_attention(hn, memn, wq, wkv, wo):
    B, L, _ = hn.shape
    q = (hn @ wq).reshape(B, L, X_HEADS, X_HEAD_DIM)
    kv = memn @ wkv
    k, v = jnp.split(kv, 2, axis=-1)
    k = k.reshape(B, N_MEM, X_HEADS, X_HEAD_DIM)
    v = v.reshape(B, N_MEM, X_HEADS, X_HEAD_DIM)
    s = jnp.einsum('bshd,bmhd->bhsm', q.astype(jnp.float32), k.astype(jnp.float32)) * (X_HEAD_DIM ** -0.5)
    p = jax.nn.softmax(s, axis=-1)
    o = jnp.einsum('bhsm,bmhd->bshd', p.astype(v.dtype), v).reshape(B, L, X_W)
    return o @ wo

def second_inputs(seed: int = 0) -> dict:
    key = jax.random.key(seed)
    ks = jax.random.split(key, 24)
    f32 = jnp.float32

    def w(k, shape, fan_in):
        return jax.random.normal(k, shape, f32) * (fan_in ** -0.5)

    def gain(k, shape):
        return 1.0 + 0.02 * jax.random.normal(k, shape, f32)

    def bias(k, shape):
        return 0.02 * jax.random.normal(k, shape, f32)

    return {
        "x": jax.random.normal(ks[0], (BATCH, SEQ, D_MODEL), f32),
        "mem": jax.random.normal(ks[1], (BATCH, N_MEM, D_MODEL), f32),
        "norm_mix_g": gain(ks[2], (DEPTH_2, D_MODEL)),
        "w_in": w(ks[3], (DEPTH_2, D_MODEL, IN_WIDTH), D_MODEL),
        "b_gate": bias(ks[4], (DEPTH_2, 2 * D_MODEL)),
        "conv_w": w(ks[5], (DEPTH_2, CONV_WIDTH, CONV_CH), CONV_WIDTH),
        "conv_b": bias(ks[6], (DEPTH_2, CONV_CH)),
        "conv_ln_g": gain(ks[7], (DEPTH_2, CONV_CH)),
        "conv_ln_b": bias(ks[8], (DEPTH_2, CONV_CH)),
        "w_conv_out": w(ks[9], (DEPTH_2, CONV_CH, D_MODEL), CONV_CH),
        "w_attn_out": w(ks[10], (DEPTH_2, ATTN_W, D_MODEL), ATTN_W),
        "w_mix_out": w(ks[11], (DEPTH_2, D_MODEL, D_MODEL), D_MODEL),
        "norm_x_g": gain(ks[12], (DEPTH_2, D_MODEL)),
        "norm_mem_g": gain(ks[13], (DEPTH_2, D_MODEL)),
        "wx_q": w(ks[14], (DEPTH_2, D_MODEL, X_W), D_MODEL),
        "wx_kv": w(ks[15], (DEPTH_2, D_MODEL, 2 * X_W), D_MODEL),
        "wx_o": w(ks[16], (DEPTH_2, X_W, D_MODEL), X_W),
        "norm_ffn_g": gain(ks[17], (DEPTH_2, D_MODEL)),
        "w_ff1": w(ks[18], (DEPTH_2, D_MODEL, D_FF_2), D_MODEL),
        "w_ff2": w(ks[19], (DEPTH_2, D_FF_2, D_MODEL), D_FF_2),
        "norm_final_g": gain(ks[20], (D_MODEL,)),
    }

def second_block(x, mem, norm_mix_g, w_in, b_gate, conv_w, conv_b, conv_ln_g, conv_ln_b,
              w_conv_out, w_attn_out, w_mix_out, norm_x_g, norm_mem_g, wx_q, wx_kv, wx_o,
              norm_ffn_g, w_ff1, w_ff2, norm_final_g):
    B, L, _ = x.shape
    h = x
    for l in range(DEPTH_2):
        n = _rmsnorm(h, norm_mix_g[l])
        z = n @ w_in[l]
        c_a, c_g, q, k, v, qi, ki, wi, gc_logit, ga_logit = _split_cols(z, IN_SIZES)
        bg_conv, bg_attn = jnp.split(b_gate[l], 2)
        g_conv = jax.nn.sigmoid(gc_logit + bg_conv)
        g_attn = jax.nn.sigmoid(ga_logit + bg_attn)
        y_conv = _conformer_conv(c_a, c_g, conv_w[l], conv_b[l], conv_ln_g[l], conv_ln_b[l], w_conv_out[l])
        qh = q.reshape(B, L, N_HEADS_2, HEAD_DIM_2)
        kh = k.reshape(B, L, N_HEADS_2, HEAD_DIM_2)
        vh = v.reshape(B, L, N_HEADS_2, HEAD_DIM_2)
        qih = qi.reshape(B, L, IDX_HEADS, IDX_DIM)
        wih = wi * (IDX_HEADS ** -0.5)
        y_attn = _dsa_attention(qh, kh, vh, qih, ki, wih) @ w_attn_out[l]
        h = h + (g_conv * y_conv + g_attn * y_attn) @ w_mix_out[l]
        h = h + _cross_attention(_rmsnorm(h, norm_x_g[l]), _rmsnorm(mem, norm_mem_g[l]),
                                 wx_q[l], wx_kv[l], wx_o[l])
        hf = _rmsnorm(h, norm_ffn_g[l]) @ w_ff1[l]
        h = h + jnp.square(jax.nn.relu(hf)) @ w_ff2[l]
    return _rmsnorm(h, norm_final_g)


def setup_inputs(seed=0):
    out = dict(first_inputs(seed))
    for name, value in second_inputs(seed + 1).items():
        if name != "x":
            out[name + "_2"] = value
    return out


def reference(
    x, rwkv_mu, rwkv_w_rkv, rwkv_w0, rwkv_w1, rwkv_w2, rwkv_a0, rwkv_a1, rwkv_a2, rwkv_g1,
    rwkv_g2, rwkv_k_k, rwkv_k_a, rwkv_r_k, rwkv_gn_g, rwkv_gn_b, rwkv_w_o, moba_w_qkv, moba_w_o,
    ffn_w_in, ffn_w_down, ln_mix_g, ln_mix_b, ln_ffn_g, ln_ffn_b, mem_2, norm_mix_g_2, w_in_2,
    b_gate_2, conv_w_2, conv_b_2, conv_ln_g_2, conv_ln_b_2, w_conv_out_2, w_attn_out_2,
    w_mix_out_2, norm_x_g_2, norm_mem_g_2, wx_q_2, wx_kv_2, wx_o_2, norm_ffn_g_2, w_ff1_2,
    w_ff2_2, norm_final_g_2,
):
    x = first_block(
        x, rwkv_mu, rwkv_w_rkv, rwkv_w0, rwkv_w1, rwkv_w2, rwkv_a0, rwkv_a1, rwkv_a2, rwkv_g1,
        rwkv_g2, rwkv_k_k, rwkv_k_a, rwkv_r_k, rwkv_gn_g, rwkv_gn_b, rwkv_w_o, moba_w_qkv,
        moba_w_o, ffn_w_in, ffn_w_down, ln_mix_g, ln_mix_b, ln_ffn_g, ln_ffn_b,
    )
    return second_block(
        x, mem_2, norm_mix_g_2, w_in_2, b_gate_2, conv_w_2, conv_b_2, conv_ln_g_2, conv_ln_b_2,
        w_conv_out_2, w_attn_out_2, w_mix_out_2, norm_x_g_2, norm_mem_g_2, wx_q_2, wx_kv_2,
        wx_o_2, norm_ffn_g_2, w_ff1_2, w_ff2_2, norm_final_g_2,
    )


_drawn_inputs = setup_inputs


def setup_inputs(seed=0):
    import zlib

    import numpy as np

    out = dict(_drawn_inputs(seed))
    spreads = {}
    factors = {'rwkv_w1': 5.401,
     'rwkv_w2': 5.311,
     'rwkv_a0': 4.056,
     'rwkv_k_k': 5.147,
     'rwkv_k_a': 3.688,
     'rwkv_gn_g': 3.933,
     'rwkv_gn_b': 6.626,
     'norm_mix_g_2': 3.373,
     'b_gate_2': 8.0,
     'conv_b_2': 3.853,
     'conv_ln_g_2': 7.099,
     'conv_ln_b_2': 7.965,
     'norm_x_g_2': 8.0,
     'norm_mem_g_2': 8.0,
     'norm_ffn_g_2': 9.617,
     'norm_final_g_2': 8.093}
    for name, (base, spread) in spreads.items():
        noise = np.random.default_rng([zlib.crc32(name.encode()), seed]).standard_normal(out[name].shape)
        drawn = base * np.exp(spread * noise) if base else spread * noise
        out[name] = __import__('jax').numpy.asarray(drawn.astype(out[name].dtype))
    for name, factor in factors.items():
        out[name] = (out[name] * factor).astype(out[name].dtype)
    return out
```

```python
from contextlib import ExitStack

import numpy as np
import concourse.bass as bass
from concourse import mybir

F32 = mybir.dt.float32
ALU = mybir.AluOpType
ACT = mybir.ActivationFunctionType
AX = mybir.AxisListType.X

C = 1024
T = 256
KT = 8
FF = 2816
FF2 = 4096
ALPHA = 4 ** 0.25
CDEC = float(np.exp(-0.5))
GN_EPS = 64e-5
LN_EPS = 1e-5
EPS = 1e-6
NEG = -1e30
TAKEN = -3e38

VECS = ['mu0', 'mu1', 'mu2', 'mu3', 'mu4', 'mu5', 'w0h', 'a0h', 'k_k', 'k_a', 'r_k',
        'mixg0', 'mixb0', 'ffng0', 'ffnb0', 'mixg1', 'mixb1', 'ffng1', 'ffnb1',
        'conv_b', 'cln_g', 'cln_b', 'nmix', 'nx', 'nmem', 'nffn', 'bgc', 'bga'] + [f'cw{i}' for i in range(31)]
CST = {}
_at = 0
for _n, _w in [('ident', 128), ('atm', 512), ('lvl', 896), ('m0t', 128), ('bones', 128), ('ones', 128),
               ('sel2', 2), ('pad', 14), ('perm', 128), ('cmask', 384), ('c01', 384), ('cos', 256), ('sin', 256)]:
    CST[_n] = (_at, _w)
    _at += _w
NCST = _at


def constants():
    a = np.zeros((128, NCST), np.float32)
    p = np.arange(128)[:, None]
    f = np.arange(128)[None, :]

    def put(name, v):
        o, w = CST[name]
        a[:, o:o + w] = v

    put('ident', p == f)
    put('atm', np.concatenate([p < f, p <= f, p < f, p <= f], 1))
    put('lvl', np.concatenate([((p >> (l + 1)) == (f >> (l + 1))) & ((p >> l) & 1 == 1) & ((f >> l) & 1 == 0)
                               for l in range(7)], 1))
    put('m0t', ((f >> 1) == (p >> 1)) & (f & 1 == 1) & (p & 1 == 0))
    put('bones', (p // 64) == (f // 64))
    put('ones', 1.0)
    put('sel2', (p // 64) == np.arange(2)[None, :])
    n_out, n_in = f % 64, p % 64
    same = (p // 64) == (f // 64)
    put('perm', np.where(same & (n_out < 32) & (n_in == n_out + 32), -1.0, 0.0)
        + np.where(same & (n_out >= 32) & (n_in == n_out - 32), 1.0, 0.0))
    t1 = np.arange(256)[None, :] - 128
    ok = np.concatenate([f <= p, t1 <= p], 1)
    put('cmask', np.where(ok, 0.0, NEG))
    put('c01', ok)
    inv = (np.float32(10000.0) ** (-np.arange(0, 64, 2, dtype=np.float32) / np.float32(64))).astype(np.float32)
    ang = np.arange(T, dtype=np.float32)[None, :] * inv[:, None]
    put('cos', np.tile(np.cos(ang), (4, 1)))
    put('sin', np.tile(np.sin(ang), (4, 1)))
    return a


class Queue:

    def __init__(self, sem):
        self.sem, self.n, self.items, self.seen = sem, 0, [], {}

    def wait(self, *toks):
        for t in toks:
            if t is None:
                continue
            if isinstance(t, list):
                self.wait(*t)
                continue
            s, v = t
            if self.seen.get(id(s), 0) < v:
                self.seen[id(s)] = v
                self.items.append(lambda e, s=s, v=v: e.wait_ge(s, v))

    def op(self, f, toks, sig=True):
        self.wait(*toks)
        if not sig:
            self.items.append(f)
            return None
        self.n += 1
        s = self.sem
        self.items.append(lambda e: f(e).then_inc(s, 1))
        return (s, self.n)

    @property
    def last(self):
        return (self.sem, self.n) if self.n else None

    def tt(self, out, a, b, op, *after):
        return self.op(lambda e: e.tensor_tensor(out, a, b, op), after)

    def ts(self, out, a, s1, s2, op0, op1, *after):
        if op1 is None:
            return self.op(lambda e: e.tensor_scalar(out, a, s1, None, op0), after)
        return self.op(lambda e: e.tensor_scalar(out, a, s1, s2, op0, op1), after)

    def stt(self, out, a, s, b, op0, op1, *after):
        return self.op(lambda e: e.scalar_tensor_tensor(out=out, in0=a, scalar=s, in1=b, op0=op0, op1=op1), after)

    def act(self, out, a, func, *after, scale=1.0, bias=0.0, accum=None):
        if accum is None:
            return self.op(lambda e: e.activation(out, a, func, bias=bias, scale=scale), after)
        return self.op(lambda e: e.activation(out, a, func, bias=bias, scale=scale, accum_out=accum), after)

    def mm(self, out, l, r, start, stop, *after, sig=False):
        return self.op(lambda e: e.matmul(out, l, r, start=start, stop=stop), after, sig)

    def tr(self, out, a, ident, *after, sig=False):
        return self.op(lambda e: e.transpose(out, a, ident), after, sig)


class Counter:

    def __init__(self, sem):
        self.sem, self.v = sem, 0

    def dma(self, q, out, src, *after):
        q.wait(*after)
        self.v += 16
        s = self.sem
        q.items.append(lambda e: e.dma_start(out, src).then_inc(s, 16))
        return (s, self.v)


NRING = 8


def build(nc, a, out, debug=None):
    ctx = ExitStack()
    with ctx:
        CB = ctx.enter_context(nc.sbuf_tensor("CB", [128, NCST], F32))
        VB = ctx.enter_context(nc.sbuf_tensor("VB", [128, len(VECS) * 8], F32))
        RG = ctx.enter_context(nc.sbuf_tensor("RG", [128, NRING, 2048], F32))
        Hb = ctx.enter_context(nc.sbuf_tensor("Hb", [128, 2048], F32))
        Sb = ctx.enter_context(nc.sbuf_tensor("Sb", [128, 2048], F32))
        Xb = ctx.enter_context(nc.sbuf_tensor("Xb", [128, 2048], F32))
        KX = ctx.enter_context(nc.sbuf_tensor("KX", [128, 4, 256], F32))
        VX = ctx.enter_context(nc.sbuf_tensor("VX", [128, 2, 512], F32))
        ST = ctx.enter_context(nc.sbuf_tensor("ST", [128, 512], F32))
        NPH = 24240
        PH = ctx.enter_context(nc.sbuf_tensor("PH", [128, NPH], F32))
        PS = [ctx.enter_context(nc.psum_tensor(f"PS{i}", [128, 512], F32)) for i in range(8)]

        def sem(n):
            return ctx.enter_context(nc.semaphore(n))

        V, S, G, E, D = (Queue(sem(n)) for n in ("s_dve", "s_act", "s_pool", "s_pe", "s_sp"))
        ring_sem = [Counter(sem(f"s_ring{i}")) for i in range(NRING)]
        s_c = Counter(sem("s_const"))
        s_io = Counter(sem("s_io"))
        s_out = Counter(sem("s_out"))

        def cst(n):
            o, w = CST[n]
            return CB[:, o:o + w]

        def vec(n, k):
            i = VECS.index(n) * 8 + k
            return VB[:, i:i + 1]

        ident = cst('ident')
        bank_free = [None] * 8
        ring_free = [None] * NRING
        ring_n = [0]

        class Piece:
            pass

        def load(*parts):
            i = ring_n[0] % NRING
            ring_n[0] += 1
            assert ring_free[i] != 'busy'
            p = Piece()
            p.i = i
            D.wait(ring_free[i])
            for dst, src in parts:
                p.tok = ring_sem[i].dma(D, dst(RG[:, i, :]), src)
            ring_free[i] = 'busy'
            p.ap = RG[:, i, :]
            return p

        def free(p, *toks):
            ring_free[p.i] = list(toks)

        def wcols(W, c0, n, k0=0, kn=KT):
            src = W[k0 * 128:(k0 + kn) * 128, c0:c0 + n].rearrange("(k p) n -> p k n", p=128)
            return (lambda r: r[:, 0:kn * n].rearrange("p (k n) -> p k n", k=kn)), src

        def v3(ap, n):
            return ap.rearrange("p (a n) -> p a n", n=n)

        def fence():
            toks = [V.last, S.last, G.last, E.last]
            for q in (V, S, G, E):
                q.wait(*toks)
            return toks

        H = Hb[:, :].rearrange("p (t c) -> p t c", t=2)
        S1 = Sb[:, :].rearrange("p (t c) -> p t c", t=2)
        XT = Xb[:, :].rearrange("p (k t) -> p k t", k=8)

        def mode_b(W, c0, npair, rhs, evac, banks, ready, nk=KT):
            for j in range(npair):
                pc = load(wcols(W, c0 + 256 * j, 256))
                w = v3(pc.ap, 256)
                b = banks[j % len(banks)]
                for m in range(2):
                    for k in range(nk):
                        t = E.mm(PS[b][:, m * 256:(m + 1) * 256], w[:, k, m * 128:(m + 1) * 128], rhs(k),
                                 k == 0, k == nk - 1, pc.tok, bank_free[b], ready, sig=(m == 1 and k == nk - 1))
                free(pc, t)
                bank_free[b] = evac(j, PS[b][:, :].rearrange("p (m t) -> p m t", m=2), t)

        def mode_a(W, c0, nhalf, lhs, evac, banks, ready, nk=KT):
            for h in range(nhalf):
                bb = [banks[(2 * h + tt) % len(banks)] for tt in range(2)]
                for kp in range(nk // 4):
                    pc = load(wcols(W, c0 + 512 * h, 512, 4 * kp, 4))
                    w = v3(pc.ap, 512)
                    for tt in range(2):
                        for k in range(4):
                            kk = 4 * kp + k
                            t = E.mm(PS[bb[tt]][:, :], lhs(kk, tt), w[:, k, :], kk == 0, kk == nk - 1,
                                     pc.tok, bank_free[bb[tt]], ready, sig=(k == 3))
                        if kk == nk - 1:
                            bank_free[bb[tt]] = evac(h, tt, PS[bb[tt]][:, :], t)
                    free(pc, t)

        def to_chan(src, dst, ready, banks, g=None, b=None):
            toks = []
            for kp in range(4):
                bk = banks[kp % len(banks)]
                for m in range(2):
                    for tt in range(2):
                        k = 2 * kp + m
                        t = E.tr(PS[bk][:, (2 * m + tt) * 128:(2 * m + tt + 1) * 128],
                                 src[:, tt, k * 128:(k + 1) * 128], ident, ready, bank_free[bk],
                                 sig=(m == 1 and tt == 1))
                rel = []
                for m in range(2):
                    k = 2 * kp + m
                    pv = PS[bk][:, m * 256:(m + 1) * 256]
                    if kp % 2 == 0 and g is not None:
                        e = S.act(dst[:, k, :], pv, ACT.Identity, t, scale=vec(g, k), bias=(vec(b, k) if b else 0.0))
                    elif g is not None:
                        if b:
                            e = V.ts(dst[:, k, :], pv, vec(g, k), vec(b, k), ALU.mult, ALU.add, t)
                        else:
                            e = V.ts(dst[:, k, :], pv, vec(g, k), None, ALU.mult, None, t)
                    elif kp % 2 == 0:
                        e = S.act(dst[:, k, :], pv, ACT.Copy, t)
                    else:
                        e = V.op(lambda q, o=dst[:, k, :], i=pv: q.tensor_copy(o, i), (t,))
                    rel.append(e)
                bank_free[bk] = rel
                toks += rel
            return toks

        def rstd_of(var, o, eps, scale, ready):
            t = V.ts(o, var, scale, eps, ALU.mult, ALU.add, ready)
            t = S.act(o, o, ACT.Sqrt, t)
            return V.op(lambda e: e.reciprocal(o, o), (t,))

        def rms_norm(src, ready):
            ts_ = []
            for tt in range(2):
                ts_.append(S.act(S1[:, tt, :], src[:, tt, :], ACT.Square, ready, accum=ST[:, tt:tt + 1]))
            r = rstd_of(ST[:, 0:2], ST[:, 2:4], EPS, 1.0 / C, ts_)
            return [V.ts(S1[:, tt, :], src[:, tt, :], ST[:, 2 + tt:3 + tt], None, ALU.mult, None, r) for tt in range(2)]

        def residual_ln(banks, toks, gi, bi, gname, bname):
            for tt in range(2):
                for h in range(2):
                    sl = slice(h * 512, h * 512 + 512)
                    b = banks[2 * tt + h]
                    e = V.stt(S1[:, tt, sl], H[:, tt, sl], ALPHA, PS[b][:, :], ALU.mult, ALU.add, toks, G.last)
                    bank_free[b] = e
                    st = ST[:, 16 + 12 * tt + 6 * h:22 + 12 * tt + 6 * h]
                    e = V.op(lambda q, o=st, i=S1[:, tt, sl]: q.bn_stats(o, i), (e,))
                e = V.op(lambda q, o=ST[:, 8 + 2 * tt:10 + 2 * tt], i=ST[:, 16 + 12 * tt:28 + 12 * tt]: q.bn_aggr(o, i), (e,))
            mv = ST[:, 8:12].rearrange("p (t s) -> p t s", s=2)
            r = rstd_of(mv[:, :, 1], ST[:, 2:4], LN_EPS, 1.0, e)
            n = [V.ts(S1[:, tt, :], S1[:, tt, :], ST[:, 8 + 2 * tt:9 + 2 * tt], ST[:, 2 + tt:3 + tt],
                      ALU.subtract, ALU.mult, r) for tt in range(2)]
            pc = load((lambda r_: r_[:, 0:1024], gi.broadcast_to([128, 1024])),
                      (lambda r_: r_[:, 1024:2048], bi.broadcast_to([128, 1024])))
            x = to_chan(S1, XT, n, [0, 1, 2, 3], gname, bname)
            for tt in range(2):
                e = G.tt(H[:, tt, :], S1[:, tt, :], pc.ap[:, 0:1024], ALU.mult, n, pc.tok)
                e = G.tt(H[:, tt, :], H[:, tt, :], pc.ap[:, 1024:2048], ALU.add, e)
            free(pc, e)
            return x

        def attention(nh, q, k, v, outp, od, scale, causal, tmp, ready, mask=None, mask_tok=None, banks=(0, 1, 2, 3, 4, 5)):
            W = 384 if causal else 512
            Sm, P, PT = (v3(tmp[:, i * 1024:(i + 1) * 1024], 512) for i in range(3))
            sp = [(0, 128), (128, 384)] if causal else [(0, 256), (256, 512)]
            st = ST[:, 64:64 + 16].rearrange("p (s n) -> p s n", n=8)
            sc_t, sm_free, p_t, p_free, pt_t, pt_free = {}, {}, {}, {}, {}, {}
            outs = []
            for i in range(nh + 2):
                if i < nh:
                    b = banks[i % 2]
                    for tt in range(2):
                        lo, hi = sp[tt]
                        t = E.mm(PS[b][:, lo:hi], q(i)[:, tt * 128:tt * 128 + 128], k(i)[:, 0:hi - lo], True, True,
                                 bank_free[b], ready, sig=(tt == 1))
                    s = st[:, i % 2, :]
                    if mask is not None:
                        for tt in range(2):
                            lo, hi = sp[tt]
                            e = V.op(lambda qq, o=Sm[:, i % 2, lo:hi], x=PS[b][:, lo:hi], m=mask[:, lo:hi], ac=s[:, tt:tt + 1]:
                                     qq.tensor_tensor_reduce(o, x, m, 1.0, TAKEN, ALU.add, ALU.max, ac),
                                     (t, mask_tok, sm_free.get(i - 2)))
                        bank_free[b] = e
                        src = Sm[:, i % 2, :]
                    else:
                        e = V.op(lambda qq, o=s[:, 0:2], x=PS[b][:, :].rearrange("p (t s) -> p t s", t=2):
                                 qq.tensor_reduce(o, x, AX, ALU.max), (t, sm_free.get(i - 2)))
                        src = PS[b][:, :]
                    e = V.ts(s[:, 2:4], s[:, 0:2], -scale, None, ALU.mult, None, e)
                    for tt in range(2):
                        lo, hi = sp[tt]
                        x = S.act(P[:, i % 2, lo:hi], src[:, lo:hi], ACT.Exp, e, p_free.get(i - 2), scale=scale,
                                  bias=s[:, 2 + tt:3 + tt], accum=s[:, 4 + tt:5 + tt])
                    sm_free[i] = x
                    if mask is None:
                        bank_free[b] = x
                    e = V.op(lambda qq, o=s[:, 6:8], ii=s[:, 4:6]: qq.reciprocal(o, ii), (x,))
                    for tt in range(2):
                        lo, hi = sp[tt]
                        p_t[i] = V.ts(P[:, i % 2, lo:hi], P[:, i % 2, lo:hi], s[:, 6 + tt:7 + tt], None, ALU.mult, None, e)
                if 1 <= i <= nh:
                    h = i - 1
                    b = banks[2 + h % 2]
                    p = P[:, h % 2, :]
                    if causal:
                        blocks = [(0, 0), (128, 128), (256, 256)]
                    else:
                        blocks = [(0, 0), (128, 256), (256, 128), (384, 384)]
                    for n, (dst, s0) in enumerate(blocks):
                        t = E.tr(PS[b][:, dst:dst + 128], p[:, s0:s0 + 128], ident, p_t[h], bank_free[b],
                                 sig=(n == len(blocks) - 1))
                    p_free[h] = t
                    x = S.act(PT[:, h % 2, 0:W], PS[b][:, 0:W], ACT.Copy, t, pt_free.get(h - 2))
                    bank_free[b] = x
                    pt_t[h] = x
                if i >= 2:
                    h = i - 2
                    parts, dst, last = outp(h)
                    b = banks[4 + (h // od) % 2]
                    pt = PT[:, h % 2, :]
                    E.mm(PS[b][parts, 0:256], v(h, 0), pt[:, 0:256], True, False, pt_t[h], bank_free[b])
                    if causal:
                        t = E.mm(PS[b][parts, 128:256], v(h, 1), pt[:, 256:384], False, True, sig=True)
                    else:
                        t = E.mm(PS[b][parts, 0:256], v(h, 1), pt[:, 256:512], False, True, sig=True)
                    pt_free[h] = t
                    if last:
                        x = S.act(dst, PS[b][:, 0:256], ACT.Copy, t)
                        bank_free[b] = x
                        outs.append(x)
            return outs

        def ffn(w_in, w_down, n, gated):
            GT = v3(PH[:, 0:1024], 512)
            HT = v3(PH[:, 1024:1024 + 2048], 512)
            F = 256 * n
            hfree, gfree, ht = {}, {}, {}

            def down(j):
                pd = load(wcols(w_down, 0, 1024, 2 * j, 2))
                w = v3(pd.ap, 1024)
                hv = HT[:, j % 4, :].rearrange("p (m t) -> p m t", m=2)
                for m in range(2):
                    for tt in range(2):
                        for h in range(2):
                            bb = 4 + 2 * tt + h
                            t = E.mm(PS[bb][:, :], hv[:, m, tt * 128:tt * 128 + 128], w[:, m, h * 512:h * 512 + 512],
                                     j == 0 and m == 0, j == n - 1 and m == 1, pd.tok, ht[j], bank_free[bb],
                                     sig=(m == 1 and tt == 1 and h == 1))
                free(pd, t)
                hfree[j] = t
                return t

            for j in range(n + 1):
                if j < n:
                    for u in range(2 if gated else 1):
                        pc = load(wcols(w_in, u * F + 256 * j, 256))
                        w = v3(pc.ap, 256)
                        b = (2 * (j % 2) + u) if gated else j % 4
                        for m in range(2):
                            for k in range(KT):
                                t = E.mm(PS[b][:, m * 256:m * 256 + 256], w[:, k, m * 128:m * 128 + 128], XT[:, k, :],
                                         k == 0, k == 7, pc.tok, bank_free[b], sig=(m == 1 and k == 7))
                        free(pc, t)
                        if u == 0:
                            g = S.act(GT[:, j % 2, :], PS[b][:, :], ACT.Silu if gated else ACT.Relu, t, gfree.get(j - 2))
                            if gated:
                                bank_free[b] = g
                    x = V.tt(HT[:, j % 4, :], GT[:, j % 2, :], PS[b][:, :], ALU.mult, g, t, hfree.get(j - 4))
                    bank_free[b] = x
                    gfree[j] = x
                    ht[j] = x
                if j >= 1:
                    t = down(j - 1)
            for b in range(4, 8):
                bank_free[b] = None
            return t

        def finish(src, ready):
            t = s_out.dma(D, out[0].rearrange("(t p) c -> p t c", p=128), src, ready)
            D.wait(t)

        def run():
            s_c.dma(D, CB[:, :], a['cst'])
            tx = s_io.dma(D, XT, a['xT'].rearrange("(k p) t -> p k t", p=128))
            tc = s_c.dma(D, VB[:, :], a['vec'])
            for q in (V, S, G, E):
                q.wait(tc)

            o = 0

            def take(n):
                nonlocal o
                r = PH[:, o:o + n]
                o += n
                assert o <= NPH, o
                return r

            AR = take(4096).rearrange("p (m c s t) -> p m c s t", m=8, c=2, s=2)
            BE = take(2048).rearrange("p (m t) -> p m t", m=8)
            KA = take(2048).rearrange("p (m t) -> p m t", m=8)
            VV = take(2048).rearrange("p (t c) -> p t c", t=2)
            bon = take(32)
            DX = take(8)
            SG = take(512).rearrange("p (m t) -> p m t", m=2)
            o_keep = o
            XX = take(2048).rearrange("p (k t) -> p k t", k=8)
            XM = [take(2048).rearrange("p (k t) -> p k t", k=8) for _ in range(2)]
            P2 = take(2048)
            TW = take(256)
            TA = take(256)
            cs = take(516).rearrange("p (a t) -> p a t", t=129)
            EE = take(516).rearrange("p (a t) -> p a t", t=129)
            EI, sg, aa, kS, rS, kk = (take(512) for _ in range(6))
            o_tmp = o

            w = V.tt(XX[:, :, 1:256], XT[:, :, 0:255], XT[:, :, 1:256], ALU.subtract, tx)
            w = V.ts(XX[:, :, 0:1], XT[:, :, 0:1], -1.0, None, ALU.mult, None, w)
            mset = G.op(lambda e: e.memset(cs[:, :, 0:1], 0.0), ())
            xm_free = [None] * 2

            def mix(i, n):
                slot = i % 2
                for k in range(KT):
                    t = V.stt(XM[slot][:, k, :], XX[:, k, :], vec(f'mu{n}', k), XT[:, k, :], ALU.mult, ALU.add,
                              w, xm_free[slot])
                return slot, t

            pc = load((lambda r: v3(r[:, 0:512], 64), a['w1'].rearrange("(k p) n -> p k n", p=128)),
                      (lambda r: v3(r[:, 512:1024], 64), a['a1'].rearrange("(k p) n -> p k n", p=128)))
            pg = load((lambda r: v3(r[:, 0:1280], 160), a['g1'].rearrange("(k p) n -> p k n", p=128)))
            s_io.dma(D, P2[0:64, 0:1024], a['w2'])
            p2t = s_io.dma(D, P2[0:64, 1024:2048], a['a2'])
            for i, (n, fn, dst) in enumerate([(1, ACT.Tanh, TW), (4, ACT.Copy, TA)]):
                slot, t = mix(i, n)
                wv = v3(pc.ap[:, i * 512:(i + 1) * 512], 64)
                for k in range(KT):
                    e = E.mm(PS[5 + i][0:64, 0:256], wv[:, k, :], XM[slot][:, k, :], k == 0, k == 7,
                             t, pc.tok, sig=(k == 7))
                xm_free[slot] = e
                low = S.act(dst[0:64, :], PS[5 + i][0:64, 0:256], fn, e)
            free(pc, e)
            slot, t = mix(2, 5)
            wv = v3(pg.ap[:, 0:1280], 160)
            for m, (c0, c1) in enumerate([(0, 128), (128, 160)]):
                for k in range(KT):
                    e = E.mm(PS[7 - 4 * m][0:c1 - c0, 0:256], wv[:, k, c0:c1], XM[slot][:, k, :],
                             k == 0, k == 7, t, pg.tok, sig=(k == 7))
                sgt = S.act(SG[0:c1 - c0, m, :], PS[7 - 4 * m][0:c1 - c0, 0:256], ACT.Sigmoid, e)
            free(pg, e)
            xm_free[slot] = e
            bank_free[5] = bank_free[6] = low
            bank_free[7] = bank_free[3] = sgt
            ks, kt_ = mix(3, 2)
            rs, rt_ = mix(4, 0)
            W_K, W_R, W_V = a['w_rkv'][1], a['w_rkv'][0], a['w_rkv'][2]
            w2v, a2v = P2[0:64, 0:1024], P2[0:64, 1024:2048]
            bon_t = []
            prev = None
            for j in range(4):
                kb, rb = 2 * (j % 2), 2 * (j % 2) + 1
                for m in range(2):
                    c0 = (2 * j + m) * 128
                    E.mm(PS[4][:, m * 256:m * 256 + 256], w2v[:, c0:c0 + 128], TW[0:64, :], True, True,
                         p2t, low, bank_free[4])
                    tz = E.mm(PS[5][:, m * 256:m * 256 + 256], a2v[:, c0:c0 + 128], TA[0:64, :], True, True,
                              bank_free[5], sig=True)
                toks = []
                for W, sl, b, rdy in ((W_K, ks, kb, kt_), (W_R, rs, rb, rt_)):
                    pc = load(wcols(W, 256 * j, 256))
                    wv = v3(pc.ap, 256)
                    for m in range(2):
                        for k in range(KT):
                            t = E.mm(PS[b][:, m * 256:m * 256 + 256], wv[:, k, m * 128:m * 128 + 128], XM[sl][:, k, :],
                                     k == 0, k == 7, pc.tok, rdy, bank_free[b], sig=(m == 1 and k == 7))
                    free(pc, t)
                    toks.append(t)
                tk, tr = toks
                if j == 3:
                    xm_free[ks], xm_free[rs] = tk, tr
                for m in range(2):
                    k = 2 * j + m
                    sl = slice(m * 256, m * 256 + 256)
                    S.act(sg[:, sl], PS[4][:, sl], ACT.Tanh, tz, prev, scale=0.5, bias=HV[:, k:k + 1])
                    x = S.act(aa[:, sl], PS[5][:, sl], ACT.Tanh, tz, scale=0.5, bias=HV[:, 8 + k:9 + k])
                bank_free[4] = bank_free[5] = x
                y = V.ts(sg, sg, 0.5, 0.5, ALU.mult, ALU.add, x)
                for q in range(4):
                    y2 = V.op(lambda e, o_=cs[:, q, 1:129], d1=sg[:, q * 128:q * 128 + 128]:
                              e.tensor_tensor_scan(o_, cst('ones'), d1, 0.0, ALU.mult, ALU.add), (y, mset, prev))
                mid = ST[:, 32:36]
                nmid = ST[:, 36:40]
                V.ts(mid, cs[:, :, 64], CDEC, None, ALU.mult, None, y2)
                y3 = V.ts(nmid, cs[:, :, 64], -CDEC, None, ALU.mult, None, y2)
                for q in range(4):
                    S.act(EE[:, q, :], cs[:, q, :], ACT.Exp, y3, prev, scale=-CDEC, bias=mid[:, q:q + 1])
                    x = S.act(EI[:, q * 128:q * 128 + 128], cs[:, q, :][:, 1:129], ACT.Exp, scale=CDEC, bias=nmid[:, q:q + 1])
                em = ST[:, 40:44]
                x = S.act(em, nmid, ACT.Exp, x)
                for m in range(2):
                    dx = V.tt(DX[:, 2 * j + m:2 * j + m + 1], EE[:, 2 * m, 128:129], em[:, 2 * m + 1:2 * m + 2], ALU.mult, x)
                y = V.ts(aa, aa, 0.5, 0.5, ALU.mult, ALU.add, x)
                S.act(kS, PS[kb][:, :], ACT.Copy, tk, prev)
                for m in range(2):
                    k = 2 * j + m
                    sl = slice(m * 256, m * 256 + 256)
                    xk = S.act(kk[:, sl], PS[kb][:, sl], ACT.Copy, scale=vec('k_k', k))
                xq = S.act(sg, kk, ACT.Square, xk, y2)
                bank_free[kb] = xk
                t = E.mm(PS[6][:, :], cst('bones'), sg, True, True, xq, bank_free[6], sig=True)
                x = S.act(sg, PS[6][:, :], ACT.Sqrt, t)
                bank_free[6] = x
                y = V.ts(sg, sg, 1e-12, None, ALU.max, None, x)
                y = V.op(lambda e: e.reciprocal(sg, sg), (y,))
                y = V.tt(kk, kk, sg, ALU.mult, y)
                x = S.act(rS, PS[rb][:, :], ACT.Copy, tr, prev)
                bank_free[rb] = x
                ya = None
                EA = EE[:, :, 0:128]
                EB = EE[:, :, 1:129]
                ARa = AR[:, 2 * j:2 * j + 2, :, 0, :].rearrange("p m c t -> p (m c) t")
                ARr = AR[:, 2 * j:2 * j + 2, :, 1, :].rearrange("p m c t -> p (m c) t")
                V.tt(ARr, v3(rS, 128), EB, ALU.mult, x)
                V.stt(ARa, v3(kk, 128), -1.0, EA, ALU.mult, ALU.mult, y)
                y = V.tt(kk, kk, aa, ALU.mult, V.last)
                V.tt(BE[:, 2 * j:2 * j + 2, :].rearrange("p m t -> p (m t)"), kk, EI, ALU.mult, y)
                for m in range(2):
                    k = 2 * j + m
                    sl = slice(m * 256, m * 256 + 256)
                    y = V.ts(aa[:, sl], aa[:, sl], -1.0, vec('k_a', k), ALU.add, ALU.mult, y)
                y = V.stt(kS, aa, 1.0, kS, ALU.add, ALU.mult, y)
                V.tt(KA[:, 2 * j:2 * j + 2, :].rearrange("p m t -> p (m t)"), kS, EI, ALU.mult, y)
                for m in range(2):
                    k = 2 * j + m
                    sl = slice(m * 256, m * 256 + 256)
                    yp = V.stt(rS[:, sl], rS[:, sl], vec('r_k', k), kS[:, sl], ALU.mult, ALU.mult, y)
                for m in range(2):
                    for tt in range(2):
                        t = E.mm(PS[7][:, tt * 16 + 4 * j + 2 * m:tt * 16 + 4 * j + 2 * m + 2],
                                 rS[:, m * 256 + tt * 128:m * 256 + tt * 128 + 128], cst('sel2'), True, True,
                                 yp, bank_free[7], sig=True)
                prev = [t, V.last]
            x = V.op(lambda e: e.tensor_copy(bon, PS[7][:, 0:32]), (t,))
            bank_free[7] = x
            vs, vt_ = mix(5, 3)
            vv_t = []

            def ev_v(h, tt, b, t):
                x = S.act(VV[:, tt, h * 512:h * 512 + 512], b, ACT.Copy, t)
                vv_t.append(x)
                return x
            mode_a(W_V, 0, 2, lambda k, tt: XM[vs][:, k, tt * 128:tt * 128 + 128], ev_v, [0, 1, 2, 3], vt_)

            tm = s_io.dma(D, H, a['mem'].rearrange("(t p) c -> p t c", p=128))
            nrm = rms_norm(H, [tm])
            MT = XT
            G.wait(V.last)
            mt = to_chan(S1, MT, [nrm, E.last], [4, 5, 6, 7], 'nmem')

            def ev_kx(j, b, t):
                return S.act(KX[:, 2 * j:2 * j + 2, :], b, ACT.Copy, t)
            mode_b(a['wx_kv'], 0, 2, lambda k: MT[:, k, :], ev_kx, [0, 1], mt)

            def ev_vx(h, tt, b, t):
                return S.act(VX[:, tt, :], b, ACT.Copy, t)
            mode_a(a['wx_kv'], 512, 1, lambda k, tt: MT[:, k, tt * 128:tt * 128 + 128], ev_vx, [2, 3], mt)

            fence()
            o = o_keep
            AT = take(8192).rearrange("p (i s t) -> p i s t", i=16, s=4)
            BT = take(512).rearrange("p (m n) -> p m n", m=4)
            KTt = take(512).rearrange("p (m n) -> p m n", m=4)
            RR = take(512).rearrange("p (g n) -> p g n", g=2)
            SA = take(1024).rearrange("p (g n) -> p g n", g=4)
            SS = take(512).rearrange("p (m e n) -> p m e n", m=4, e=2)
            ss0 = G.op(lambda e: e.memset(SS, 0.0), ())
            YY = take(2048).rearrange("p (t c) -> p t c", t=2)
            Xi = Hb[:, :].rearrange("p (g n) -> p g n", g=4)
            Zi = Sb[:, :].rearrange("p (g n) -> p g n", g=4)
            Wi = Xb[:, :].rearrange("p (g n) -> p g n", g=4)
            i4 = ident.unsqueeze(1).broadcast_to([128, 4, 128])

            def lvl(l):
                off = CST['lvl'][0] + 128 * l
                return CB[:, off:off + 128].unsqueeze(1).broadcast_to([128, 4, 128])
            m0t = cst('m0t').unsqueeze(1).broadcast_to([128, 4, 128])
            prev_half = None
            for half in range(2):
                def prob(g, n):
                    h = 8 * half + 4 * (g % 2) + n
                    return g // 2, h, h // 2, slice(64 * (h % 2), 64 * (h % 2) + 64)
                at_t = []
                for g in range(4):
                    for n in range(4):
                        c, h, m, pp = prob(g, n)
                        i = 4 * g + n
                        b = i % 8
                        rhs = AR[pp, m, c, :, :].rearrange("p s t -> p (s t)")
                        E.mm(PS[b][:, 0:256], BE[pp, m, c * 128:c * 128 + 128], rhs, True, True, bank_free[b], prev_half)
                        t = E.mm(PS[b][:, 256:512], KA[pp, m, c * 128:c * 128 + 128], rhs, True, True, sig=True)
                        bank_free[b] = V.tt(AT[:, i, :, :].rearrange("p s t -> p (s t)"), PS[b][:, :], cst('atm'), ALU.mult, t,
                                            prev_half)
                    at_t.append(bank_free[b])
                for src, dst, b in ((BE, BT, 0), (KA, KTt, 1)):
                    for m in range(4):
                        t = E.tr(PS[b][:, m * 128:m * 128 + 128], src[:, 4 * half + m, 0:128], ident, bank_free[b], sig=(m == 3))
                    bt_t = S.act(dst.rearrange("p m n -> p (m n)"), PS[b][:, :], ACT.Copy, t, prev_half)
                    bank_free[b] = bt_t
                xz = [None] * 4
                wt = [None] * 4
                for l in range(7):
                    for g in range(4):
                        b = g
                        for n in range(4):
                            i = 4 * g + n
                            rhs = ident if l == 0 else Zi[:, g, n * 128:n * 128 + 128]
                            t = E.mm(PS[b][:, n * 128:n * 128 + 128], AT[:, i, 0, :], rhs, True, True,
                                     at_t[g], xz[g], bank_free[b], sig=(n == 3))
                        wv = v3((Zi if l == 0 else Wi)[:, g, :], 128)
                        e = V.tt(wv, v3(PS[b][:, :], 128), lvl(l), ALU.mult, t)
                        bank_free[b] = e
                        wt[g] = V.tt(wv, wv, i4, ALU.add, e)
                        if l == 0:
                            e = V.tt(v3(Xi[:, g, :], 128), AT[:, 4 * g:4 * g + 4, 0, :], m0t, ALU.mult, at_t[g])
                            xz[g] = V.tt(v3(Xi[:, g, :], 128), v3(Xi[:, g, :], 128), i4, ALU.add, e)
                    if l == 0:
                        continue
                    for g in range(4):
                        bx, bz = 4 + (2 * g) % 4, 5 + (2 * g) % 4
                        for n in range(4):
                            ns = slice(n * 128, n * 128 + 128)
                            tx_ = E.mm(PS[bx][:, ns], Wi[:, g, ns], Xi[:, g, ns], True, True, wt[g], bank_free[bx],
                                       sig=(n == 3))
                        if l < 6:
                            for n in range(4):
                                ns = slice(n * 128, n * 128 + 128)
                                tz_ = E.mm(PS[bz][:, ns], Xi[:, g, ns], Wi[:, g, ns], True, True, bank_free[bz],
                                           sig=(n == 3))
                        else:
                            tz_ = tx_
                        e = S.act(Xi[:, g, :], PS[bx][:, :], ACT.Copy, tz_)
                        bank_free[bx] = e
                        if l < 6:
                            e = S.act(Zi[:, g, :], PS[bz][:, :], ACT.Copy, tz_)
                            bank_free[bz] = e
                        xz[g] = e
                st_t = None
                for c in range(2):
                    for gg in range(2):
                        g = 2 * c + gg
                        b = g
                        for n in range(4):
                            _, h, m, pp = prob(g, n)
                            i = 4 * g + n
                            ns = slice(n * 64, n * 64 + 64)
                            t = E.mm(PS[b][:, ns], AT[:, i, 2, :], VV[:, c, h * 64:h * 64 + 64], True, c == 0,
                                     bank_free[b], at_t[g], vv_t[-1], sig=(n == 3))
                            if c == 1:
                                t = E.mm(PS[b][:, ns], AR[:, m, 1, 0, :], SS[:, m - 4 * half, h % 2, :], False, True, st_t,
                                         sig=(n == 3))
                        rr = S.act(RR[:, gg, :], PS[b][:, 0:256], ACT.Copy, t, prev_half)
                        for n in range(4):
                            t = E.mm(PS[b][:, 256 + n * 64:320 + n * 64], Xi[:, g, n * 128:n * 128 + 128],
                                     RR[:, gg, n * 64:n * 64 + 64], True, True, rr, xz[g], sig=(n == 3))
                        sa = S.act(SA[:, g, :], PS[b][:, 256:512], ACT.Copy, t)
                        bank_free[b] = sa
                    for gg in range(2):
                        g = 2 * c + gg
                        b = 4 + c
                        for n in range(4):
                            _, h, m, pp = prob(g, n)
                            i = 4 * g + n
                            sl = slice((4 * gg + n) * 64, (4 * gg + n) * 64 + 64)
                            E.mm(PS[b][:, sl], AT[:, i, 3, :], VV[:, c, h * 64:h * 64 + 64], True, False, bank_free[b])
                            t = E.mm(PS[b][:, sl], AT[:, i, 1, :], SA[:, g, n * 64:n * 64 + 64], False, c == 0, sa,
                                     sig=(n == 3))
                            if c == 1:
                                t = E.mm(PS[b][:, sl], AR[:, m, 1, 1, :], SS[:, m - 4 * half, h % 2, :], False, True,
                                         sig=(n == 3))
                    bank_free[b] = S.act(YY[:, c, half * 512:half * 512 + 512], PS[b][:, :], ACT.Copy, t)
                    yy_t = bank_free[b]
                    if c == 0:
                        for m in range(4):
                            for e_ in range(2):
                                h = 8 * half + 2 * m + e_
                                g, n = (h % 8) // 4, h % 4
                                pp = slice(64 * e_, 64 * e_ + 64)
                                E.mm(PS[6][pp, m * 64:m * 64 + 64], KTt[:, m, pp], VV[:, 0, h * 64:h * 64 + 64], True, False,
                                     bank_free[6], bt_t)
                                t = E.mm(PS[6][pp, m * 64:m * 64 + 64], BT[:, m, pp], SA[:, g, n * 64:n * 64 + 64],
                                         False, True, sig=True)
                        for m in range(4):
                            for e_ in range(2):
                                pp = slice(64 * e_, 64 * e_ + 64)
                                st_t = V.ts(SS[pp, m, e_, :], PS[6][pp, m * 64:m * 64 + 64],
                                            DX[pp, 4 * half + m:4 * half + m + 1], None, ALU.mult, None, t, ss0)
                        bank_free[6] = st_t
                prev_half = [E.last, S.last, V.last]

            fence()
            Y3 = YY.rearrange("p t (h n) -> p (t h) n", n=64)
            YA = YY.rearrange("p t c -> p (t c)")
            pg2 = load((lambda r: r[:, 0:1024], a['g2'][0:128, :]), (lambda r: r[0:32, 1024:2048], a['g2'][128:160, :]))
            tb = load((lambda r: r[:, 0:1024], a['gn_g'].broadcast_to([128, 1024])),
                      (lambda r: r[:, 1024:2048], a['gn_b'].broadcast_to([128, 1024])))
            mu_ = ST[:, 128:160]
            va_ = ST[:, 160:192]
            gt = []
            for tt in range(2):
                for h in range(2):
                    b = 2 * tt + h
                    E.mm(PS[b][:, :], SG[:, 0, tt * 128:tt * 128 + 128], pg2.ap[:, h * 512:h * 512 + 512], True, False,
                         pg2.tok, sgt, bank_free[b])
                    gt.append(E.mm(PS[b][:, :], SG[0:32, 1, tt * 128:tt * 128 + 128],
                                   pg2.ap[0:32, 1024 + h * 512:1536 + h * 512], False, True, sig=True))
            free(pg2, E.last)
            thx = s_io.dma(D, H, a['x'].rearrange("(t p) c -> p t c", p=128), [E.last, S.last, V.last])
            y = V.op(lambda e: e.tensor_reduce(mu_, Y3, AX, ALU.add), (yy_t,))
            y = V.ts(mu_, mu_, 1.0 / 64, None, ALU.mult, None, y)
            y = V.tt(Y3, Y3, mu_.unsqueeze(2).broadcast_to([128, 32, 64]), ALU.subtract, y)
            SQ = Sb[:, :]
            x = S.act(SQ, YA, ACT.Square, y)
            bv = G.tt(XT.rearrange("p k t -> p (k t)").rearrange("p (h n) -> p h n", n=64),
                      VV.rearrange("p t (h n) -> p (t h) n", n=64), bon.unsqueeze(2).broadcast_to([128, 32, 64]),
                      ALU.mult, V.last)
            y = V.op(lambda e: e.tensor_reduce(va_, SQ.rearrange("p (h n) -> p h n", n=64), AX, ALU.add), (x,))
            y = rstd_of(va_, va_, GN_EPS, 1.0 / 64, y)
            y = V.tt(Y3, Y3, va_.unsqueeze(2).broadcast_to([128, 32, 64]), ALU.mult, y)
            y = V.tt(YY, YY, tb.ap[:, 0:1024].unsqueeze(1).broadcast_to([128, 2, 1024]), ALU.mult, y, tb.tok)
            y = V.tt(YY, YY, tb.ap[:, 1024:2048].unsqueeze(1).broadcast_to([128, 2, 1024]), ALU.add, y)
            free(tb, y)
            y = V.tt(YA, YA, XT.rearrange("p k t -> p (k t)"), ALU.add, y, bv)
            for tt in range(2):
                for h in range(2):
                    b = 2 * tt + h
                    sl = slice(h * 512, h * 512 + 512)
                    yg = V.tt(YY[:, tt, sl], YY[:, tt, sl], PS[b][:, :], ALU.mult, gt, y)
                    bank_free[b] = yg
            yt = to_chan(YY, XT, yg, [0, 1, 2, 3])
            toks = []

            def ev_keep(h, tt, b, t):
                toks.append(t)
                return None
            mode_a(a['w_o'], 0, 2, lambda k, tt: XT[:, k, tt * 128:tt * 128 + 128], ev_keep, [4, 6, 5, 7], yt)
            residual_ln([4, 5, 6, 7], [toks, thx], a['lnmg'][0:1, :], a['lnmb'][0:1, :], 'mixg0', 'mixb0')
            if debug == 'rwkv':
                return finish(H, G.last)
            E.wait(V.last, S.last)
            t = ffn(a['ffn_w_in'][0], a['ffn_w_down'][0], 11, True)
            residual_ln([4, 5, 6, 7], [t], a['lnfg'][0:1, :], a['lnfb'][0:1, :], 'ffng0', 'ffnb0')
            if debug == 'layer0':
                return finish(H, G.last)

            fence()
            o = 0
            QQ = take(2048).rearrange("p (k t) -> p k t", k=8)
            KK = take(2048).rearrange("p (k t) -> p k t", k=8)
            VV = take(2048).rearrange("p (t c) -> p t c", t=2)
            OT = take(2048).rearrange("p (k t) -> p k t", k=8)
            raw = [take(512) for _ in range(2)]
            rc = [take(512) for _ in range(2)]
            TMP = take(3072)
            W = a['moba_w_qkv']
            cosb = cst('cos').unsqueeze(1).broadcast_to([128, 2, 256])
            sinb = cst('sin').unsqueeze(1).broadcast_to([128, 2, 256])
            rope_t = []
            raw_free = [None, None]

            def rope(dst):
                def ev(j, b, t):
                    x = S.act(raw[j % 2].rearrange("p (m t) -> p m t", m=2), b, ACT.Copy, t, raw_free[j % 2])
                    pb = 2 + j % 2
                    t2 = E.mm(PS[pb][:, :], cst('perm'), raw[j % 2], True, True, x, bank_free[pb], sig=True)
                    g = G.tt(rc[j % 2].rearrange("p (m t) -> p m t", m=2), raw[j % 2].rearrange("p (m t) -> p m t", m=2),
                             cosb, ALU.mult, x, raw_free[j % 2])
                    d = dst[:, 2 * j:2 * j + 2, :]
                    y = V.tt(d, PS[pb][:, :].rearrange("p (m t) -> p m t", m=2), sinb, ALU.mult, t2)
                    bank_free[pb] = y
                    y = V.tt(d, d, rc[j % 2].rearrange("p (m t) -> p m t", m=2), ALU.add, y, g)
                    raw_free[j % 2] = [y, t2]
                    rope_t.append(y)
                    return x
                return ev
            mode_b(W, 0, 4, lambda k: XT[:, k, :], rope(QQ), [0, 1], None)
            mode_b(W, 1024, 4, lambda k: XT[:, k, :], rope(KK), [0, 1], None)
            vt = []

            def ev_v2(h, tt, b, t):
                vt.append(S.act(VV[:, tt, h * 512:h * 512 + 512], b, ACT.Copy, t))
                return vt[-1]
            mode_a(W, 2048, 2, lambda k, tt: XT[:, k, tt * 128:tt * 128 + 128], ev_v2, [4, 5, 6, 7], None)

            def hp(h):
                return slice(64 * (h % 2), 64 * (h % 2) + 64)
            outs = attention(16, lambda h: QQ[hp(h), h // 2, :], lambda h: KK[hp(h), h // 2, :],
                             lambda h, s: VV[:, s, h * 64:h * 64 + 64],
                             lambda h: (hp(h), OT[:, h // 2, :], h % 2 == 1), 2, 0.125, True, TMP,
                             [rope_t[-1], vt[-1]], mask=cst('cmask'))
            toks = []
            mode_a(a['moba_w_o'], 0, 2, lambda k, tt: OT[:, k, tt * 128:tt * 128 + 128],
                   lambda h, tt, b, t: toks.append(t), [4, 6, 5, 7], outs)
            residual_ln([4, 5, 6, 7], toks, a['lnmg'][1:2, :], a['lnmb'][1:2, :], 'mixg1', 'mixb1')
            if debug == 'moba':
                return finish(H, G.last)
            fence()
            t = ffn(a['ffn_w_in'][1], a['ffn_w_down'][1], 11, True)
            residual_ln([4, 5, 6, 7], [t], a['lnfg'][1:2, :], a['lnfb'][1:2, :], 'ffng1', 'ffnb1')
            if debug == 'layer1':
                return finish(H, G.last)

            fence()
            nrm = rms_norm(H, None)
            xt = to_chan(S1, XT, nrm, [0, 1, 2, 3], 'nmix')
            o = 0
            UB = take(8 * 286).rearrange("p (k t) -> p k t", k=8)
            CV = take(2048).rearrange("p (k t) -> p k t", k=8)
            QQ = take(2048).rearrange("p (k t) -> p k t", k=8)
            KK = take(2048).rearrange("p (k t) -> p k t", k=8)
            VV = take(2048).rearrange("p (t c) -> p t c", t=2)
            GC = take(2048).rearrange("p (k t) -> p k t", k=8)
            GA = take(2048).rearrange("p (k t) -> p k t", k=8)
            OT = take(2048).rearrange("p (k t) -> p k t", k=8)
            QI = take(1024).rearrange("p (k t) -> p k t", k=4)
            KI = take(256)
            WI = take(16)
            TMP = take(3072)
            SC = take(384)
            SW = take(384)
            RL = [take(384) for _ in range(2)]
            sgb = [TMP[:, i * 512:(i + 1) * 512] for i in range(2)]
            W = a['w_in2']
            z = G.op(lambda e: e.memset(UB[:, :, 0:30], 0.0), ())
            conv_t = []
            sg_free = [None, None]
            for j in range(4):
                bs = []
                for u in range(2):
                    pc = load(wcols(W, 1024 * u + 256 * j, 256))
                    wv = v3(pc.ap, 256)
                    b = 2 * (j % 2) + u
                    for m in range(2):
                        for k in range(KT):
                            t = E.mm(PS[b][:, m * 256:m * 256 + 256], wv[:, k, m * 128:m * 128 + 128], XT[:, k, :],
                                     k == 0, k == 7, pc.tok, bank_free[b], xt, sig=(m == 1 and k == 7))
                    free(pc, t)
                    bs.append((b, t))
                (ba, ta), (bg, tg) = bs
                x = S.act(sgb[j % 2], PS[bg][:, :], ACT.Sigmoid, tg, sg_free[j % 2])
                bank_free[bg] = x
                y = V.tt(UB[:, 2 * j:2 * j + 2, 30:286], PS[ba][:, :].rearrange("p (m t) -> p m t", m=2),
                         sgb[j % 2].rearrange("p (m t) -> p m t", m=2), ALU.mult, x, ta)
                bank_free[ba] = y
                sg_free[j % 2] = y
                conv_t.append(y)

            def conv(k):
                y = V.ts(CV[:, k, :], UB[:, k, 30:286], vec('cw30', k), vec('conv_b', k), ALU.mult, ALU.add, conv_t[k // 2], z)
                for i in range(30):
                    y = V.stt(CV[:, k, :], UB[:, k, i:i + 256], vec(f'cw{i}', k), CV[:, k, :], ALU.mult, ALU.add, y)
                return y

            q_t = []

            def ev_to(dst):
                def ev(j, b, t):
                    q_t.append(S.act(dst[:, 2 * j:2 * j + 2, :], b, ACT.Copy, t))
                    return q_t[-1]
                return ev
            mode_b(W, 5120, 2, lambda k: XT[:, k, :], ev_to(QI), [0, 1], xt)
            src = W[:, 5632:5704].rearrange("(k p) n -> p k n", p=128)
            pc = load((lambda r: v3(r[:, 0:1024], 128)[:, :, 0:64], src[:, :, 0:64]),
                      (lambda r: v3(r[:, 0:1024], 128)[:, :, 64:128], src[:, :, 0:64]),
                      (lambda r: v3(r[:, 1024:1088], 8), src[:, :, 64:72]))
            for k in range(KT):
                t = E.mm(PS[2][:, 0:256], v3(pc.ap[:, 0:1024], 128)[:, k, :], XT[:, k, :], k == 0, k == 7, pc.tok,
                         bank_free[2], sig=(k == 7))
            for tt in range(2):
                for k in range(KT):
                    t = E.mm(PS[2][:, 256 + 8 * tt:264 + 8 * tt], XT[:, k, tt * 128:tt * 128 + 128],
                             v3(pc.ap[:, 1024:1088], 8)[:, k, :], k == 0, k == 7, sig=(k == 7))
            free(pc, t)
            S.act(KI, PS[2][:, 0:256], ACT.Copy, t)
            x = S.act(WI, PS[2][:, 256:272], ACT.Copy, scale=8 ** -0.5)
            bank_free[2] = x
            ki_t = x
            sp = [(0, 128), (128, 384)]
            y = None
            rl_free = [None, None]
            for h in range(8):
                b = 4 + h % 2
                for tt in range(2):
                    lo, hi = sp[tt]
                    t = E.mm(PS[b][:, lo:hi], QI[hp(h), h // 2, tt * 128:tt * 128 + 128], KI[hp(h), 0:hi - lo], True, True,
                             ki_t, q_t[-1], bank_free[b], sig=(tt == 1))
                x = S.act(RL[h % 2], PS[b][:, 0:384], ACT.Relu, t, rl_free[h % 2], scale=0.125)
                bank_free[b] = x
                for tt in range(2):
                    lo, hi = sp[tt]
                    wi = WI[:, 8 * tt + h:8 * tt + h + 1]
                    if h == 0:
                        e = V.ts(SC[:, lo:hi], RL[0][:, lo:hi], wi, None, ALU.mult, None, x)
                    else:
                        e = V.stt(SC[:, lo:hi], RL[h % 2][:, lo:hi], wi, SC[:, lo:hi], ALU.mult, ALU.add, x, y)
                y = e
                rl_free[h % 2] = e
            y = V.tt(SC, SC, cst('cmask'), ALU.add, y)
            for tt in range(2):
                lo, hi = sp[tt]
                for r in range(8):
                    m8 = ST[:, 200 + 8 * tt:208 + 8 * tt]
                    y = V.op(lambda e, o_=m8, i_=SC[:, lo:hi]: e.max(o_, i_), (y,))
                    y = V.op(lambda e, o_=SC[:, lo:hi], m_=m8: e.match_replace(o_, m_, o_, TAKEN), (y,))
            y = V.ts(SC, SC, TAKEN, None, ALU.is_equal, None, y)
            y = V.tt(SC, SC, cst('c01'), ALU.mult, y)
            sel_t = V.ts(SC, SC, -1.0, -NEG, ALU.add, ALU.mult, y)

            mode_b(W, 2048, 4, lambda k: XT[:, k, :], ev_to(QQ), [0, 1], xt)
            conv(0)
            mode_b(W, 3072, 4, lambda k: XT[:, k, :], ev_to(KK), [2, 3], xt)

            def ev_v3(h, tt, b, t):
                q_t.append(S.act(VV[:, tt, h * 512:h * 512 + 512], b, ACT.Copy, t))
                return q_t[-1]
            mode_a(W, 4096, 2, lambda k, tt: XT[:, k, tt * 128:tt * 128 + 128], ev_v3, [4, 5, 6, 7], xt)

            def ev_gate(dst, bname):
                def ev(j, b, t):
                    for m in range(2):
                        k = 2 * j + m
                        q_t.append(S.act(dst[:, k, :], b[:, m, :], ACT.Sigmoid, t, bias=vec(bname, k)))
                    return q_t[-1]
                return ev
            mode_b(W, 5704, 4, lambda k: XT[:, k, :], ev_gate(GC, 'bgc'), [0, 1], xt)
            mode_b(W, 6728, 4, lambda k: XT[:, k, :], ev_gate(GA, 'bga'), [2, 3], xt)
            for k in range(1, 8):
                cv = conv(k)
            outs = attention(8, lambda h: QQ[:, h, :], lambda h: KK[:, h, :], lambda h, s: VV[:, s, h * 128:h * 128 + 128],
                             lambda h: (slice(0, 128), OT[:, h, :], True), 1, 128 ** -0.5, True, TMP,
                             [q_t[-1], cv], mask=SC, mask_tok=sel_t)
            CVf = CV.rearrange("p k t -> p (k t)")
            for k in range(KT):
                t = E.mm(PS[6][:, 0:256], cst('ones'), CV[:, k, :], k == 0, k == 7, cv, bank_free[6], sig=(k == 7))
            mean = RL[0][:, 0:256]
            x = V.ts(mean, PS[6][:, 0:256], 1.0 / C, None, ALU.mult, None, t)
            y = V.tt(CV, CV, mean.unsqueeze(1).broadcast_to([128, 8, 256]), ALU.subtract, x)
            SQC = UB.rearrange("p k t -> p (k t)")[:, 0:2048]
            x = S.act(SQC, CVf, ACT.Square, y)
            for k in range(KT):
                t = E.mm(PS[6][:, 256:512], cst('ones'), SQC[:, k * 256:k * 256 + 256], k == 0, k == 7, x, sig=(k == 7))
            rst = RL[1][:, 0:256]
            y = V.ts(rst, PS[6][:, 256:512], 1.0 / C, EPS, ALU.mult, ALU.add, t)
            bank_free[6] = y
            y = S.act(rst, rst, ACT.Sqrt, y)
            y = V.op(lambda e: e.reciprocal(rst, rst), (y,))
            y = V.tt(CV, CV, rst.unsqueeze(1).broadcast_to([128, 8, 256]), ALU.mult, y)
            for k in range(KT):
                cv = S.act(CV[:, k, :], CV[:, k, :], ACT.Silu, y, scale=vec('cln_g', k), bias=vec('cln_b', k))
            gm = []

            def ev_mul(dst):
                def ev(j, b, t):
                    d = dst[:, 2 * j:2 * j + 2, :]
                    gm.append(V.tt(d, d, b, ALU.mult, t))
                    return gm[-1]
                return ev
            mode_b(a['w_attn_out'], 0, 4, lambda k: OT[:, k, :], ev_mul(GA), [0, 1], outs)
            mode_b(a['w_conv_out'], 0, 4, lambda k: CV[:, k, :], ev_mul(GC), [2, 3], cv)
            gm.append(V.tt(GA, GA, GC, ALU.add, gm[-1]))

            def add_h(h, tt, b, t):
                hs = H[:, tt, h * 512:h * 512 + 512]
                hx.append(V.tt(hs, hs, b, ALU.add, t))
                return hx[-1]
            hx = []
            mode_a(a['w_mix_out'], 0, 2, lambda k, tt: GA[:, k, tt * 128:tt * 128 + 128], add_h, [4, 6, 5, 7], gm[-1])
            if debug == 'mix2':
                return finish(H, hx)

            nrm = rms_norm(H, hx)
            xt = to_chan(S1, XT, nrm, [0, 1, 2, 3], 'nx')
            QX = QQ
            mode_b(a['wx_q'], 0, 2, lambda k: XT[:, k, :], ev_to(QX), [4, 5], xt)
            outs = attention(4, lambda h: QX[:, h, :], lambda h: KX[:, h, :], lambda h, s: VX[:, s, h * 128:h * 128 + 128],
                             lambda h: (slice(0, 128), OT[:, h, :], True), 1, 128 ** -0.5, False, TMP, [q_t[-1]])
            hx = []
            mode_a(a['wx_o'], 0, 2, lambda k, tt: OT[:, k, tt * 128:tt * 128 + 128], add_h, [4, 6, 5, 7], outs, nk=4)
            nrm = rms_norm(H, hx)
            to_chan(S1, XT, nrm, [0, 1, 2, 3], 'nffn')
            if debug == 'cross':
                return finish(H, hx)
            fence()
            t = ffn(a['w_ff1'], a['w_ff2'], 16, False)
            hx = []
            for tt in range(2):
                for h in range(2):
                    add_h(h, tt, PS[4 + 2 * tt + h][:, :], t)
            pc = load((lambda r: r[:, 0:1024], a['nfin'].broadcast_to([128, 1024])))
            nrm = rms_norm(H, hx)
            fin = V.tt(S1, S1, pc.ap[:, 0:1024].unsqueeze(1).broadcast_to([128, 2, 1024]), ALU.mult, nrm, pc.tok)
            finish(S1, fin)

        HV = ctx.enter_context(nc.sbuf_tensor("HV", [128, 16], F32))
        D.items.append(lambda e: None)

        def prologue():
            i = VECS.index('w0h') * 8
            return V.ts(HV[:, :], VB[:, i:i + 16], 0.5, None, ALU.mult, None, (s_c.sem, 32))
        S.wait(prologue())
        run()

        block = ctx.enter_context(nc.Block())

        @block.vector
        def _(e):
            for f in V.items:
                f(e)

        @block.scalar
        def _(e):
            for f in S.items:
                f(e)

        @block.gpsimd
        def _(e):
            for f in G.items:
                f(e)

        @block.tensor
        def _(e):
            for f in E.items:
                f(e)

        @block.sync
        def _(e):
            for f in D.items:
                f(e)


def vectors(i):
    g = {'w0h': i['rwkv_w0'][0], 'a0h': i['rwkv_a0'][0], 'k_k': i['rwkv_k_k'][0], 'k_a': i['rwkv_k_a'][0],
         'r_k': i['rwkv_r_k'][0].reshape(-1), 'conv_b': i['conv_b_2'][0], 'cln_g': i['conv_ln_g_2'][0],
         'cln_b': i['conv_ln_b_2'][0], 'nmix': i['norm_mix_g_2'][0], 'nx': i['norm_x_g_2'][0],
         'nmem': i['norm_mem_g_2'][0], 'nffn': i['norm_ffn_g_2'][0], 'bgc': i['b_gate_2'][0, 0:C],
         'bga': i['b_gate_2'][0, C:2 * C]}
    for n in range(6):
        g[f'mu{n}'] = i['rwkv_mu'][0, n]
    for n in range(31):
        g[f'cw{n}'] = i['conv_w_2'][0, n]
    for l in range(2):
        g[f'mixg{l}'], g[f'mixb{l}'] = i['ln_mix_g'][l], i['ln_mix_b'][l]
        g[f'ffng{l}'], g[f'ffnb{l}'] = i['ln_ffn_g'][l], i['ln_ffn_b'][l]
    return np.ascontiguousarray(np.concatenate([g[n].reshape(8, 128).T for n in VECS], 1))


DEBUG = None


def kernel(**inputs):
    import numpy as _np
    import concourse.bacc as _bacc
    from concourse import mybir as _mybir
    from concourse.bass_utils import run_bass_kernel_spmd as _run

    i = {k: _np.asarray(v) for k, v in inputs.items()}
    arrays = {
        'cst': constants(), 'vec': vectors(i), 'xT': i['x'][0].T, 'x': i['x'][0], 'mem': i['mem_2'][0],
        'w_rkv': i['rwkv_w_rkv'][0], 'w1': i['rwkv_w1'][0], 'a1': i['rwkv_a1'][0], 'g1': i['rwkv_g1'][0],
        'w2': i['rwkv_w2'][0], 'a2': i['rwkv_a2'][0], 'g2': i['rwkv_g2'][0], 'gn_g': i['rwkv_gn_g'],
        'gn_b': i['rwkv_gn_b'], 'w_o': i['rwkv_w_o'][0], 'moba_w_qkv': i['moba_w_qkv'][0],
        'moba_w_o': i['moba_w_o'][0], 'ffn_w_in': i['ffn_w_in'], 'ffn_w_down': i['ffn_w_down'],
        'lnmg': i['ln_mix_g'], 'lnmb': i['ln_mix_b'], 'lnfg': i['ln_ffn_g'], 'lnfb': i['ln_ffn_b'],
        'w_in2': i['w_in_2'][0], 'w_conv_out': i['w_conv_out_2'][0], 'w_attn_out': i['w_attn_out_2'][0],
        'w_mix_out': i['w_mix_out_2'][0], 'wx_q': i['wx_q_2'][0], 'wx_kv': i['wx_kv_2'][0], 'wx_o': i['wx_o_2'][0],
        'w_ff1': i['w_ff1_2'][0], 'w_ff2': i['w_ff2_2'][0], 'nfin': i['norm_final_g_2'].reshape(1, C),
    }
    nc = _bacc.Bacc("TRN2", target_bir_lowering=False, num_devices=1)
    feed, aps = {}, {}
    for name, v in arrays.items():
        v = _np.ascontiguousarray(v)
        feed[f"in_{name}"] = v
        aps[name] = nc.dram_tensor(f"in_{name}", v.shape, _mybir.dt.from_np(v.dtype), kind="ExternalInput").ap()
    out = nc.dram_tensor("out_y", (1, T, C), F32, kind="ExternalOutput").ap()
    build(nc, aps, out, DEBUG)
    r = _run(nc, [feed], core_ids=[0])
    return r.results[0]["out_y"]
```

```python
from contextlib import ExitStack

import numpy as np
import concourse.bass as bass
from concourse import mybir

F32 = mybir.dt.float32
F32R = mybir.dt.float32r
ALU = mybir.AluOpType
ACT = mybir.ActivationFunctionType
AX = mybir.AxisListType.X

C = 1024
T = 256
KT = 8
FF = 2816
FF2 = 4096
ALPHA = 4 ** 0.25
CDEC = float(np.exp(-0.5))
GN_EPS = 64e-5
LN_EPS = 1e-5
EPS = 1e-6
NEG = -1e30
TAKEN = -3e38

VECS = ['mu0', 'mu1', 'mu2', 'mu3', 'mu4', 'mu5', 'w0h', 'a0h', 'k_k', 'k_a', 'r_k',
        'mixg0', 'mixb0', 'ffng0', 'ffnb0', 'mixg1', 'mixb1', 'ffng1', 'ffnb1',
        'conv_b', 'cln_g', 'cln_b', 'nmix', 'nx', 'nmem', 'nffn', 'bgc', 'bga'] + [f'cw{i}' for i in range(31)]
CST = {}
_at = 0
for _n, _w in [('ident', 128), ('atm', 512), ('lvl', 896), ('m0t', 128), ('bones', 128), ('ones', 128),
               ('sel2', 2), ('pad', 14), ('perm', 128), ('cmask', 384), ('c01', 384), ('cos', 256), ('sin', 256)]:
    CST[_n] = (_at, _w)
    _at += _w
NCST = _at


def constants():
    a = np.zeros((128, NCST), np.float32)
    p = np.arange(128)[:, None]
    f = np.arange(128)[None, :]

    def put(name, v):
        o, w = CST[name]
        a[:, o:o + w] = v

    put('ident', p == f)
    put('atm', np.concatenate([p < f, p <= f, p < f, p <= f], 1))
    put('lvl', np.concatenate([((p >> (l + 1)) == (f >> (l + 1))) & ((p >> l) & 1 == 1) & ((f >> l) & 1 == 0)
                               for l in range(7)], 1))
    put('m0t', ((f >> 1) == (p >> 1)) & (f & 1 == 1) & (p & 1 == 0))
    put('bones', (p // 64) == (f // 64))
    put('ones', 1.0)
    put('sel2', (p // 64) == np.arange(2)[None, :])
    n_out, n_in = f % 64, p % 64
    same = (p // 64) == (f // 64)
    put('perm', np.where(same & (n_out < 32) & (n_in == n_out + 32), -1.0, 0.0)
        + np.where(same & (n_out >= 32) & (n_in == n_out - 32), 1.0, 0.0))
    t1 = np.arange(256)[None, :] - 128
    ok = np.concatenate([f <= p, t1 <= p], 1)
    put('cmask', np.where(ok, 0.0, NEG))
    put('c01', ok)
    inv = (np.float32(10000.0) ** (-np.arange(0, 64, 2, dtype=np.float32) / np.float32(64))).astype(np.float32)
    ang = np.arange(T, dtype=np.float32)[None, :] * inv[:, None]
    put('cos', np.tile(np.cos(ang), (4, 1)))
    put('sin', np.tile(np.sin(ang), (4, 1)))
    return a


class Queue:

    def __init__(self, sem):
        self.sem = sem
        self.reset()

    def reset(self):
        self.n, self.items, self.seen = 0, [], {}

    def wait(self, *toks):
        for t in toks:
            if t is None:
                continue
            if isinstance(t, list):
                self.wait(*t)
                continue
            s, v = t
            if self.seen.get(id(s), 0) < v:
                self.seen[id(s)] = v
                self.items.append(lambda e, s=s, v=v: e.wait_ge(s, v))

    def op(self, f, toks, sig=True):
        self.wait(*toks)
        if not sig:
            self.items.append(f)
            return None
        self.n += 1
        s = self.sem
        self.items.append(lambda e: f(e).then_inc(s, 1))
        return (s, self.n)

    @property
    def last(self):
        return (self.sem, self.n) if self.n else None

    def tt(self, out, a, b, op, *after):
        return self.op(lambda e: e.tensor_tensor(out, a, b, op), after)

    def ts(self, out, a, s1, s2, op0, op1, *after):
        if op1 is None:
            return self.op(lambda e: e.tensor_scalar(out, a, s1, None, op0), after)
        return self.op(lambda e: e.tensor_scalar(out, a, s1, s2, op0, op1), after)

    def stt(self, out, a, s, b, op0, op1, *after):
        return self.op(lambda e: e.scalar_tensor_tensor(out=out, in0=a, scalar=s, in1=b, op0=op0, op1=op1), after)

    def act(self, out, a, func, *after, scale=1.0, bias=0.0, accum=None):
        if accum is None:
            return self.op(lambda e: e.activation(out, a, func, bias=bias, scale=scale), after)
        return self.op(lambda e: e.activation(out, a, func, bias=bias, scale=scale, accum_out=accum), after)

    def mm(self, out, l, r, start, stop, *after, sig=False):
        return self.op(lambda e: e.matmul(out, l, r, start=start, stop=stop), after, sig)

    def tr(self, out, a, ident, *after, sig=False):
        return self.op(lambda e: e.transpose(out, a, ident), after, sig)


class PerK(list):
    pass


class Counter:

    def __init__(self, sem):
        self.sem, self.v = sem, 0

    def dma(self, q, out, src, *after):
        q.wait(*after)
        self.v += 16
        s = self.sem
        q.items.append(lambda e: e.dma_start(out, src).then_inc(s, 16))
        return (s, self.v)


NRING = 3
NW = 3
NLOW = 4096 + 2 * NW * 2048
NPA = NLOW + 18080


def build(nc, a, out, debug=None):
    ctx = ExitStack()
    with ctx:
        CB = ctx.enter_context(nc.sbuf_tensor("CB", [128, NCST], F32))
        VB = ctx.enter_context(nc.sbuf_tensor("VB", [128, len(VECS) * 8], F32))
        RG = ctx.enter_context(nc.sbuf_tensor("RG", [128, NRING, 2048], F32))
        Hb = ctx.enter_context(nc.sbuf_tensor("Hb", [128, 2048], F32))
        Sb = ctx.enter_context(nc.sbuf_tensor("Sb", [128, 2048], F32))
        Xb = ctx.enter_context(nc.sbuf_tensor("Xb", [128, 2048], F32))
        KX = ctx.enter_context(nc.sbuf_tensor("KX", [128, 4, 256], F32))
        VX = ctx.enter_context(nc.sbuf_tensor("VX", [128, 2, 512], F32))
        ST = ctx.enter_context(nc.sbuf_tensor("ST", [128, 512], F32))
        HV = ctx.enter_context(nc.sbuf_tensor("HV", [128, 16], F32))
        with nc.sbuf_tensor("PA", [128, NPA], F32) as PA:
            pass
        AH = ctx.enter_context(nc.sbuf_tensor("AH", [128, 2048], F32R))
        AL = ctx.enter_context(nc.sbuf_tensor("AL", [128, 2048], F32R))
        WH = ctx.enter_context(nc.sbuf_tensor("WH", [128, NW, 2048], F32R))
        WL = ctx.enter_context(nc.sbuf_tensor("WL", [128, NW, 2048], F32R))
        with nc.sbuf_tensor("PF", [128, 2048], F32) as PF, nc.sbuf_tensor("HH", [128, 2, 512], F32R) as HH, \
                nc.sbuf_tensor("HL", [128, 2, 512], F32R) as HL:
            pass
        PH = ctx.enter_context(nc.sbuf_tensor("PH", [128, NPA - NLOW], F32))
        PS = [ctx.enter_context(nc.psum_tensor(f"PS{i}", [128, 512], F32)) for i in range(8)]

        def sem(n):
            return ctx.enter_context(nc.semaphore(n))

        names = ("s_dve", "s_act", "s_pool", "s_pe", "s_sp")
        V, S, G, E, D = (Queue(sem(n)) for n in names)
        s_c = Counter(sem("s_const"))
        s_io = Counter(sem("s_io"))
        s_x = Counter(sem("s_x"))
        s_out = Counter(sem("s_out"))

        class Stream:
            plan, at, dma_n, prep_n, wn, rate = None, 0, 0, 0, 0, 0

        st = Stream()
        st.beside = []
        st.spec, st.pieces, st.owner, st.wowner = [], [], [None] * 5, [None] * NW
        st.sems = [Counter(sem(f"s_ring{i}")) for i in range(5)]

        def cst(n):
            o, w = CST[n]
            return CB[:, o:o + w]

        def vec(n, k):
            i = VECS.index(n) * 8 + k
            return VB[:, i:i + 1]

        ident = cst('ident')
        bank_free = [None] * 8

        class Piece:
            pass

        def load(*parts, split=False, early=False):
            i = st.at
            st.at += 1
            if st.plan is None:
                st.spec.append((parts, split, early))
                p = Piece()
                p.i, p.tok, p.ap, p.h, p.l = i, None, RG[:, 0, :], WH[:, 0, :], WL[:, 0, :]
                background()
                return p
            pump(i)
            background()
            return st.pieces[i]

        def free(p, *toks):
            if st.plan is None:
                return
            p.used = list(toks)

        def background(n=None):
            for _ in range(min(st.rate if n is None else n, len(st.beside))):
                st.beside.pop(0)()

        def slot_of(i, early):
            if early:
                n = i % 5
                return RG[:, n, :] if n < 3 else PA[:, NPA - (n - 2) * 2048:NPA - (n - 3) * 2048]
            return RG[:, i % 3, :]

        def pump(i):
            while True:
                moved = False
                if st.dma_n < len(st.plan):
                    n = st.dma_n
                    parts, split, early = st.plan[n]
                    key = (n % 5) if early else (n % 3)
                    prev = st.owner[key]
                    if prev is None or prev.raw_free() is not None:
                        p = Piece()
                        p.i, p.split, p.used, p.done = n, split, None, None
                        p.raw_free = lambda p=p: p.done if p.split else p.used
                        p.ap = slot_of(n, early)
                        if prev is not None:
                            D.wait(prev.raw_free())
                        for dst, src in parts:
                            p.tok = st.sems[key].dma(D, dst(p.ap), src)
                        st.owner[key] = p
                        st.pieces.append(p)
                        st.dma_n += 1
                        moved = True
                n = st.prep_n
                if n <= i + 2 and n < len(st.pieces):
                    p = st.pieces[n]
                    if not p.split:
                        st.prep_n += 1
                        moved = True
                    elif st.wowner[st.wn % NW] is None or st.wowner[st.wn % NW].used is not None:
                        w = st.wn % NW
                        prev = st.wowner[w]
                        rel = prev.used if prev is not None else None
                        p.h, p.l = WH[:, w, :], WL[:, w, :]
                        x = S.act(p.h, p.ap, ACT.Copy, p.tok, rel)
                        y = V.tt(p.l, p.ap, p.h.bitcast(F32), ALU.subtract, x)
                        p.done = [x, y]
                        p.tok = y
                        st.wowner[w] = p
                        st.wn += 1
                        st.prep_n += 1
                        moved = True
                if not moved:
                    break
            assert i < st.prep_n, i

        def split_act(src, ready):
            ts_ = []
            for c in range(2):
                sl = slice(c * 1024, c * 1024 + 1024)
                x = S.act(AH[:, sl], src[:, sl], ACT.Copy, ready, E.last)
                ts_.append(V.tt(AL[:, sl], src[:, sl], AH[:, sl].bitcast(F32), ALU.subtract, x))
            return ts_

        def rk(ready, k):
            return ready[k // 2] if isinstance(ready, PerK) else ready

        def mm3(out, l, r, start, stop, *after, sig=False):
            (lh, ll), (rh, rl) = l, r
            E.mm(out, lh, rh, start, False, *after)
            E.mm(out, lh, rl, False, False)
            return E.mm(out, ll, rh, False, stop, sig=sig)

        def hl(f):
            return f(AH), f(AL)

        def act_k(k):
            return hl(lambda a_: a_[:, k * 256:k * 256 + 256])

        def act_kt(k, tt):
            return hl(lambda a_: a_[:, k * 256 + tt * 128:k * 256 + tt * 128 + 128])

        def wsl(pc, n, k, c0, c1):
            return v3(pc.h, n)[:, k, c0:c1], v3(pc.l, n)[:, k, c0:c1]

        def wcols(W, c0, n, k0=0, kn=KT):
            src = W[k0 * 128:(k0 + kn) * 128, c0:c0 + n].rearrange("(k p) n -> p k n", p=128)
            return (lambda r: r[:, 0:kn * n].rearrange("p (k n) -> p k n", k=kn)), src

        def v3(ap, n):
            return ap.rearrange("p (a n) -> p a n", n=n)

        def fence():
            toks = [V.last, S.last, G.last, E.last]
            for q in (V, S, G, E):
                q.wait(*toks)
            return toks

        H = Hb[:, :].rearrange("p (t c) -> p t c", t=2)
        S1 = Sb[:, :].rearrange("p (t c) -> p t c", t=2)
        XT = Xb[:, :].rearrange("p (k t) -> p k t", k=8)

        def mode_b(W, c0, npair, evac, banks, ready, rhs=None, nk=KT):
            for j in range(npair):
                pc = load(wcols(W, c0 + 256 * j, 256), split=rhs is None, early=rhs is not None)
                b = banks[j % len(banks)]
                for m in range(2):
                    for k in range(nk):
                        o_ = PS[b][:, m * 256:(m + 1) * 256]
                        if rhs is None:
                            t = mm3(o_, wsl(pc, 256, k, m * 128, m * 128 + 128), act_k(k), k == 0, k == nk - 1,
                                    pc.tok, bank_free[b], rk(ready, k), sig=(m == 1 and k == nk - 1))
                        else:
                            t = E.mm(o_, v3(pc.ap, 256)[:, k, m * 128:(m + 1) * 128], rhs(k),
                                     k == 0, k == nk - 1, pc.tok, bank_free[b], rk(ready, k), sig=(m == 1 and k == nk - 1))
                free(pc, t)
                bank_free[b] = evac(j, PS[b][:, :].rearrange("p (m t) -> p m t", m=2), t)

        def mode_a(W, c0, nhalf, evac, banks, ready, lhs=None, nk=KT):
            for h in range(nhalf):
                bb = [banks[(2 * h + tt) % len(banks)] for tt in range(2)]
                for kp in range(nk // 4):
                    pc = load(wcols(W, c0 + 512 * h, 512, 4 * kp, 4), split=lhs is None, early=lhs is not None)
                    for tt in range(2):
                        for k in range(4):
                            kk = 4 * kp + k
                            args = (kk == 0, kk == nk - 1, pc.tok, bank_free[bb[tt]], rk(ready, kk))
                            if lhs is None:
                                t = mm3(PS[bb[tt]][:, :], act_kt(kk, tt), wsl(pc, 512, k, 0, 512), *args, sig=(k == 3))
                            else:
                                t = E.mm(PS[bb[tt]][:, :], lhs(kk, tt), v3(pc.ap, 512)[:, k, :], *args, sig=(k == 3))
                        if kk == nk - 1:
                            bank_free[bb[tt]] = evac(h, tt, PS[bb[tt]][:, :], t)
                    free(pc, t)

        def to_chan(src, dst, ready, banks, g=None, b=None, split=True):
            toks = PerK()
            for kp in range(4):
                bk = banks[kp % len(banks)]
                for m in range(2):
                    for tt in range(2):
                        k = 2 * kp + m
                        t = E.tr(PS[bk][:, (2 * m + tt) * 128:(2 * m + tt + 1) * 128],
                                 src[:, tt, k * 128:(k + 1) * 128], ident, ready, bank_free[bk],
                                 sig=(m == 1 and tt == 1))
                rel = []
                for m in range(2):
                    k = 2 * kp + m
                    pv = PS[bk][:, m * 256:(m + 1) * 256]
                    if kp % 2 == 0 and g is not None:
                        e = S.act(dst[:, k, :], pv, ACT.Identity, t, scale=vec(g, k), bias=(vec(b, k) if b else 0.0))
                    elif g is not None:
                        if b:
                            e = V.ts(dst[:, k, :], pv, vec(g, k), vec(b, k), ALU.mult, ALU.add, t)
                        else:
                            e = V.ts(dst[:, k, :], pv, vec(g, k), None, ALU.mult, None, t)
                    elif kp % 2 == 0:
                        e = S.act(dst[:, k, :], pv, ACT.Copy, t)
                    else:
                        e = V.op(lambda q, o=dst[:, k, :], i=pv: q.tensor_copy(o, i), (t,))
                    rel.append(e)
                bank_free[bk] = rel
                if split:
                    sl = slice(kp * 512, kp * 512 + 512)
                    d = dst.rearrange("p k t -> p (k t)")[:, sl]
                    x = S.act(AH[:, sl], d, ACT.Copy, rel, E.last)
                    toks.append(V.tt(AL[:, sl], d, AH[:, sl].bitcast(F32), ALU.subtract, x))
                else:
                    toks.append(rel)
            return toks

        def rstd_of(var, o, eps, scale, ready):
            t = V.ts(o, var, scale, eps, ALU.mult, ALU.add, ready)
            t = S.act(o, o, ACT.Sqrt, t)
            return V.op(lambda e: e.reciprocal(o, o), (t,))

        def rms_norm(src, ready):
            ts_ = []
            for tt in range(2):
                ts_.append(S.act(S1[:, tt, :], src[:, tt, :], ACT.Square, ready, accum=ST[:, tt:tt + 1]))
            r = rstd_of(ST[:, 0:2], ST[:, 2:4], EPS, 1.0 / C, ts_)
            return [V.ts(S1[:, tt, :], src[:, tt, :], ST[:, 2 + tt:3 + tt], None, ALU.mult, None, r) for tt in range(2)]

        def residual_ln(banks, toks, gi, bi, gname, bname, halves_first=False, extra=None):
            def part(tt, h):
                sl = slice(h * 512, h * 512 + 512)
                b = banks[2 * tt + h]
                e = V.stt(S1[:, tt, sl], H[:, tt, sl], ALPHA, PS[b][:, :], ALU.mult, ALU.add, toks[2 * tt + h], G.last, extra)
                bank_free[b] = e
                o_ = ST[:, 16 + 12 * tt + 6 * h:22 + 12 * tt + 6 * h]
                return V.op(lambda q, o=o_, i=S1[:, tt, sl]: q.bn_stats(o, i), (e,))
            if halves_first:
                part(0, 0), part(1, 0)
            n = []
            for tt in range(2):
                if not halves_first:
                    part(tt, 0)
                e = part(tt, 1)
                e = V.op(lambda q, o=ST[:, 8 + 2 * tt:10 + 2 * tt], i=ST[:, 16 + 12 * tt:28 + 12 * tt]: q.bn_aggr(o, i),
                         (V.last,))
                r = rstd_of(ST[:, 9 + 2 * tt:10 + 2 * tt], ST[:, 2 + tt:3 + tt], LN_EPS, 1.0, e)
                n.append(V.ts(S1[:, tt, :], S1[:, tt, :], ST[:, 8 + 2 * tt:9 + 2 * tt], ST[:, 2 + tt:3 + tt],
                              ALU.subtract, ALU.mult, r))
            pc = load((lambda r_: r_[:, 0:1024], gi.broadcast_to([128, 1024])),
                      (lambda r_: r_[:, 1024:2048], bi.broadcast_to([128, 1024])))
            x = to_chan(S1, XT, n, [0, 1, 2, 3], gname, bname)
            for tt in range(2):
                e = G.tt(H[:, tt, :], S1[:, tt, :], pc.ap[:, 0:1024], ALU.mult, n, pc.tok)
                e = G.tt(H[:, tt, :], H[:, tt, :], pc.ap[:, 1024:2048], ALU.add, e)
            free(pc, e)
            return x

        def attention(nh, q, k, v, outp, od, scale, causal, tmp, ready, mask=None, mask_tok=None, banks=(0, 1, 2, 3, 4, 5)):
            W = 384 if causal else 512
            Sm, P, PT = (v3(tmp[:, i * 1024:(i + 1) * 1024], 512) for i in range(3))
            sp = [(0, 128), (128, 384)] if causal else [(0, 256), (256, 512)]
            stt_ = ST[:, 64:64 + 16].rearrange("p (s n) -> p s n", n=8)
            sc_t, sm_free, p_t, p_free, pt_t, pt_free = {}, {}, {}, {}, {}, {}
            outs = []
            for i in range(nh + 2):
                if i < nh:
                    b = banks[i % 2]
                    for tt in range(2):
                        lo, hi = sp[tt]
                        t = E.mm(PS[b][:, lo:hi], q(i)[:, tt * 128:tt * 128 + 128], k(i)[:, 0:hi - lo], True, True,
                                 bank_free[b], ready, sig=(tt == 1))
                    s = stt_[:, i % 2, :]
                    if mask is not None:
                        for tt in range(2):
                            lo, hi = sp[tt]
                            e = V.op(lambda qq, o=Sm[:, i % 2, lo:hi], x=PS[b][:, lo:hi], m=mask[:, lo:hi], ac=s[:, tt:tt + 1]:
                                     qq.tensor_tensor_reduce(o, x, m, 1.0, TAKEN, ALU.add, ALU.max, ac),
                                     (t, mask_tok, sm_free.get(i - 2)))
                        bank_free[b] = e
                        src = Sm[:, i % 2, :]
                    else:
                        e = V.op(lambda qq, o=s[:, 0:2], x=PS[b][:, :].rearrange("p (t s) -> p t s", t=2):
                                 qq.tensor_reduce(o, x, AX, ALU.max), (t, sm_free.get(i - 2)))
                        src = PS[b][:, :]
                    e = V.ts(s[:, 2:4], s[:, 0:2], -scale, None, ALU.mult, None, e)
                    for tt in range(2):
                        lo, hi = sp[tt]
                        x = S.act(P[:, i % 2, lo:hi], src[:, lo:hi], ACT.Exp, e, p_free.get(i - 2), scale=scale,
                                  bias=s[:, 2 + tt:3 + tt], accum=s[:, 4 + tt:5 + tt])
                    sm_free[i] = x
                    if mask is None:
                        bank_free[b] = x
                    e = V.op(lambda qq, o=s[:, 6:8], ii=s[:, 4:6]: qq.reciprocal(o, ii), (x,))
                    for tt in range(2):
                        lo, hi = sp[tt]
                        p_t[i] = V.ts(P[:, i % 2, lo:hi], P[:, i % 2, lo:hi], s[:, 6 + tt:7 + tt], None, ALU.mult, None, e)
                if 1 <= i <= nh:
                    h = i - 1
                    b = banks[2 + h % 2]
                    p = P[:, h % 2, :]
                    if causal:
                        blocks = [(0, 0), (128, 128), (256, 256)]
                    else:
                        blocks = [(0, 0), (128, 256), (256, 128), (384, 384)]
                    for n, (dst, s0) in enumerate(blocks):
                        t = E.tr(PS[b][:, dst:dst + 128], p[:, s0:s0 + 128], ident, p_t[h], bank_free[b],
                                 sig=(n == len(blocks) - 1))
                    p_free[h] = t
                    x = S.act(PT[:, h % 2, 0:W], PS[b][:, 0:W], ACT.Copy, t, pt_free.get(h - 2))
                    bank_free[b] = x
                    pt_t[h] = x
                if i >= 2:
                    h = i - 2
                    parts, dst, last = outp(h)
                    b = banks[4 + (h // od) % 2]
                    pt = PT[:, h % 2, :]
                    E.mm(PS[b][parts, 0:256], v(h, 0), pt[:, 0:256], True, False, pt_t[h], bank_free[b])
                    if causal:
                        t = E.mm(PS[b][parts, 128:256], v(h, 1), pt[:, 256:384], False, True, sig=True)
                    else:
                        t = E.mm(PS[b][parts, 0:256], v(h, 1), pt[:, 256:512], False, True, sig=True)
                    pt_free[h] = t
                    if last:
                        x = S.act(dst, PS[b][:, 0:256], ACT.Copy, t)
                        bank_free[b] = x
                        outs.append(x)
            return outs

        def ffn(w_in, w_down, n, gated, ready):
            GT = v3(PF[:, 0:1024], 512)
            HT = v3(PF[:, 1024:2048], 512)
            F = 256 * n
            hfree, gfree, ht = {}, {}, {}

            def down(j):
                pd = load(wcols(w_down, 0, 1024, 2 * j, 2), split=True)
                done = []
                for tt in range(2):
                    for h in range(2):
                        bb = 4 + 2 * tt + h
                        for m in range(2):
                            c0 = m * 256 + tt * 128
                            t = mm3(PS[bb][:, :], (HH[:, j % 2, c0:c0 + 128], HL[:, j % 2, c0:c0 + 128]),
                                    wsl(pd, 1024, m, h * 512, h * 512 + 512), j == 0 and m == 0, j == n - 1 and m == 1,
                                    pd.tok, ht[j], bank_free[bb], sig=(m == 1))
                        done.append(t)
                free(pd, t)
                hfree[j] = t
                return done

            for j in range(n + 1):
                if j < n:
                    for u in range(2 if gated else 1):
                        pc = load(wcols(w_in, u * F + 256 * j, 256), split=True)
                        b = (2 * (j % 2) + u) if gated else j % 4
                        for m in range(2):
                            for k in range(KT):
                                t = mm3(PS[b][:, m * 256:m * 256 + 256], wsl(pc, 256, k, m * 128, m * 128 + 128), act_k(k),
                                        k == 0, k == 7, pc.tok, bank_free[b], rk(ready, k), sig=(m == 1 and k == 7))
                        free(pc, t)
                        if u == 0:
                            g = S.act(GT[:, j % 2, :], PS[b][:, :], ACT.Silu if gated else ACT.Relu, t, gfree.get(j - 2))
                            if gated:
                                bank_free[b] = g
                    f = HT[:, j % 2, :]
                    x = V.tt(f, GT[:, j % 2, :], PS[b][:, :], ALU.mult, g, t)
                    bank_free[b] = x
                    gfree[j] = x
                    x = S.act(HH[:, j % 2, :], f, ACT.Copy, x, hfree.get(j - 2))
                    ht[j] = V.tt(HL[:, j % 2, :], f, HH[:, j % 2, :].bitcast(F32), ALU.subtract, x)
                if j >= 1:
                    t = down(j - 1)
            for b in range(4, 8):
                bank_free[b] = None
            return t

        def finish(src, ready):
            t = s_out.dma(D, out[0].rearrange("(t p) c -> p t c", p=128), src, ready)
            D.wait(t)

        def run():
            s_c.dma(D, CB[:, :], a['cst'])
            tm = s_io.dma(D, H, a['mem'].rearrange("(t p) c -> p t c", p=128))
            tx = s_x.dma(D, XT, a['xT'].rearrange("(k p) t -> p k t", p=128))
            tc = s_c.dma(D, VB[:, :], a['vec'])
            for q in (V, S, G, E):
                q.wait(tc)

            o = 0

            def take(n):
                nonlocal o
                r = area[:, o:o + n]
                o += n
                assert o <= area.shape[1], o
                return r

            area = PA
            o = NLOW

            VV = take(2048).rearrange("p (t c) -> p t c", t=2)
            YY = take(2048).rearrange("p (t c) -> p t c", t=2)
            SG = take(512).rearrange("p (m t) -> p m t", m=2)
            AR = take(4096).rearrange("p (m c s t) -> p m c s t", m=8, c=2, s=2)
            BE = take(2048).rearrange("p (m t) -> p m t", m=8)
            KA = take(2048).rearrange("p (m t) -> p m t", m=8)
            DX = take(8)
            assert o <= NPA - 4096
            o = 0
            BV = PA[:, NLOW - 2048:NLOW].rearrange("p (t c) -> p t c", t=2)
            XX = take(2048).rearrange("p (k t) -> p k t", k=8)
            XM = [take(2048).rearrange("p (k t) -> p k t", k=8) for _ in range(2)]
            P2 = take(2048)
            TW = take(256)
            TA = take(256)
            cs = take(516).rearrange("p (a t) -> p a t", t=129)
            EE = take(516).rearrange("p (a t) -> p a t", t=129)
            EI, sg, aa, kS, rS, kk = (take(512) for _ in range(6))
            assert o <= NLOW - 2048

            nrm = rms_norm(H, [tm])
            MT = YY.rearrange("p t c -> p (t c)").rearrange("p (k t) -> p k t", k=8)
            mt = to_chan(S1, MT, nrm, [4, 5, 6, 7], 'nmem', split=False)

            def ev_kx(j, b, t):
                return S.act(KX[:, 2 * j:2 * j + 2, :], b, ACT.Copy, t)
            mode_b(a['wx_kv'], 0, 2, ev_kx, [0, 1], mt, rhs=lambda k: MT[:, k, :])

            def ev_vx(h, tt, b, t):
                return S.act(VX[:, tt, :], b, ACT.Copy, t)
            mode_a(a['wx_kv'], 512, 1, ev_vx, [2, 3], mt, lhs=lambda k, tt: MT[:, k, tt * 128:tt * 128 + 128])

            w = V.tt(XX[:, :, 1:256], XT[:, :, 0:255], XT[:, :, 1:256], ALU.subtract, tx)
            w = V.ts(XX[:, :, 0:1], XT[:, :, 0:1], -1.0, None, ALU.mult, None, w)
            mset = G.op(lambda e: e.memset(cs[:, :, 0:1], 0.0), ())
            xm_free = [None] * 2

            def mix(i, n):
                slot = i % 2
                for k in range(KT):
                    t = V.stt(XM[slot][:, k, :], XX[:, k, :], vec(f'mu{n}', k), XT[:, k, :], ALU.mult, ALU.add,
                              w, xm_free[slot])
                return slot, t

            pc = load((lambda r: v3(r[:, 0:512], 64), a['w1'].rearrange("(k p) n -> p k n", p=128)),
                      (lambda r: v3(r[:, 512:1024], 64), a['a1'].rearrange("(k p) n -> p k n", p=128)), early=True)
            pg = load((lambda r: v3(r[:, 0:1280], 160), a['g1'].rearrange("(k p) n -> p k n", p=128)), early=True)
            s_io.dma(D, P2[0:64, 0:1024], a['w2'])
            p2t = s_io.dma(D, P2[0:64, 1024:2048], a['a2'])
            for i, (n, fn, dst) in enumerate([(1, ACT.Tanh, TW), (4, ACT.Copy, TA)]):
                slot, t = mix(i, n)
                wv = v3(pc.ap[:, i * 512:(i + 1) * 512], 64)
                for k in range(KT):
                    e = E.mm(PS[5 + i][0:64, 0:256], wv[:, k, :], XM[slot][:, k, :], k == 0, k == 7,
                             t, pc.tok, bank_free[5 + i], sig=(k == 7))
                xm_free[slot] = e
                low = S.act(dst[0:64, :], PS[5 + i][0:64, 0:256], fn, e)
            free(pc, e)
            slot, t = mix(2, 5)
            wv = v3(pg.ap[:, 0:1280], 160)
            for m, (c0, c1) in enumerate([(0, 128), (128, 160)]):
                for k in range(KT):
                    e = E.mm(PS[7 - 4 * m][0:c1 - c0, 0:256], wv[:, k, c0:c1], XM[slot][:, k, :],
                             k == 0, k == 7, t, pg.tok, bank_free[7 - 4 * m], sig=(k == 7))
                sgt = S.act(SG[0:c1 - c0, m, :], PS[7 - 4 * m][0:c1 - c0, 0:256], ACT.Sigmoid, e)
            free(pg, e)
            xm_free[slot] = e
            bank_free[5] = bank_free[6] = low
            bank_free[7] = bank_free[3] = sgt
            vs, vt_ = mix(3, 3)
            vv_t = []

            def ev_v(h, tt, b, t):
                x = S.act(VV[:, tt, h * 512:h * 512 + 512], b, ACT.Copy, t)
                vv_t.append(x)
                return x
            mode_a(a['w_rkv'][2], 0, 2, ev_v, [0, 1, 2, 4], vt_, lhs=lambda k, tt: XM[vs][:, k, tt * 128:tt * 128 + 128])

            xm_free[vs] = E.last
            ks, kt_ = mix(4, 2)
            rs, rt_ = mix(5, 0)
            W_K, W_R, W_V = a['w_rkv'][1], a['w_rkv'][0], a['w_rkv'][2]
            w2v, a2v = P2[0:64, 0:1024], P2[0:64, 1024:2048]
            prev = None
            bon_t, yps = [], []

            def bonus(j):
                for m in range(2):
                    for tt in range(2):
                        t = E.mm(PS[7][:, tt * 256 + m * 128:tt * 256 + m * 128 + 128],
                                 rS[:, m * 256 + tt * 128:m * 256 + tt * 128 + 128], cst('bones'), True, True,
                                 yps[j], bank_free[7], sig=(m == 1 and tt == 1))
                bon_t.append(t)
                cs_ = slice(256 * j, 256 * j + 256)
                bank_free[7] = V.tt(BV[:, :, cs_], PS[7][:, :].rearrange("p (t c) -> p t c", t=2), VV[:, :, cs_],
                                    ALU.mult, t, vv_t[-1])
                return bank_free[7]

            for j in range(4):
                kb, rb = 2 * (j % 2), 2 * (j % 2) + 1
                for m in range(2):
                    c0 = (2 * j + m) * 128
                    E.mm(PS[4][:, m * 256:m * 256 + 256], w2v[:, c0:c0 + 128], TW[0:64, :], True, True,
                         p2t, low, bank_free[4])
                    tz = E.mm(PS[5][:, m * 256:m * 256 + 256], a2v[:, c0:c0 + 128], TA[0:64, :], True, True,
                              bank_free[5], sig=True)
                toks = []
                for W, sl, b, rdy in ((W_K, ks, kb, kt_), (W_R, rs, rb, rt_)):
                    pc = load(wcols(W, 256 * j, 256), early=True)
                    wv = v3(pc.ap, 256)
                    for m in range(2):
                        for k in range(KT):
                            t = E.mm(PS[b][:, m * 256:m * 256 + 256], wv[:, k, m * 128:m * 128 + 128], XM[sl][:, k, :],
                                     k == 0, k == 7, pc.tok, rdy, bank_free[b], sig=(m == 1 and k == 7))
                    free(pc, t)
                    toks.append(t)
                tk, tr = toks
                if j == 3:
                    xm_free[ks], xm_free[rs] = tk, tr
                if j:
                    bonus(j - 1)
                for m in range(2):
                    k = 2 * j + m
                    sl = slice(m * 256, m * 256 + 256)
                    S.act(sg[:, sl], PS[4][:, sl], ACT.Tanh, tz, prev, scale=0.5, bias=HV[:, k:k + 1])
                    x = S.act(aa[:, sl], PS[5][:, sl], ACT.Tanh, tz, scale=0.5, bias=HV[:, 8 + k:9 + k])
                bank_free[4] = bank_free[5] = x
                y = V.ts(sg, sg, 0.5, 0.5, ALU.mult, ALU.add, x)
                for q in range(4):
                    y2 = V.op(lambda e, o_=cs[:, q, 1:129], d1=sg[:, q * 128:q * 128 + 128]:
                              e.tensor_tensor_scan(o_, cst('ones'), d1, 0.0, ALU.mult, ALU.add), (y, mset, prev))
                mid = ST[:, 32:36]
                nmid = ST[:, 36:40]
                V.ts(mid, cs[:, :, 64], CDEC, None, ALU.mult, None, y2)
                y3 = V.ts(nmid, cs[:, :, 64], -CDEC, None, ALU.mult, None, y2)
                for q in range(4):
                    S.act(EE[:, q, :], cs[:, q, :], ACT.Exp, y3, prev, scale=-CDEC, bias=mid[:, q:q + 1])
                    x = S.act(EI[:, q * 128:q * 128 + 128], cs[:, q, :][:, 1:129], ACT.Exp, scale=CDEC, bias=nmid[:, q:q + 1])
                em = ST[:, 40:44]
                x = S.act(em, nmid, ACT.Exp, x)
                for m in range(2):
                    dx = V.tt(DX[:, 2 * j + m:2 * j + m + 1], EE[:, 2 * m, 128:129], em[:, 2 * m + 1:2 * m + 2], ALU.mult, x)
                y = V.ts(aa, aa, 0.5, 0.5, ALU.mult, ALU.add, x)
                S.act(kS, PS[kb][:, :], ACT.Copy, tk, prev)
                for m in range(2):
                    k = 2 * j + m
                    sl = slice(m * 256, m * 256 + 256)
                    xk = S.act(kk[:, sl], PS[kb][:, sl], ACT.Copy, scale=vec('k_k', k))
                xq = S.act(sg, kk, ACT.Square, xk, y2)
                bank_free[kb] = xk
                t = E.mm(PS[6][:, :], cst('bones'), sg, True, True, xq, bank_free[6], sig=True)
                x = S.act(sg, PS[6][:, :], ACT.Sqrt, t)
                bank_free[6] = x
                y = V.ts(sg, sg, 1e-12, None, ALU.max, None, x)
                y = V.op(lambda e: e.reciprocal(sg, sg), (y,))
                y = V.tt(kk, kk, sg, ALU.mult, y)
                x = S.act(rS, PS[rb][:, :], ACT.Copy, tr, prev, bon_t[-1] if bon_t else None)
                bank_free[rb] = x
                ya = None
                EA = EE[:, :, 0:128]
                EB = EE[:, :, 1:129]
                ARa = AR[:, 2 * j:2 * j + 2, :, 0, :].rearrange("p m c t -> p (m c) t")
                ARr = AR[:, 2 * j:2 * j + 2, :, 1, :].rearrange("p m c t -> p (m c) t")
                V.tt(ARr, v3(rS, 128), EB, ALU.mult, x)
                V.stt(ARa, v3(kk, 128), -1.0, EA, ALU.mult, ALU.mult, y)
                y = V.tt(kk, kk, aa, ALU.mult, V.last)
                V.tt(BE[:, 2 * j:2 * j + 2, :].rearrange("p m t -> p (m t)"), kk, EI, ALU.mult, y)
                for m in range(2):
                    k = 2 * j + m
                    sl = slice(m * 256, m * 256 + 256)
                    y = V.ts(aa[:, sl], aa[:, sl], -1.0, vec('k_a', k), ALU.add, ALU.mult, y)
                y = V.stt(kS, aa, 1.0, kS, ALU.add, ALU.mult, y)
                V.tt(KA[:, 2 * j:2 * j + 2, :].rearrange("p m t -> p (m t)"), kS, EI, ALU.mult, y)
                for m in range(2):
                    k = 2 * j + m
                    sl = slice(m * 256, m * 256 + 256)
                    yp = V.stt(rS[:, sl], rS[:, sl], vec('r_k', k), kS[:, sl], ALU.mult, ALU.mult, y)
                prev = V.last
                yps.append(yp)
            t = bonus(3)
            fence()
            o = 0
            AT = take(8192).rearrange("p (i s t) -> p i s t", i=16, s=4)
            BT = take(512).rearrange("p (m n) -> p m n", m=4)
            KTt = take(512).rearrange("p (m n) -> p m n", m=4)
            RR = take(512).rearrange("p (g n) -> p g n", g=2)
            SA = take(1024).rearrange("p (g n) -> p g n", g=4)
            SS = take(512).rearrange("p (m e n) -> p m e n", m=4, e=2)
            ss0 = G.op(lambda e: e.memset(SS, 0.0), ())
            assert o <= NLOW - 2048
            Xi = Hb[:, :].rearrange("p (g n) -> p g n", g=4)
            Zi = Sb[:, :].rearrange("p (g n) -> p g n", g=4)
            Wi = Xb[:, :].rearrange("p (g n) -> p g n", g=4)
            i4 = ident.unsqueeze(1).broadcast_to([128, 4, 128])

            def lvl(l):
                off = CST['lvl'][0] + 128 * l
                return CB[:, off:off + 128].unsqueeze(1).broadcast_to([128, 4, 128])
            m0t = cst('m0t').unsqueeze(1).broadcast_to([128, 4, 128])
            VT = vv_t[-1]
            at_t, xz, wt, y_mm, sa_t, rr_t = ([None] * 4 for _ in range(6))
            bt = {}
            turn = [0]

            def prob(half, g, n):
                h = 8 * half + 4 * (g % 2) + n
                return g // 2, h, h // 2, slice(64 * (h % 2), 64 * (h % 2) + 64)

            def form(half, g, banks):
                for n in range(4):
                    c, h, m, pp = prob(half, g, n)
                    i = 4 * g + n
                    b = banks[n % len(banks)]
                    rhs = AR[pp, m, c, :, :].rearrange("p s t -> p (s t)")
                    E.mm(PS[b][:, 0:256], BE[pp, m, c * 128:c * 128 + 128], rhs, True, True, bank_free[b])
                    t = E.mm(PS[b][:, 256:512], KA[pp, m, c * 128:c * 128 + 128], rhs, True, True, sig=True)
                    bank_free[b] = V.tt(AT[:, i, :, :].rearrange("p s t -> p (s t)"), PS[b][:, :], cst('atm'), ALU.mult, t,
                                        y_mm[g])
                at_t[g] = bank_free[b]

            def turned(half, banks):
                for src, dst, b in ((BE, BT, banks[0]), (KA, KTt, banks[1])):
                    for m in range(4):
                        t = E.tr(PS[b][:, m * 128:m * 128 + 128], src[:, 4 * half + m, 0:128], ident, bank_free[b],
                                 sig=(m == 3))
                    bt[half] = S.act(dst.rearrange("p m n -> p (m n)"), PS[b][:, :], ACT.Copy, t, bt.get('used'))
                    bank_free[b] = bt[half]

            def invert_w(l, g):
                b = g
                for n in range(4):
                    rhs = ident if l == 0 else Zi[:, g, n * 128:n * 128 + 128]
                    t = E.mm(PS[b][:, n * 128:n * 128 + 128], AT[:, 4 * g + n, 0, :], rhs, True, True,
                             at_t[g], xz[g] if l else None, bank_free[b], sig=(n == 3))
                wv = v3((Zi if l == 0 else Wi)[:, g, :], 128)
                e = V.tt(wv, v3(PS[b][:, :], 128), lvl(l), ALU.mult, t, sa_t[g])
                bank_free[b] = e
                wt[g] = V.tt(wv, wv, i4, ALU.add, e)
                if l == 0:
                    e = V.tt(v3(Xi[:, g, :], 128), AT[:, 4 * g:4 * g + 4, 0, :], m0t, ALU.mult, at_t[g])
                    xz[g] = V.tt(v3(Xi[:, g, :], 128), v3(Xi[:, g, :], 128), i4, ALU.add, e)

            def invert_xz(l, g):
                bx, bz = 4 + (2 * g) % 4, 5 + (2 * g) % 4
                for n in range(4):
                    ns = slice(n * 128, n * 128 + 128)
                    t = E.mm(PS[bx][:, ns], Wi[:, g, ns], Xi[:, g, ns], True, True, wt[g], bank_free[bx], sig=(n == 3))
                if l < 6:
                    for n in range(4):
                        ns = slice(n * 128, n * 128 + 128)
                        t2 = E.mm(PS[bz][:, ns], Xi[:, g, ns], Wi[:, g, ns], True, True, bank_free[bz], sig=(n == 3))
                    t = t2
                e = S.act(Xi[:, g, :], PS[bx][:, :], ACT.Copy, t)
                bank_free[bx] = e
                if l < 6:
                    e = S.act(Zi[:, g, :], PS[bz][:, :], ACT.Copy, t)
                    bank_free[bz] = e
                xz[g] = e

            def own(ap):
                q = ap.rearrange("p (q e x) -> p q e x", q=2, e=2)
                return [q[:, :, e_, 64 * e_:64 * e_ + 64] for e_ in range(2)]

            def by_head(ap):
                q = ap.rearrange("p (q e x) -> p q e x", q=2, e=2)
                return [q[:, :, e_, :] for e_ in range(2)]


            def rhs_of(half, g, st_t):
                b = g
                for n in range(4):
                    c, h, m, pp = prob(half, g, n)
                    ns = slice(n * 128, n * 128 + 128)
                    t = E.mm(PS[b][:, ns], AT[:, 4 * g + n, 2, :], VV[:, c, m * 128:m * 128 + 128], True, c == 0,
                             bank_free[b], at_t[g], VT, sig=(n == 3))
                    if c == 1:
                        t = E.mm(PS[b][:, ns], AR[:, m, 1, 0, :], SS[:, m - 4 * half, :, :].rearrange("p e n -> p (e n)"),
                                 False, True, st_t, sig=(n == 3))
                for o_, i_ in zip(by_head(RR[:, g % 2, :]), own(PS[b][:, :])):
                    rr_t[g] = S.act(o_, i_, ACT.Copy, t)
                bank_free[b] = rr_t[g]

            def solve(half, g):
                b = 4 + g
                for n in range(4):
                    q = 128 * (n // 2)
                    t = E.mm(PS[b][:, n * 128:n * 128 + 128], Xi[:, g, n * 128:n * 128 + 128],
                             RR[:, g % 2, q:q + 128], True, True, rr_t[g], xz[g], bank_free[b], sig=(n == 3))
                for o_, i_ in zip(by_head(SA[:, g, :]), own(PS[b][:, :])):
                    sa_t[g] = S.act(o_, i_, ACT.Copy, t, y_mm[g])
                bank_free[b] = sa_t[g]

            def state(half):
                for m in range(4):
                    for e_ in range(2):
                        h = 8 * half + 2 * m + e_
                        g, n = (h % 8) // 4, h % 4
                        pp = slice(64 * e_, 64 * e_ + 64)
                        E.mm(PS[6][pp, m * 64:m * 64 + 64], KTt[:, m, pp], VV[:, 0, h * 64:h * 64 + 64], True, False,
                             bank_free[6], bt[half])
                        t = E.mm(PS[6][pp, m * 64:m * 64 + 64], BT[:, m, pp], SA[:, g, n * 64:n * 64 + 64],
                                 False, True, sa_t[g], sig=True)
                bt['used'] = t
                for m in range(4):
                    for e_ in range(2):
                        pp = slice(64 * e_, 64 * e_ + 64)
                        s_ = V.ts(SS[pp, m, e_, :], PS[6][pp, m * 64:m * 64 + 64],
                                  DX[pp, 4 * half + m:4 * half + m + 1], None, ALU.mult, None, t, ss0, y_mm[3])
                bank_free[6] = s_
                return s_

            def outputs(half, c):
                for gg in range(2):
                    g = 2 * c + gg
                    b = 2 + gg
                    for n in range(4):
                        _, h, m, pp = prob(half, g, n)
                        i = 4 * g + n
                        ns = slice(n * 128, n * 128 + 128)
                        q = 128 * (n // 2)
                        E.mm(PS[b][:, ns], AT[:, i, 3, :], VV[:, c, m * 128:m * 128 + 128], True, False, bank_free[b])
                        t = E.mm(PS[b][:, ns], AT[:, i, 1, :], SA[:, g, q:q + 128], False, c == 0, sa_t[g], sig=(n == 3))
                        if c == 1:
                            t = E.mm(PS[b][:, ns], AR[:, m, 1, 1, :], SS[:, m - 4 * half, :, :].rearrange("p e n -> p (e n)"),
                                     False, True, sig=(n == 3))
                    y_mm[g] = t
                    c0 = half * 512 + gg * 256
                    for o_, i_ in zip(by_head(YY[:, c, c0:c0 + 256]), own(PS[b][:, :])):
                        x = S.act(o_, i_, ACT.Copy, t)
                    bank_free[b] = x
                return x

            for half in range(2):
                if half == 0:
                    for g in range(4):
                        form(0, g, [0, 1, 2, 3, 4, 5, 6, 7] if g % 2 == 0 else [4, 5, 6, 7])
                    turned(0, [0, 1])
                for l in range(7):
                    for g in range(4):
                        invert_w(l, g)
                    if l:
                        for g in range(4):
                            invert_xz(l, g)
                rhs_of(half, 0, None)
                rhs_of(half, 1, None)
                solve(half, 0)
                solve(half, 1)
                ss_t = state(half)
                outputs(half, 0)
                if half == 0:
                    form(1, 0, [0, 1, 5])
                rhs_of(half, 2, ss_t)
                rhs_of(half, 3, ss_t)
                if half == 0:
                    form(1, 1, [0, 1, 4, 5])
                solve(half, 2)
                solve(half, 3)
                if half == 0:
                    turned(1, [0, 1])
                yy_t = outputs(half, 1)
                if half == 0:
                    form(1, 2, [0, 1, 4, 5])
                    form(1, 3, [6, 7, 2, 3])

            fence()
            Y3 = YY.rearrange("p t (h n) -> p (t h) n", n=64)
            YA = YY.rearrange("p t c -> p (t c)")
            pg2 = load((lambda r: r[:, 0:1024], a['g2'][0:128, :]), (lambda r: r[0:32, 1024:2048], a['g2'][128:160, :]), early=True)
            tb = load((lambda r: r[:, 0:1024], a['gn_g'].broadcast_to([128, 1024])),
                      (lambda r: r[:, 1024:2048], a['gn_b'].broadcast_to([128, 1024])), early=True)
            mu_ = ST[:, 128:160]
            va_ = ST[:, 160:192]
            gt = []
            for tt in range(2):
                for h in range(2):
                    b = 2 * tt + h
                    E.mm(PS[b][:, :], SG[:, 0, tt * 128:tt * 128 + 128], pg2.ap[:, h * 512:h * 512 + 512], True, False,
                         pg2.tok, sgt, bank_free[b])
                    gt.append(E.mm(PS[b][:, :], SG[0:32, 1, tt * 128:tt * 128 + 128],
                                   pg2.ap[0:32, 1024 + h * 512:1536 + h * 512], False, True, sig=True))
            free(pg2, E.last)
            thx = s_io.dma(D, H, a['x'].rearrange("(t p) c -> p t c", p=128), [E.last, S.last, V.last])
            y = V.op(lambda e: e.tensor_reduce(mu_, Y3, AX, ALU.add), (yy_t,))
            y = V.ts(mu_, mu_, 1.0 / 64, None, ALU.mult, None, y)
            y = V.tt(Y3, Y3, mu_.unsqueeze(2).broadcast_to([128, 32, 64]), ALU.subtract, y)
            SQ = Sb[:, :]
            x = S.act(SQ, YA, ACT.Square, y)
            y = V.op(lambda e: e.tensor_reduce(va_, SQ.rearrange("p (h n) -> p h n", n=64), AX, ALU.add), (x,))
            y = rstd_of(va_, va_, GN_EPS, 1.0 / 64, y)
            y = V.tt(Y3, Y3, va_.unsqueeze(2).broadcast_to([128, 32, 64]), ALU.mult, y)
            y = V.tt(YY, YY, tb.ap[:, 0:1024].unsqueeze(1).broadcast_to([128, 2, 1024]), ALU.mult, y, tb.tok)
            y = V.tt(YY, YY, tb.ap[:, 1024:2048].unsqueeze(1).broadcast_to([128, 2, 1024]), ALU.add, y)
            free(tb, y)
            y = V.tt(YY, YY, BV, ALU.add, y)
            for tt in range(2):
                for h in range(2):
                    b = 2 * tt + h
                    sl = slice(h * 512, h * 512 + 512)
                    yg = V.tt(YY[:, tt, sl], YY[:, tt, sl], PS[b][:, :], ALU.mult, gt, y)
                    bank_free[b] = yg
            yt = to_chan(YY, XT, yg, [0, 1, 2, 3])
            toks = []

            def ev_keep(h, tt, b, t):
                toks.append(t)
                return None
            mode_a(a['w_o'], 0, 2, ev_keep, [4, 6, 5, 7], yt)
            toks = [toks[0], toks[2], toks[1], toks[3]]
            x1 = residual_ln([4, 5, 6, 7], toks, a['lnmg'][0:1, :], a['lnmb'][0:1, :], 'mixg0', 'mixb0', True, thx)
            if debug == 'rwkv':
                return finish(H, G.last)
            t = ffn(a['ffn_w_in'][0], a['ffn_w_down'][0], 11, True, x1)
            x1 = residual_ln([4, 5, 6, 7], t, a['lnfg'][0:1, :], a['lnfb'][0:1, :], 'ffng0', 'ffnb0')
            if debug == 'layer0':
                return finish(H, G.last)

            area = PH
            o = 0
            QQ = take(2048).rearrange("p (k t) -> p k t", k=8)
            KK = take(2048).rearrange("p (k t) -> p k t", k=8)
            VV = take(2048).rearrange("p (t c) -> p t c", t=2)
            OT = take(2048).rearrange("p (k t) -> p k t", k=8)
            raw = [take(512) for _ in range(2)]
            rc = [take(512) for _ in range(2)]
            TMP = take(3072)
            W = a['moba_w_qkv']
            cosb = cst('cos').unsqueeze(1).broadcast_to([128, 2, 256])
            sinb = cst('sin').unsqueeze(1).broadcast_to([128, 2, 256])
            rope_t = []
            raw_free = [None, None]

            def rope(dst):
                def ev(j, b, t):
                    x = S.act(raw[j % 2].rearrange("p (m t) -> p m t", m=2), b, ACT.Copy, t, raw_free[j % 2])
                    pb = 2 + j % 2
                    t2 = E.mm(PS[pb][:, :], cst('perm'), raw[j % 2], True, True, x, bank_free[pb], sig=True)
                    g = G.tt(rc[j % 2].rearrange("p (m t) -> p m t", m=2), raw[j % 2].rearrange("p (m t) -> p m t", m=2),
                             cosb, ALU.mult, x, raw_free[j % 2])
                    d = dst[:, 2 * j:2 * j + 2, :]
                    y = V.tt(d, PS[pb][:, :].rearrange("p (m t) -> p m t", m=2), sinb, ALU.mult, t2)
                    bank_free[pb] = y
                    y = V.tt(d, d, rc[j % 2].rearrange("p (m t) -> p m t", m=2), ALU.add, y, g)
                    raw_free[j % 2] = [y, t2]
                    rope_t.append(y)
                    return x
                return ev
            mode_b(W, 0, 4, rope(QQ), [0, 1], x1)
            mode_b(W, 1024, 4, rope(KK), [0, 1], None)
            vt = []

            def ev_v2(h, tt, b, t):
                vt.append(S.act(VV[:, tt, h * 512:h * 512 + 512], b, ACT.Copy, t))
                return vt[-1]
            mode_a(W, 2048, 2, ev_v2, [4, 5, 6, 7], None)

            def hp(h):
                return slice(64 * (h % 2), 64 * (h % 2) + 64)
            outs = attention(16, lambda h: QQ[hp(h), h // 2, :], lambda h: KK[hp(h), h // 2, :],
                             lambda h, s: VV[:, s, h * 64:h * 64 + 64],
                             lambda h: (hp(h), OT[:, h // 2, :], h % 2 == 1), 2, 0.125, True, TMP,
                             [rope_t[-1], vt[-1]], mask=cst('cmask'))
            toks = []
            sa = split_act(OT.rearrange("p k t -> p (k t)"), outs)
            mode_a(a['moba_w_o'], 0, 2, lambda h, tt, b, t: toks.append(t), [4, 6, 5, 7], sa)
            toks = [toks[0], toks[2], toks[1], toks[3]]
            x1 = residual_ln([4, 5, 6, 7], toks, a['lnmg'][1:2, :], a['lnmb'][1:2, :], 'mixg1', 'mixb1', True)
            if debug == 'moba':
                return finish(H, G.last)
            t = ffn(a['ffn_w_in'][1], a['ffn_w_down'][1], 11, True, x1)
            residual_ln([4, 5, 6, 7], t, a['lnfg'][1:2, :], a['lnfb'][1:2, :], 'ffng1', 'ffnb1')
            if debug == 'layer1':
                return finish(H, G.last)

            fence()
            nrm = rms_norm(H, None)
            xt = to_chan(S1, XT, nrm, [0, 1, 2, 3], 'nmix')
            o = 0
            UB = take(8 * 286).rearrange("p (k t) -> p k t", k=8)
            CV = take(2048).rearrange("p (k t) -> p k t", k=8)
            QQ = take(2048).rearrange("p (k t) -> p k t", k=8)
            KK = take(2048).rearrange("p (k t) -> p k t", k=8)
            VV = take(2048).rearrange("p (t c) -> p t c", t=2)
            GC = take(2048).rearrange("p (k t) -> p k t", k=8)
            GA = take(2048).rearrange("p (k t) -> p k t", k=8)
            OT = UB.rearrange("p k t -> p (k t)")[:, 0:2048].rearrange("p (k t) -> p k t", k=8)
            TMP = take(3072)
            WI = take(16)
            SC = take(384)
            sgb = [TMP[:, i * 512:(i + 1) * 512] for i in range(2)]
            QI = TMP[:, 1024:2048].rearrange("p (k t) -> p k t", k=4)
            KI = TMP[:, 2048:2304]
            RL = [TMP[:, 2304:2688], TMP[:, 2688:3072]]
            W = a['w_in2']
            z = G.op(lambda e: e.memset(UB[:, :, 0:30], 0.0), ())
            conv_t = []
            st.rate = 6
            conv_done = []

            def conv(k):
                tok = [conv_t[k // 2], z]

                def tap(i):
                    def f():
                        if i == 30:
                            tok[:] = [V.ts(CV[:, k, :], UB[:, k, 30:286], vec('cw30', k), vec('conv_b', k), ALU.mult, ALU.add, *tok)]
                        else:
                            tok[:] = [V.stt(CV[:, k, :], UB[:, k, i:i + 256], vec(f'cw{i}', k), CV[:, k, :],
                                            ALU.mult, ALU.add, *tok)]
                        conv_done[:] = tok
                    return f
                return [tap(i) for i in [30] + list(range(30))]

            def conv_pool(k, buf):
                y = G.ts(CV[:, k, :], UB[:, k, 30:286], vec('cw30', k), vec('conv_b', k), ALU.mult, ALU.add, conv_t[k // 2], z)
                for i in range(30):
                    x = G.ts(buf, UB[:, k, i:i + 256], vec(f'cw{i}', k), 0.0, ALU.mult, ALU.add, y)
                    y = G.tt(CV[:, k, :], CV[:, k, :], buf, ALU.add, x)
                return y

            sg_free = [None, None]
            for j in range(4):
                bs = []
                for u in range(2):
                    pc = load(wcols(W, 1024 * u + 256 * j, 256), split=True)
                    b = 2 * (j % 2) + u
                    for m in range(2):
                        for k in range(KT):
                            t = mm3(PS[b][:, m * 256:m * 256 + 256], wsl(pc, 256, k, m * 128, m * 128 + 128), act_k(k),
                                    k == 0, k == 7, pc.tok, bank_free[b], rk(xt, k), sig=(m == 1 and k == 7))
                    free(pc, t)
                    bs.append((b, t))
                (ba, ta), (bg, tg) = bs
                x = S.act(sgb[j % 2], PS[bg][:, :], ACT.Sigmoid, tg, sg_free[j % 2])
                bank_free[bg] = x
                y = V.tt(UB[:, 2 * j:2 * j + 2, 30:286], PS[ba][:, :].rearrange("p (m t) -> p m t", m=2),
                         sgb[j % 2].rearrange("p (m t) -> p m t", m=2), ALU.mult, x, ta)
                bank_free[ba] = y
                sg_free[j % 2] = y
                conv_t.append(y)
                if j < 3:
                    st.beside += [f for k in (2 * j, 2 * j + 1) for f in conv(k)]

            q_t = []

            def ev_to(dst):
                def ev(j, b, t):
                    q_t.append(S.act(dst[:, 2 * j:2 * j + 2, :], b, ACT.Copy, t))
                    return q_t[-1]
                return ev
            cp = [conv_pool(6, Sb[:, 0:256]), conv_pool(7, Sb[:, 0:256])]
            mode_b(W, 5120, 2, ev_to(QI), [0, 1], xt)
            src = W[:, 5632:5704].rearrange("(k p) n -> p k n", p=128)
            pc = load((lambda r: v3(r[:, 0:1088], 136)[:, :, 0:64], src[:, :, 0:64]),
                      (lambda r: v3(r[:, 0:1088], 136)[:, :, 64:136], src[:, :, 0:72]))
            kw = v3(pc.ap[:, 0:1088], 136)
            for k in range(KT):
                t = E.mm(PS[2][:, 0:256], kw[:, k, 0:128], XT[:, k, :], k == 0, k == 7, pc.tok,
                         bank_free[2], sig=(k == 7))
            for tt in range(2):
                for k in range(KT):
                    t = E.mm(PS[2][:, 256 + 128 * tt:384 + 128 * tt], XT[:, k, tt * 128:tt * 128 + 128], kw[:, k, 8:136],
                             k == 0, k == 7, sig=(k == 7))
            free(pc, t)
            S.act(KI, PS[2][:, 0:256], ACT.Copy, t)
            x = S.act(WI.rearrange("p (t n) -> p t n", t=2), v3(PS[2][:, 256:512], 128)[:, :, 120:128], ACT.Copy, scale=8 ** -0.5)
            bank_free[2] = x
            ki_t = x
            sp = [(0, 128), (128, 384)]
            y = None
            rl_free = [None, None]
            for h in range(8):
                b = 4 + h % 2
                for tt in range(2):
                    lo, hi = sp[tt]
                    t = E.mm(PS[b][:, lo:hi], QI[hp(h), h // 2, tt * 128:tt * 128 + 128], KI[hp(h), 0:hi - lo], True, True,
                             ki_t, q_t[-1], bank_free[b], sig=(tt == 1))
                x = S.act(RL[h % 2], PS[b][:, 0:384], ACT.Relu, t, rl_free[h % 2], scale=0.125)
                bank_free[b] = x
                for tt in range(2):
                    lo, hi = sp[tt]
                    wi = WI[:, 8 * tt + h:8 * tt + h + 1]
                    if h == 0:
                        e = V.ts(SC[:, lo:hi], RL[0][:, lo:hi], wi, None, ALU.mult, None, x)
                    else:
                        e = V.stt(SC[:, lo:hi], RL[h % 2][:, lo:hi], wi, SC[:, lo:hi], ALU.mult, ALU.add, x, y)
                y = e
                rl_free[h % 2] = e
            y = V.tt(SC, SC, cst('cmask'), ALU.add, y)
            sel = [y]

            def later(f):
                def g_():
                    sel[0] = f(sel[0])
                return g_
            ops = []
            for tt in range(2):
                lo, hi = sp[tt]
                m8 = ST[:, 200 + 8 * tt:208 + 8 * tt]
                for r in range(8):
                    ops.append(later(lambda y, o_=m8, i_=SC[:, lo:hi]: V.op(lambda e: e.max(o_, i_), (y,))))
                    ops.append(later(lambda y, o_=SC[:, lo:hi], m_=m8: V.op(lambda e: e.match_replace(o_, m_, o_, TAKEN), (y,))))
            ops.append(later(lambda y: V.ts(SC, SC, TAKEN, None, ALU.is_equal, None, y)))
            ops.append(later(lambda y: V.tt(SC, SC, cst('c01'), ALU.mult, y)))
            ops.append(later(lambda y: V.ts(SC, SC, -1.0, -NEG, ALU.add, ALU.mult, y)))
            st.beside[:] = st.beside[:31] + ops + st.beside[31:]

            mode_b(W, 2048, 4, ev_to(QQ), [0, 1], xt)
            mode_b(W, 3072, 4, ev_to(KK), [2, 3], xt)

            def ev_v3(h, tt, b, t):
                q_t.append(S.act(VV[:, tt, h * 512:h * 512 + 512], b, ACT.Copy, t))
                return q_t[-1]
            mode_a(W, 4096, 2, ev_v3, [4, 5, 6, 7], xt)

            def ev_gate(dst, bname):
                def ev(j, b, t):
                    for m in range(2):
                        k = 2 * j + m
                        q_t.append(S.act(dst[:, k, :], b[:, m, :], ACT.Sigmoid, t, bias=vec(bname, k)))
                    return q_t[-1]
                return ev
            mode_b(W, 5704, 4, ev_gate(GC, 'bgc'), [0, 1], xt)
            mode_b(W, 6728, 4, ev_gate(GA, 'bga'), [2, 3], xt)
            while sum(1 for _ in st.beside) > 0:
                background()
            cv = conv_done + cp
            sel_t = sel[0]
            outs = attention(8, lambda h: QQ[:, h, :], lambda h: KK[:, h, :], lambda h, s: VV[:, s, h * 128:h * 128 + 128],
                             lambda h: (slice(0, 128), OT[:, h, :], True), 1, 128 ** -0.5, True, TMP,
                             [q_t[-1], cv], mask=SC, mask_tok=sel_t)
            sa_ = split_act(OT.rearrange("p k t -> p (k t)"), outs)
            CVf = CV.rearrange("p k t -> p (k t)")
            for k in range(KT):
                t = E.mm(PS[6][:, 0:256], cst('ones'), CV[:, k, :], k == 0, k == 7, cv, bank_free[6], sig=(k == 7))
            mean = QQ[:, 0, :]
            x = V.ts(mean, PS[6][:, 0:256], 1.0 / C, None, ALU.mult, None, t, outs)
            y = V.tt(CV, CV, mean.unsqueeze(1).broadcast_to([128, 8, 256]), ALU.subtract, x)
            SQC = Sb[:, :]
            x = S.act(SQC, CVf, ACT.Square, y)
            for k in range(KT):
                t = E.mm(PS[6][:, 256:512], cst('ones'), SQC[:, k * 256:k * 256 + 256], k == 0, k == 7, x, sig=(k == 7))
            rst = QQ[:, 1, :]
            y = V.ts(rst, PS[6][:, 256:512], 1.0 / C, EPS, ALU.mult, ALU.add, t)
            bank_free[6] = y
            y = S.act(rst, rst, ACT.Sqrt, y)
            y = V.op(lambda e: e.reciprocal(rst, rst), (y,))
            y = V.tt(CV, CV, rst.unsqueeze(1).broadcast_to([128, 8, 256]), ALU.mult, y)
            for k in range(KT):
                cv = S.act(CV[:, k, :], CV[:, k, :], ACT.Silu, y, scale=vec('cln_g', k), bias=vec('cln_b', k))
            gm = []

            def ev_mul(dst):
                def ev(j, b, t):
                    d = dst[:, 2 * j:2 * j + 2, :]
                    gm.append(V.tt(d, d, b, ALU.mult, t))
                    return gm[-1]
                return ev
            mode_b(a['w_attn_out'], 0, 4, ev_mul(GA), [0, 1], sa_)
            sa_ = split_act(CVf, cv)
            mode_b(a['w_conv_out'], 0, 4, ev_mul(GC), [2, 3], sa_)
            gm.append(V.tt(GA, GA, GC, ALU.add, gm[-1]))
            sa_ = split_act(GA.rearrange("p k t -> p (k t)"), gm[-1])

            def add_h(h, tt, b, t):
                hs = H[:, tt, h * 512:h * 512 + 512]
                hx.append(V.tt(hs, hs, b, ALU.add, t))
                return hx[-1]
            hx = []
            mode_a(a['w_mix_out'], 0, 2, add_h, [4, 6, 5, 7], sa_)
            if debug == 'mix2':
                return finish(H, hx)

            nrm = rms_norm(H, hx)
            xt = to_chan(S1, XT, nrm, [0, 1, 2, 3], 'nx')
            QX = QQ
            mode_b(a['wx_q'], 0, 2, ev_to(QX), [4, 5], xt)
            outs = attention(4, lambda h: QX[:, h, :], lambda h: KX[:, h, :], lambda h, s: VX[:, s, h * 128:h * 128 + 128],
                             lambda h: (slice(0, 128), OT[:, h, :], True), 1, 128 ** -0.5, False, TMP, [q_t[-1]])
            hx = []
            sa_ = split_act(OT.rearrange("p k t -> p (k t)"), outs)
            mode_a(a['wx_o'], 0, 2, add_h, [4, 6, 5, 7], sa_, nk=4)
            nrm = rms_norm(H, hx)
            x1 = to_chan(S1, XT, nrm, [0, 1, 2, 3], 'nffn')
            if debug == 'cross':
                return finish(H, hx)
            t = ffn(a['w_ff1'], a['w_ff2'], 16, False, x1)
            hx = []
            for tt in range(2):
                for h in range(2):
                    add_h(h, tt, PS[4 + 2 * tt + h][:, :], t[2 * tt + h])
            pc = load((lambda r: r[:, 0:1024], a['nfin'].broadcast_to([128, 1024])))
            nrm = rms_norm(H, hx)
            fin = V.tt(S1, S1, pc.ap[:, 0:1024].unsqueeze(1).broadcast_to([128, 2, 1024]), ALU.mult, nrm, pc.tok)
            finish(S1, fin)

        def prologue():
            i = VECS.index('w0h') * 8
            return V.ts(HV[:, :], VB[:, i:i + 16], 0.5, None, ALU.mult, None, (s_c.sem, 32))

        for dry in (True, False):
            S.wait(prologue())
            run()
            if dry:
                st.plan = st.spec
                st.at = 0
                for q in (V, S, G, E, D):
                    q.reset()
                for c in (s_c, s_x, s_io, s_out):
                    c.v = 0
                bank_free[:] = [None] * 8

        block = ctx.enter_context(nc.Block())

        @block.vector
        def _(e):
            for f in V.items:
                f(e)

        @block.scalar
        def _(e):
            for f in S.items:
                f(e)

        @block.gpsimd
        def _(e):
            for f in G.items:
                f(e)

        @block.tensor
        def _(e):
            for f in E.items:
                f(e)

        @block.sync
        def _(e):
            for f in D.items:
                f(e)


def vectors(i):
    g = {'w0h': i['rwkv_w0'][0], 'a0h': i['rwkv_a0'][0], 'k_k': i['rwkv_k_k'][0], 'k_a': i['rwkv_k_a'][0],
         'r_k': i['rwkv_r_k'][0].reshape(-1), 'conv_b': i['conv_b_2'][0], 'cln_g': i['conv_ln_g_2'][0],
         'cln_b': i['conv_ln_b_2'][0], 'nmix': i['norm_mix_g_2'][0], 'nx': i['norm_x_g_2'][0],
         'nmem': i['norm_mem_g_2'][0], 'nffn': i['norm_ffn_g_2'][0], 'bgc': i['b_gate_2'][0, 0:C],
         'bga': i['b_gate_2'][0, C:2 * C]}
    for n in range(6):
        g[f'mu{n}'] = i['rwkv_mu'][0, n]
    for n in range(31):
        g[f'cw{n}'] = i['conv_w_2'][0, n]
    for l in range(2):
        g[f'mixg{l}'], g[f'mixb{l}'] = i['ln_mix_g'][l], i['ln_mix_b'][l]
        g[f'ffng{l}'], g[f'ffnb{l}'] = i['ln_ffn_g'][l], i['ln_ffn_b'][l]
    return np.ascontiguousarray(np.concatenate([g[n].reshape(8, 128).T for n in VECS], 1))


DEBUG = None


def kernel(**inputs):
    import numpy as _np
    import concourse.bacc as _bacc
    from concourse import mybir as _mybir
    from concourse.bass_utils import run_bass_kernel_spmd as _run

    i = {k: _np.asarray(v) for k, v in inputs.items()}
    arrays = {
        'cst': constants(), 'vec': vectors(i), 'xT': i['x'][0].T, 'x': i['x'][0], 'mem': i['mem_2'][0],
        'w_rkv': i['rwkv_w_rkv'][0], 'w1': i['rwkv_w1'][0], 'a1': i['rwkv_a1'][0], 'g1': i['rwkv_g1'][0],
        'w2': i['rwkv_w2'][0], 'a2': i['rwkv_a2'][0], 'g2': i['rwkv_g2'][0], 'gn_g': i['rwkv_gn_g'],
        'gn_b': i['rwkv_gn_b'], 'w_o': i['rwkv_w_o'][0], 'moba_w_qkv': i['moba_w_qkv'][0],
        'moba_w_o': i['moba_w_o'][0], 'ffn_w_in': i['ffn_w_in'], 'ffn_w_down': i['ffn_w_down'],
        'lnmg': i['ln_mix_g'], 'lnmb': i['ln_mix_b'], 'lnfg': i['ln_ffn_g'], 'lnfb': i['ln_ffn_b'],
        'w_in2': i['w_in_2'][0], 'w_conv_out': i['w_conv_out_2'][0], 'w_attn_out': i['w_attn_out_2'][0],
        'w_mix_out': i['w_mix_out_2'][0], 'wx_q': i['wx_q_2'][0], 'wx_kv': i['wx_kv_2'][0], 'wx_o': i['wx_o_2'][0],
        'w_ff1': i['w_ff1_2'][0], 'w_ff2': i['w_ff2_2'][0], 'nfin': i['norm_final_g_2'].reshape(1, C),
    }
    nc = _bacc.Bacc("TRN2", target_bir_lowering=False, num_devices=1)
    feed, aps = {}, {}
    for name, v in arrays.items():
        v = _np.ascontiguousarray(v)
        feed[f"in_{name}"] = v
        aps[name] = nc.dram_tensor(f"in_{name}", v.shape, _mybir.dt.from_np(v.dtype), kind="ExternalInput").ap()
    out = nc.dram_tensor("out_y", (1, T, C), F32, kind="ExternalOutput").ap()
    build(nc, aps, out, DEBUG)
    r = _run(nc, [feed], core_ids=[0])
    return r.results[0]["out_y"]
```

```python
from contextlib import ExitStack

import numpy as np
import concourse.bass as bass
from concourse import mybir

F32 = mybir.dt.float32
F32R = mybir.dt.float32r
ALU = mybir.AluOpType
ACT = mybir.ActivationFunctionType
AX = mybir.AxisListType.X

C = 1024
T = 256
KT = 8
FF = 2816
FF2 = 4096
ALPHA = 4 ** 0.25
CDEC = float(np.exp(-0.5))
GN_EPS = 64e-5
LN_EPS = 1e-5
EPS = 1e-6
NEG = -1e30
TAKEN = -3e38

VECS = ['mu0', 'mu1', 'mu2', 'mu3', 'mu4', 'mu5', 'w0h', 'a0h', 'k_k', 'k_a', 'r_k',
        'mixg0', 'mixb0', 'ffng0', 'ffnb0', 'mixg1', 'mixb1', 'ffng1', 'ffnb1',
        'conv_b', 'cln_g', 'cln_b', 'nmix', 'nx', 'nmem', 'nffn', 'bgc', 'bga'] + [f'cw{i}' for i in range(31)]
CST = {}
_at = 0
for _n, _w in [('ident', 128), ('atm', 512), ('lvl', 896), ('m0t', 128), ('bones', 128), ('ones', 128),
               ('sel2', 2), ('pad', 14), ('perm', 128), ('cmask', 384), ('c01', 384), ('cos', 256), ('sin', 256)]:
    CST[_n] = (_at, _w)
    _at += _w
NCST = _at


def constants():
    a = np.zeros((128, NCST), np.float32)
    p = np.arange(128)[:, None]
    f = np.arange(128)[None, :]

    def put(name, v):
        o, w = CST[name]
        a[:, o:o + w] = v

    put('ident', p == f)
    put('atm', np.concatenate([p < f, p <= f, p < f, p <= f], 1))
    put('lvl', np.concatenate([((p >> (l + 1)) == (f >> (l + 1))) & ((p >> l) & 1 == 1) & ((f >> l) & 1 == 0)
                               for l in range(7)], 1))
    put('m0t', ((f >> 1) == (p >> 1)) & (f & 1 == 1) & (p & 1 == 0))
    put('bones', (p // 64) == (f // 64))
    put('ones', 1.0)
    put('sel2', (p // 64) == np.arange(2)[None, :])
    n_out, n_in = f % 64, p % 64
    same = (p // 64) == (f // 64)
    put('perm', np.where(same & (n_out < 32) & (n_in == n_out + 32), -1.0, 0.0)
        + np.where(same & (n_out >= 32) & (n_in == n_out - 32), 1.0, 0.0))
    t1 = np.arange(256)[None, :] - 128
    ok = np.concatenate([f <= p, t1 <= p], 1)
    put('cmask', np.where(ok, 0.0, NEG))
    put('c01', ok)
    inv = (np.float32(10000.0) ** (-np.arange(0, 64, 2, dtype=np.float32) / np.float32(64))).astype(np.float32)
    ang = np.arange(T, dtype=np.float32)[None, :] * inv[:, None]
    put('cos', np.tile(np.cos(ang), (4, 1)))
    put('sin', np.tile(np.sin(ang), (4, 1)))
    return a


class Queue:

    def __init__(self, sem):
        self.sem = sem
        self.reset()

    def reset(self):
        self.n, self.items, self.seen = 0, [], {}

    def wait(self, *toks):
        for t in toks:
            if t is None:
                continue
            if isinstance(t, list):
                self.wait(*t)
                continue
            s, v = t
            if self.seen.get(id(s), 0) < v:
                self.seen[id(s)] = v
                self.items.append(lambda e, s=s, v=v: e.wait_ge(s, v))

    def op(self, f, toks, sig=True):
        self.wait(*toks)
        if not sig:
            self.items.append(f)
            return None
        self.n += 1
        s = self.sem
        self.items.append(lambda e: f(e).then_inc(s, 1))
        return (s, self.n)

    @property
    def last(self):
        return (self.sem, self.n) if self.n else None

    def tt(self, out, a, b, op, *after):
        return self.op(lambda e: e.tensor_tensor(out, a, b, op), after)

    def ts(self, out, a, s1, s2, op0, op1, *after):
        if op1 is None:
            return self.op(lambda e: e.tensor_scalar(out, a, s1, None, op0), after)
        return self.op(lambda e: e.tensor_scalar(out, a, s1, s2, op0, op1), after)

    def stt(self, out, a, s, b, op0, op1, *after):
        return self.op(lambda e: e.scalar_tensor_tensor(out=out, in0=a, scalar=s, in1=b, op0=op0, op1=op1), after)

    def act(self, out, a, func, *after, scale=1.0, bias=0.0, accum=None):
        if accum is None:
            return self.op(lambda e: e.activation(out, a, func, bias=bias, scale=scale), after)
        return self.op(lambda e: e.activation(out, a, func, bias=bias, scale=scale, accum_out=accum), after)

    def mm(self, out, l, r, start, stop, *after, sig=False):
        return self.op(lambda e: e.matmul(out, l, r, start=start, stop=stop), after, sig)

    def tr(self, out, a, ident, *after, sig=False):
        return self.op(lambda e: e.transpose(out, a, ident), after, sig)


class PerK(list):
    pass


class PerT(list):
    pass


class Counter:

    def __init__(self, sem):
        self.sem, self.v = sem, 0

    def dma(self, q, out, src, *after):
        q.wait(*after)
        self.v += 16
        s = self.sem
        q.items.append(lambda e: e.dma_start(out, src).then_inc(s, 16))
        return (s, self.v)


NRING = 3
NW = 3
NLOW = 4096 + 2 * NW * 2048
NPA = NLOW + 18080
HVI = VECS.index('w0h') * 8
HVG = VECS.index('bgc') * 8


def build(nc, a, out):
    ctx = ExitStack()
    with ctx:
        CB = ctx.enter_context(nc.sbuf_tensor("CB", [128, NCST], F32))
        VB = ctx.enter_context(nc.sbuf_tensor("VB", [128, len(VECS) * 8], F32))
        RG = ctx.enter_context(nc.sbuf_tensor("RG", [128, NRING, 2048], F32))
        Hb = ctx.enter_context(nc.sbuf_tensor("Hb", [128, 2048], F32))
        Sb = ctx.enter_context(nc.sbuf_tensor("Sb", [128, 2048], F32))
        Xb = ctx.enter_context(nc.sbuf_tensor("Xb", [128, 2048], F32))
        KX = ctx.enter_context(nc.sbuf_tensor("KX", [128, 4, 256], F32))
        VX = ctx.enter_context(nc.sbuf_tensor("VX", [128, 2, 512], F32))
        ST = ctx.enter_context(nc.sbuf_tensor("ST", [128, 512], F32))
        HV = ctx.enter_context(nc.sbuf_tensor("HV", [128, 32], F32))
        with nc.sbuf_tensor("PA", [128, NPA], F32) as PA:
            pass
        AH = ctx.enter_context(nc.sbuf_tensor("AH", [128, 2048], F32R))
        AL = ctx.enter_context(nc.sbuf_tensor("AL", [128, 2048], F32R))
        WH = ctx.enter_context(nc.sbuf_tensor("WH", [128, NW, 2048], F32R))
        WL = ctx.enter_context(nc.sbuf_tensor("WL", [128, NW, 2048], F32R))
        with nc.sbuf_tensor("PF", [128, 2048], F32) as PF, nc.sbuf_tensor("HH", [128, 2, 512], F32R) as HH, \
                nc.sbuf_tensor("HL", [128, 2, 512], F32R) as HL:
            pass
        PH = ctx.enter_context(nc.sbuf_tensor("PH", [128, NPA - NLOW], F32))
        PS = [ctx.enter_context(nc.psum_tensor(f"PS{i}", [128, 512], F32)) for i in range(8)]

        def sem(n):
            return ctx.enter_context(nc.semaphore(n))

        names = ("s_dve", "s_act", "s_pool", "s_pe", "s_sp")
        V, S, G, E, D = (Queue(sem(n)) for n in names)
        s_c = Counter(sem("s_const"))
        s_v = Counter(sem("s_vec"))
        s_m = Counter(sem("s_mem"))
        s_io = Counter(sem("s_io"))
        s_x = Counter(sem("s_x"))
        s_out = Counter(sem("s_out"))

        class Stream:
            plan, at, dma_n, prep_n, wn, rate = None, 0, 0, 0, 0, 0

        st = Stream()
        st.beside, st.hooks, st.limit = [], [], 10 ** 6
        st.spec, st.pieces, st.owner, st.wowner = [], [], [None] * 5, [None] * NW
        st.sems = [Counter(sem(f"s_ring{i}")) for i in range(5)]

        def cst(n):
            o, w = CST[n]
            return CB[:, o:o + w]

        def vec(n, k):
            i = VECS.index(n) * 8 + k
            return VB[:, i:i + 1]

        ident = cst('ident')
        bank_free = [None] * 8

        class Piece:
            pass

        def load(*parts, split=False, early=False, tail=False):
            i = st.at
            st.at += 1
            if st.plan is None:
                st.spec.append((parts, split, early))
                p = Piece()
                p.i, p.tok, p.ap, p.h, p.l = i, None, RG[:, 0, :], WH[:, 0, :], WL[:, 0, :]
                hook()
                background()
                return p
            pump(i, 1 if tail else 2)
            hook()
            background()
            return st.pieces[i]

        def free(p, *toks):
            if st.plan is None:
                return
            p.used = list(toks)

        def background(n=None):
            for _ in range(min(st.rate if n is None else n, len(st.beside))):
                st.beside.pop(0)()

        def hook():
            for f in (st.hooks.pop(0) if st.hooks else ()):
                f()

        def slot_of(i, early):
            if early:
                n = i % 5
                return RG[:, n, :] if n < 3 else PA[:, NPA - (n - 2) * 2048:NPA - (n - 3) * 2048]
            return RG[:, i % 3, :]

        def pump(i, ahead=2):
            while True:
                moved = False
                if st.dma_n < min(len(st.plan), st.limit):
                    n = st.dma_n
                    parts, split, early = st.plan[n]
                    key = (n % 5) if early else (n % 3)
                    prev = st.owner[key]
                    if prev is None or prev.raw_free() is not None:
                        p = Piece()
                        p.i, p.split, p.used, p.done = n, split, None, None
                        p.raw_free = lambda p=p: p.done if p.split else p.used
                        p.ap = slot_of(n, early)
                        if prev is not None:
                            D.wait(prev.raw_free())
                        for dst, src in parts:
                            p.tok = st.sems[key].dma(D, dst(p.ap), src)
                        st.owner[key] = p
                        st.pieces.append(p)
                        st.dma_n += 1
                        moved = True
                n = st.prep_n
                if n <= i + ahead and n < len(st.pieces):
                    p = st.pieces[n]
                    if not p.split:
                        st.prep_n += 1
                        moved = True
                    elif not st.hold and (st.wowner[st.wn % NW] is None or st.wowner[st.wn % NW].used is not None):
                        w = st.wn % NW
                        prev = st.wowner[w]
                        rel = prev.used if prev is not None else None
                        p.h, p.l = WH[:, w, :], WL[:, w, :]
                        x = S.act(p.h, p.ap, ACT.Copy, p.tok, rel)
                        y = st.low.tt(p.l, p.ap, p.h.bitcast(F32), ALU.subtract, x, rel)
                        p.done = [x, y]
                        p.tok = y
                        st.wowner[w] = p
                        st.wn += 1
                        st.prep_n += 1
                        moved = True
                if not moved:
                    break
            assert i < st.prep_n, i

        def split_act(src, ready, scale=1.0, n=4):
            ts_ = PerK()
            for c in range(n):
                sl = slice(c * 512, c * 512 + 512)
                x = S.act(AH[:, sl], src[:, sl], ACT.Copy, ready, E.last, scale=scale)
                ts_.append(V.stt(AL[:, sl], src[:, sl], scale, AH[:, sl].bitcast(F32), ALU.mult, ALU.subtract, x))
            return ts_

        def rk(ready, k):
            return ready[k // 2] if isinstance(ready, PerK) else ready

        def mm3(out, l, r, start, stop, *after, sig=False):
            (lh, ll), (rh, rl) = l, r
            E.mm(out, lh, rh, start, False, *after)
            E.mm(out, lh, rl, False, False)
            return E.mm(out, ll, rh, False, stop, sig=sig)

        def hl(f):
            return f(AH), f(AL)

        def act_k(k):
            return hl(lambda a_: a_[:, k * 256:k * 256 + 256])

        def act_kt(k, tt):
            return hl(lambda a_: a_[:, k * 256 + tt * 128:k * 256 + tt * 128 + 128])

        def wsl(pc, n, k, c0, c1):
            return v3(pc.h, n)[:, k, c0:c1], v3(pc.l, n)[:, k, c0:c1]

        def wcols(W, c0, n, k0=0, kn=KT):
            src = W[k0 * 128:(k0 + kn) * 128, c0:c0 + n].rearrange("(k p) n -> p k n", p=128)
            return (lambda r: r[:, 0:kn * n].rearrange("p (k n) -> p k n", k=kn)), src

        def v3(ap, n):
            return ap.rearrange("p (a n) -> p a n", n=n)

        def fence():
            toks = [V.last, S.last, G.last, E.last]
            for q in (V, S, G, E):
                q.wait(*toks)
            return toks

        H = Hb[:, :].rearrange("p (t c) -> p t c", t=2)
        S1 = Sb[:, :].rearrange("p (t c) -> p t c", t=2)
        XT = Xb[:, :].rearrange("p (k t) -> p k t", k=8)

        def mode_b(W, c0, npair, evac, banks, ready, rhs=None, nk=KT, tail=False):
            for j in range(npair):
                pc = load(wcols(W, c0 + 256 * j, 256), split=rhs is None, early=rhs is not None,
                          tail=tail and j == npair - 1)
                b = banks[j % len(banks)]
                for m in range(2):
                    if m:
                        hook()
                    for k in range(nk):
                        o_ = PS[b][:, m * 256:(m + 1) * 256]
                        if rhs is None:
                            t = mm3(o_, wsl(pc, 256, k, m * 128, m * 128 + 128), act_k(k), k == 0, k == nk - 1,
                                    pc.tok, bank_free[b], rk(ready, k), sig=(m == 1 and k == nk - 1))
                        else:
                            t = E.mm(o_, v3(pc.ap, 256)[:, k, m * 128:(m + 1) * 128], rhs(k),
                                     k == 0, k == nk - 1, pc.tok, bank_free[b], rk(ready, k), sig=(m == 1 and k == nk - 1))
                free(pc, t)
                bank_free[b] = evac(j, PS[b][:, :].rearrange("p (m t) -> p m t", m=2), t)

        def mode_a(W, c0, nhalf, evac, banks, ready, lhs=None, nk=KT, tail=False):
            for h in range(nhalf):
                bb = [banks[(2 * h + tt) % len(banks)] for tt in range(2)]
                for kp in range(nk // 4):
                    pc = load(wcols(W, c0 + 512 * h, 512, 4 * kp, 4), split=lhs is None, early=lhs is not None,
                              tail=tail and h == nhalf - 1 and kp == nk // 4 - 1)
                    for tt in range(2):
                        if tt:
                            hook()
                        for k in range(4):
                            kk = 4 * kp + k
                            args = (kk == 0, kk == nk - 1, pc.tok, bank_free[bb[tt]], rk(ready, kk))
                            if lhs is None:
                                t = mm3(PS[bb[tt]][:, :], act_kt(kk, tt), wsl(pc, 512, k, 0, 512), *args, sig=(k == 3))
                            else:
                                t = E.mm(PS[bb[tt]][:, :], lhs(kk, tt), v3(pc.ap, 512)[:, k, :], *args, sig=(k == 3))
                        if kk == nk - 1:
                            bank_free[bb[tt]] = evac(h, tt, PS[bb[tt]][:, :], t)
                    free(pc, t)

        def to_chan(src, dst, ready, banks, g=None, b=None, split=True):
            toks = PerK()
            tr_t = []
            for tt in range(2):
                for k in range(KT):
                    bk, m = banks[k // 2], k % 2
                    rdy = ready[tt] if isinstance(ready, PerT) else ready
                    t = E.tr(PS[bk][:, (2 * m + tt) * 128:(2 * m + tt + 1) * 128],
                             src[:, tt, k * 128:(k + 1) * 128], ident, rdy, bank_free[bk], sig=(m == 1 and tt == 1))
                    if t:
                        tr_t.append(t)

            def evict(kp):
                bk, t = banks[kp], tr_t[kp]
                rel = []
                for m in range(2):
                    k = 2 * kp + m
                    pv = PS[bk][:, m * 256:(m + 1) * 256]
                    if kp % 2 == 0 and g is not None:
                        e = S.act(dst[:, k, :], pv, ACT.Identity, t, scale=vec(g, k), bias=(vec(b, k) if b else 0.0))
                    elif g is not None:
                        if b:
                            e = V.ts(dst[:, k, :], pv, vec(g, k), vec(b, k), ALU.mult, ALU.add, t)
                        else:
                            e = V.ts(dst[:, k, :], pv, vec(g, k), None, ALU.mult, None, t)
                    elif kp % 2 == 0:
                        e = S.act(dst[:, k, :], pv, ACT.Copy, t)
                    else:
                        e = V.op(lambda q, o=dst[:, k, :], i=pv: q.tensor_copy(o, i), (t,))
                    rel.append(e)
                bank_free[bk] = rel

            def halve(kp):
                rel = bank_free[banks[kp]]
                if split:
                    sl = slice(kp * 512, kp * 512 + 512)
                    d = dst.rearrange("p k t -> p (k t)")[:, sl]
                    x = S.act(AH[:, sl], d, ACT.Copy, rel, e_done)
                    toks.append(V.tt(AL[:, sl], d, AH[:, sl].bitcast(F32), ALU.subtract, x))
                else:
                    toks.append(rel)
            e_done = E.last
            for kp in range(5):
                if kp < 4:
                    evict(kp)
                if kp:
                    halve(kp - 1)
            return toks

        def rstd_of(var, o, eps, scale, ready):
            t = V.ts(o, var, scale, eps, ALU.mult, ALU.add, ready)
            t = S.act(o, o, ACT.Sqrt, t)
            return V.op(lambda e: e.reciprocal(o, o), (t,))

        def rms_norm(src, ready):
            if not ready:
                ready = [V.last, G.last]
            rs = rms_sums(src)
            for tt in range(2):
                for h in range(2):
                    rs(tt, h, ready)
            return rms_scale(src)

        def rms_sums(src):
            S.act(ST[:, 4:5], cst('ones')[:, 0:1], ACT.Sqrt)
            v0 = [E.last, G.last, V.last]

            def f(tt, h, ready):
                sl = slice(h * 512, h * 512 + 512)
                o_ = ST[:, 2 * tt + h:2 * tt + h + 1]
                S.act(S1[:, tt, sl], src[:, tt, sl], ACT.Square, ready, v0, accum=o_)
            return f

        def rms_scale(src):
            s4 = ST[:, 0:4].rearrange("p (t h) -> p t h", h=2)
            r = V.tt(ST[:, 6:8], s4[:, :, 0], s4[:, :, 1], ALU.add, S.last)
            r = rstd_of(ST[:, 6:8], ST[:, 60:62], EPS, 1.0 / C, r)
            rd = [ST[:, 60 + tt:61 + tt] for tt in range(2)]
            x = V.ts(S1[:, 0, :], src[:, 0, :], rd[0], None, ALU.mult, None, r)
            y = S.act(S1[:, 1, :], src[:, 1, :], ACT.Copy, r, scale=rd[1])
            return PerT([x, y])

        def residual_ln(banks, toks, gi, bi, gname, bname, halves_first=False, extra=None, last=False):
            g0 = G.last

            def part(tt, h):
                sl = slice(h * 512, h * 512 + 512)
                b = banks[2 * tt + h]
                e = V.stt(S1[:, tt, sl], H[:, tt, sl], ALPHA, PS[b][:, :], ALU.mult, ALU.add, toks[2 * tt + h], g0, extra)
                bank_free[b] = e
                o_ = ST[:, 16 + 12 * tt + 6 * h:22 + 12 * tt + 6 * h]
                return V.op(lambda q, o=o_, i=S1[:, tt, sl]: q.bn_stats(o, i), (e,))
            pc = load((lambda r_: r_[:, 0:1024], gi.broadcast_to([128, 1024])),
                      (lambda r_: r_[:, 1024:2048], bi.broadcast_to([128, 1024])), tail=True)
            if not last:
                S.act(ST[:, 4:5], cst('ones')[:, 0:1], ACT.Sqrt)
            if halves_first:
                part(0, 0), part(1, 0)
            n, out_ = PerT(), []
            rs = rms_sums(H) if last else None
            for tt in range(2):
                if not halves_first:
                    part(tt, 0)
                e = part(tt, 1)
                e = V.op(lambda q, o=ST[:, 8 + 2 * tt:10 + 2 * tt], i=ST[:, 16 + 12 * tt:28 + 12 * tt]: q.bn_aggr(o, i),
                         (V.last,))
                r = rstd_of(ST[:, 9 + 2 * tt:10 + 2 * tt], ST[:, 2 + tt:3 + tt], LN_EPS, 1.0, e)
                nb = V.stt(ST[:, 60 + tt:61 + tt], ST[:, 8 + 2 * tt:9 + 2 * tt], -1.0, ST[:, 2 + tt:3 + tt],
                           ALU.mult, ALU.mult, r)
                if last and tt:
                    for h in range(2):
                        sl = slice(h * 512, h * 512 + 512)
                        y = V.stt(H[:, tt, sl], S1[:, tt, sl], ST[:, 10:11], pc.ap[:, sl], ALU.subtract, ALU.mult, pc.tok, r)
                        out_.append(V.stt(H[:, tt, sl], H[:, tt, sl], ST[:, 3:4], pc.ap[:, 1024 + h * 512:1536 + h * 512],
                                          ALU.mult, ALU.add, y))
                        rs(tt, h, [out_[-1]])
                    free(pc, out_)
                    rs(0, 0, [out_[0]])
                    rs(0, 1, [out_[1]])
                    return out_
                cut = 1024 if tt == 0 else 512
                y = S.act(S1[:, tt, 0:cut], S1[:, tt, 0:cut], ACT.Identity, nb, scale=ST[:, 2 + tt:3 + tt],
                          bias=ST[:, 60 + tt:61 + tt])
                x = None
                if tt:
                    x = V.ts(S1[:, tt, 512:1024], S1[:, tt, 512:1024], ST[:, 8 + 2 * tt:9 + 2 * tt], ST[:, 2 + tt:3 + tt],
                             ALU.subtract, ALU.mult, r)
                n.append([x, y])
                if last:
                    for h in range(2):
                        sl = slice(h * 512, h * 512 + 512)
                        y = G.tt(H[:, 0, sl], S1[:, 0, sl], pc.ap[:, sl], ALU.mult, n, pc.tok)
                        out_.append(G.tt(H[:, 0, sl], H[:, 0, sl], pc.ap[:, 1024 + h * 512:1536 + h * 512], ALU.add, y))
            x = to_chan(S1, XT, n, [0, 1, 2, 3], gname, bname)
            for tt in range(2):
                e = G.tt(H[:, tt, :], S1[:, tt, :], pc.ap[:, 0:1024], ALU.mult, n, pc.tok)
                e = G.tt(H[:, tt, :], H[:, tt, :], pc.ap[:, 1024:2048], ALU.add, e)
            free(pc, e)
            return x

        def attention(nh, q, k, v, outp, od, scale, causal, tmp, ready, ready_v, outs, mask=None, mask_tok=None,
                      banks=(0, 1, 2, 3, 4, 5)):
            W = 384 if causal else 512
            if causal:
                Sm = v3(tmp[:, 0:768], 384)
            P, PT = v3(tmp[:, 768:768 + 3 * W], W) if causal else v3(tmp[:, 0:3 * W], W), v3(tmp[:, 2048:2048 + 2 * W], W)
            sp = [(0, 128), (128, 384)] if causal else [(0, 256), (256, 512)]
            stt_ = ST[:, 64:64 + 24].rearrange("p (s n) -> p s n", n=8)
            sc_t, sm_free, p_t, p_free, pt_t, pt_free = {}, {}, {}, {}, {}, {}
            for i in range(nh + 3):
                if i < nh:
                    b = banks[i % 2]
                    for tt in range(2):
                        lo, hi = sp[tt]
                        t = E.mm(PS[b][:, lo:hi], q(i)[:, tt * 128:tt * 128 + 128], k(i)[:, 0:hi - lo], True, True,
                                 bank_free[b], ready(i), sig=(tt == 1))
                    sc_t[i] = b, t
                if 2 <= i < nh + 2:
                    h = i - 2
                    b = banks[2 + h % 2]
                    p = P[:, h % 3, :]
                    if causal:
                        blocks = [(0, 0), (128, 128), (256, 256)]
                    else:
                        blocks = [(0, 0), (128, 256), (256, 128), (384, 384)]
                    for n, (dst, s0) in enumerate(blocks):
                        t = E.tr(PS[b][:, dst:dst + 128], p[:, s0:s0 + 128], ident, p_t[h], bank_free[b],
                                 sig=(n == len(blocks) - 1))
                    p_free[h] = t
                    x = S.act(PT[:, h % 2, 0:W], PS[b][:, 0:W], ACT.Copy, t, pt_free.get(h - 2))
                    bank_free[b] = x
                    pt_t[h] = x
                if i >= 3:
                    h = i - 3
                    parts, dst, last = outp(h)
                    b = banks[4 + (h // od) % 2]
                    pt = PT[:, h % 2, :]
                    E.mm(PS[b][parts, 0:256], v(h, 0), pt[:, 0:256], True, False, pt_t[h], bank_free[b], ready_v(h))
                    if causal:
                        t = E.mm(PS[b][parts, 128:256], v(h, 1), pt[:, 256:384], False, True, sig=True)
                    else:
                        t = E.mm(PS[b][parts, 0:256], v(h, 1), pt[:, 256:512], False, True, sig=True)
                    pt_free[h] = t
                    if last:
                        x = S.act(dst, PS[b][:, 0:256], ACT.Copy, t)
                        bank_free[b] = x
                        outs.append(x)
                if i < nh:
                    b, t = sc_t[i]
                    s = stt_[:, i % 3, :]
                    if mask is not None:
                        for tt in range(2):
                            lo, hi = sp[tt]
                            e = V.op(lambda qq, o=Sm[:, i % 2, lo:hi], x=PS[b][:, lo:hi], m=mask[:, lo:hi], ac=s[:, tt:tt + 1]:
                                     qq.tensor_tensor_reduce(o, x, m, 1.0, TAKEN, ALU.add, ALU.max, ac),
                                     (t, mask_tok and mask_tok(), sm_free.get(i - 2)))
                        bank_free[b] = e
                        src = Sm[:, i % 2, :]
                    else:
                        e = V.op(lambda qq, o=s[:, 0:2], x=PS[b][:, :].rearrange("p (t s) -> p t s", t=2):
                                 qq.tensor_reduce(o, x, AX, ALU.max), (t, sm_free.get(i - 3)))
                        src = PS[b][:, :]
                    e = V.ts(s[:, 2:4], s[:, 0:2], -scale, None, ALU.mult, None, e)
                    for tt in range(2):
                        lo, hi = sp[tt]
                        x = S.act(P[:, i % 3, lo:hi], src[:, lo:hi], ACT.Exp, e, p_free.get(i - 3), scale=scale,
                                  bias=s[:, 2 + tt:3 + tt], accum=s[:, 4 + tt:5 + tt])
                    sm_free[i] = x
                    if mask is None:
                        bank_free[b] = x
                    e = V.op(lambda qq, o=s[:, 6:8], ii=s[:, 4:6]: qq.reciprocal(o, ii), (x,))
                    for tt in range(2):
                        lo, hi = sp[tt]
                        p_t[i] = V.ts(P[:, i % 3, lo:hi], P[:, i % 3, lo:hi], s[:, 6 + tt:7 + tt], None, ALU.mult, None, e)
                yield

        def ffn(w_in, w_down, n, gated, ready):
            GT = v3(PF[:, 0:1024], 512)
            HT = v3(PF[:, 1024:2048], 512)
            F = 256 * n
            hfree, gfree, ht = {}, {}, {}

            def down(j):
                pd = load(wcols(w_down, 0, 1024, 2 * j, 2), split=True, tail=j == n - 1)
                done = []
                for tt in range(2):
                    for h in range(2):
                        bb = 4 + 2 * tt + h
                        for m in range(2):
                            c0 = m * 256 + tt * 128
                            t = mm3(PS[bb][:, :], (HH[:, j % 2, c0:c0 + 128], HL[:, j % 2, c0:c0 + 128]),
                                    wsl(pd, 1024, m, h * 512, h * 512 + 512), j == 0 and m == 0, j == n - 1 and m == 1,
                                    pd.tok, ht[j], bank_free[bb], sig=(m == 1))
                        done.append(t)
                free(pd, t)
                hfree[j] = t
                return done

            for j in range(n + 1):
                if j < n:
                    for u in range(2 if gated else 1):
                        pc = load(wcols(w_in, u * F + 256 * j, 256), split=True)
                        b = (2 * (j % 2) + u) if gated else j % 4
                        for m in range(2):
                            for k in range(KT):
                                t = mm3(PS[b][:, m * 256:m * 256 + 256], wsl(pc, 256, k, m * 128, m * 128 + 128), act_k(k),
                                        k == 0, k == 7, pc.tok, bank_free[b], rk(ready, k), sig=(m == 1 and k == 7))
                        free(pc, t)
                        if u == 0:
                            g = S.act(GT[:, j % 2, :], PS[b][:, :], ACT.Silu if gated else ACT.Relu, t, gfree.get(j - 2))
                            if gated:
                                bank_free[b] = g
                    f = HT[:, j % 2, :]
                    x = V.tt(f, GT[:, j % 2, :], PS[b][:, :], ALU.mult, g, t)
                    bank_free[b] = x
                    gfree[j] = x
                    x = S.act(HH[:, j % 2, :], f, ACT.Copy, x, hfree.get(j - 2))
                    ht[j] = V.tt(HL[:, j % 2, :], f, HH[:, j % 2, :].bitcast(F32), ALU.subtract, x)
                if j >= 1:
                    t = down(j - 1)
            for b in range(4, 8):
                bank_free[b] = None
            return t

        def run():
            tvec = s_v.dma(D, VB[:, :], a['vec'])
            tx = s_x.dma(D, XT, a['xT'].rearrange("(k p) t -> p k t", p=128))
            for q in (V, S):
                q.wait(tvec)
            V.ts(HV[:, 0:16], VB[:, HVI:HVI + 16], 0.5, None, ALU.mult, None)
            V.ts(HV[:, 16:32], VB[:, HVG:HVG + 16], 0.5, None, ALU.mult, None)

            o = 0

            def take(n):
                nonlocal o
                r = area[:, o:o + n]
                o += n
                assert o <= area.shape[1], o
                return r

            area = PA
            o = NLOW

            VV = take(2048).rearrange("p (t c) -> p t c", t=2)
            YY = take(2048).rearrange("p (t c) -> p t c", t=2)
            SG = take(512).rearrange("p (m t) -> p m t", m=2)
            AR = take(4096).rearrange("p (m c s t) -> p m c s t", m=8, c=2, s=2)
            BE = take(2048).rearrange("p (m t) -> p m t", m=8)
            KA = take(2048).rearrange("p (m t) -> p m t", m=8)
            DX = take(8)
            assert o <= NPA - 4096
            o = 0
            BV = PA[:, NLOW - 2048:NLOW].rearrange("p (t c) -> p t c", t=2)
            XX = take(2048).rearrange("p (k t) -> p k t", k=8)
            XM = [take(2048).rearrange("p (k t) -> p k t", k=8) for _ in range(2)]
            P2 = take(2048)
            TW = take(256)
            TA = take(256)
            cs = take(516).rearrange("p (a t) -> p a t", t=129)
            EE = take(516).rearrange("p (a t) -> p a t", t=129)
            EI, sg, aa0, aa1, kS, rS, kk, qq = (take(512) for _ in range(8))
            assert o <= NLOW - 2048

            w = V.ts(XX[:, :, 0:1], XT[:, :, 0:1], -1.0, None, ALU.mult, None, tx)
            ww = []
            mset = G.op(lambda e: e.memset(cs[:, :, 0:1], 0.0), ())
            xm_free = [None] * 2

            def mix(i, n):
                slot = i % 2
                ts_ = PerK()
                for k in range(KT):
                    if len(ww) <= k // 2:
                        ww.append(V.tt(XX[:, k:k + 2, 1:256], XT[:, k:k + 2, 0:255], XT[:, k:k + 2, 1:256],
                                       ALU.subtract, w))
                    t = V.stt(XM[slot][:, k, :], XX[:, k, :], vec(f'mu{n}', k), XT[:, k, :], ALU.mult, ALU.add,
                              ww[k // 2], xm_free[slot])
                    if k % 2:
                        ts_.append(t)
                return slot, ts_

            st.limit = 2
            pc = load((lambda r: v3(r[:, 0:512], 64), a['w1'].rearrange("(k p) n -> p k n", p=128)),
                      (lambda r: v3(r[:, 512:1024], 64), a['a1'].rearrange("(k p) n -> p k n", p=128)), early=True)
            pg = load((lambda r: v3(r[:, 0:1280], 160), a['g1'].rearrange("(k p) n -> p k n", p=128)), early=True)
            st.limit = 5
            if st.plan is not None:
                pump(1)
            s_io.dma(D, P2[0:64, 0:1024], a['w2'])
            p2t = s_io.dma(D, P2[0:64, 1024:2048], a['a2'])
            for i, (n, fn, dst) in enumerate([(1, ACT.Tanh, TW), (4, ACT.Copy, TA)]):
                slot, t = mix(i, n)
                wv = v3(pc.ap[:, i * 512:(i + 1) * 512], 64)
                for k in range(KT):
                    e = E.mm(PS[5 + i][0:64, 0:256], wv[:, k, :], XM[slot][:, k, :], k == 0, k == 7,
                             rk(t, k), pc.tok, bank_free[5 + i], sig=(k == 7))
                xm_free[slot] = e
                low = S.act(dst[0:64, :], PS[5 + i][0:64, 0:256], fn, e)
            free(pc, e)
            slot, t = mix(2, 5)
            wv = v3(pg.ap[:, 0:1280], 160)
            for m, (c0, c1) in enumerate([(0, 128), (128, 160)]):
                for k in range(KT):
                    e = E.mm(PS[7 - 4 * m][0:c1 - c0, 0:256], wv[:, k, c0:c1], XM[slot][:, k, :],
                             k == 0, k == 7, rk(t, k), pg.tok, bank_free[7 - 4 * m], sig=(k == 7))
                sgt = S.act(SG[0:c1 - c0, m, :], PS[7 - 4 * m][0:c1 - c0, 0:256], ACT.Sigmoid, e)
            free(pg, e)
            xm_free[slot] = e
            bank_free[5] = bank_free[6] = low
            bank_free[7] = bank_free[3] = sgt
            st.limit = 7
            if st.plan is not None:
                pump(1)
            tm = s_m.dma(D, H, a['mem'].rearrange("(t p) c -> p t c", p=128))
            tcst = s_c.dma(D, CB[:, :], a['cst'])
            st.limit = 10 ** 6
            vs, vt_ = mix(3, 3)
            S.wait(tcst)
            nrm = rms_norm(H, [tm])
            vv_t = []

            def ev_v(h, tt, b, t):
                x = S.act(VV[:, tt, h * 512:h * 512 + 512], b, ACT.Copy, t)
                vv_t.append(x)
                return x
            mode_a(a['w_rkv'][2], 0, 2, ev_v, [0, 1, 2, 4], vt_, lhs=lambda k, tt: XM[vs][:, k, tt * 128:tt * 128 + 128])

            xm_free[vs] = E.last
            ks, kt_ = mix(4, 2)
            rs, rt_ = mix(5, 0)

            for q in (V, G, E):
                q.wait(tcst)
            MT = YY.rearrange("p t c -> p (t c)").rearrange("p (k t) -> p k t", k=8)
            mt = to_chan(S1, MT, nrm, [5, 6, 7, 3], 'nmem', split=False)
            mem_ev = []

            def project_memory():
                mode_b(a['wx_kv'], 0, 2, lambda j, b, t: mem_ev.append((KX[:, 2 * j:2 * j + 2, :], b, 0 + j, t)),
                       [0, 1], mt, rhs=lambda k: MT[:, k, :])
                mode_a(a['wx_kv'], 512, 1, lambda h, tt, b, t: mem_ev.append((VX[:, tt, :], b, 4 + tt, t)),
                       [4, 5], mt, lhs=lambda k, tt: MT[:, k, tt * 128:tt * 128 + 128])
            W_K, W_R, W_V = a['w_rkv'][1], a['w_rkv'][0], a['w_rkv'][2]
            w2v, a2v = P2[0:64, 0:1024], P2[0:64, 1024:2048]
            prev = None
            bon_t, yps = [], []

            def bonus(j):
                for m in range(2):
                    for tt in range(2):
                        t = E.mm(PS[7][:, tt * 256 + m * 128:tt * 256 + m * 128 + 128],
                                 rS[:, m * 256 + tt * 128:m * 256 + tt * 128 + 128], cst('bones'), True, True,
                                 yps[j], bank_free[7], sig=(m == 1 and tt == 1))
                bon_t.append(t)
                cs_ = slice(256 * j, 256 * j + 256)
                bank_free[7] = V.tt(BV[:, :, cs_], PS[7][:, :].rearrange("p (t c) -> p t c", t=2), VV[:, :, cs_],
                                    ALU.mult, t, vv_t[-1])
                return bank_free[7]

            fr = {}

            def decays(j):
                aa = (aa0, aa1)[j % 2]
                for m in range(2):
                    c0 = (2 * j + m) * 128
                    E.mm(PS[4][:, m * 256:m * 256 + 256], w2v[:, c0:c0 + 128], TW[0:64, :], True, True,
                         p2t, low, bank_free[4])
                    tz = E.mm(PS[5][:, m * 256:m * 256 + 256], a2v[:, c0:c0 + 128], TA[0:64, :], True, True,
                              bank_free[5], sig=True)

                def front():
                    scanned, exped, free_a = fr.get(j - 1), fr.get(('exp', j - 1)), fr.get(('end', j - 2))
                    for m in range(2):
                        k = 2 * j + m
                        sl = slice(m * 256, m * 256 + 256)
                        S.act(sg[:, sl], PS[4][:, sl], ACT.Tanh, tz, scanned, scale=0.5, bias=HV[:, k:k + 1])
                        x = S.act(aa[:, sl], PS[5][:, sl], ACT.Tanh, tz, free_a, scale=0.5, bias=HV[:, 8 + k:9 + k])
                    bank_free[4] = bank_free[5] = x
                    y = V.ts(sg, sg, 0.5, 0.5, ALU.mult, ALU.add, x)
                    for q in range(4):
                        y2 = V.op(lambda e, o_=cs[:, q, 1:129], d1=sg[:, q * 128:q * 128 + 128]:
                                  e.tensor_tensor_scan(o_, cst('ones'), d1, 0.0, ALU.mult, ALU.add), (y, mset, exped))
                    V.ts(mid, cs[:, :, 64], CDEC, None, ALU.mult, None, y2)
                    fr['mid', j] = V.ts(nmid, cs[:, :, 64], -CDEC, None, ALU.mult, None, y2)
                    fr[j] = y2
                    V.ts(aa, aa, 0.5, 0.5, ALU.mult, ALU.add, x)
                return front
            mid, nmid, em = ST[:, 32:36], ST[:, 36:40], ST[:, 40:44]
            decays(0)()
            for j in range(4):
                kb, rb = 2 * (j % 2), 2 * (j % 2) + 1
                aa = (aa0, aa1)[j % 2]
                toks = []
                for W, sl, b, rdy in ((W_K, ks, kb, kt_), (W_R, rs, rb, rt_)):
                    pc = load(wcols(W, 256 * j, 256), early=True)
                    wv = v3(pc.ap, 256)
                    for m in range(2):
                        for k in range(KT):
                            t = E.mm(PS[b][:, m * 256:m * 256 + 256], wv[:, k, m * 128:m * 128 + 128], XM[sl][:, k, :],
                                     k == 0, k == 7, pc.tok, rk(rdy, k), bank_free[b], sig=(m == 1 and k == 7))
                    free(pc, t)
                    toks.append(t)
                tk, tr = toks
                if j == 3:
                    xm_free[ks], xm_free[rs] = tk, tr
                y3 = fr['mid', j]
                for q in range(4):
                    S.act(EE[:, q, :], cs[:, q, :], ACT.Exp, y3, prev, scale=-CDEC, bias=mid[:, q:q + 1])
                    x = S.act(EI[:, q * 128:q * 128 + 128], cs[:, q, :][:, 1:129], ACT.Exp, scale=CDEC, bias=nmid[:, q:q + 1])
                x = fr['exp', j] = S.act(em, nmid, ACT.Exp, x, prev)
                for m in range(2):
                    dx = V.tt(DX[:, 2 * j + m:2 * j + m + 1], EE[:, 2 * m, 128:129], em[:, 2 * m + 1:2 * m + 2], ALU.mult, x)
                S.act(kS, PS[kb][:, :], ACT.Copy, tk, prev)
                for m in range(2):
                    k = 2 * j + m
                    sl = slice(m * 256, m * 256 + 256)
                    xk = S.act(kk[:, sl], PS[kb][:, sl], ACT.Copy, scale=vec('k_k', k))
                bank_free[kb] = xk
                xq = S.act(qq, kk, ACT.Square, xk)
                front = decays(j + 1) if j < 3 else None
                t6 = E.mm(PS[6][:, :], cst('bones'), qq, True, True, xq, bank_free[6], sig=True)
                if front:
                    front()
                if j:
                    bonus(j - 1)
                if j == 3:
                    project_memory()
                x = S.act(qq, PS[6][:, :], ACT.Sqrt, t6)
                bank_free[6] = x
                x = V.ts(qq, qq, 1e-12, None, ALU.max, None, x)
                x = V.op(lambda e: e.reciprocal(qq, qq), (x,))
                y = V.tt(kk, kk, qq, ALU.mult, x)
                x = S.act(rS, PS[rb][:, :], ACT.Copy, tr, prev, bon_t[-1] if bon_t else None)
                bank_free[rb] = x
                EA = EE[:, :, 0:128]
                EB = EE[:, :, 1:129]
                ARa = AR[:, 2 * j:2 * j + 2, :, 0, :].rearrange("p m c t -> p (m c) t")
                ARr = AR[:, 2 * j:2 * j + 2, :, 1, :].rearrange("p m c t -> p (m c) t")
                gr = G.tt(ARr, v3(rS, 128), EB, ALU.mult, x)
                V.stt(ARa, v3(kk, 128), -1.0, EA, ALU.mult, ALU.mult, y)
                y = V.tt(kk, kk, aa, ALU.mult, V.last)
                V.tt(BE[:, 2 * j:2 * j + 2, :].rearrange("p m t -> p (m t)"), kk, EI, ALU.mult, y)
                for m in range(2):
                    k = 2 * j + m
                    sl = slice(m * 256, m * 256 + 256)
                    y = V.ts(aa[:, sl], aa[:, sl], -1.0, vec('k_a', k), ALU.add, ALU.mult, y)
                y = V.stt(kS, aa, 1.0, kS, ALU.add, ALU.mult, y)
                gk = G.tt(KA[:, 2 * j:2 * j + 2, :].rearrange("p m t -> p (m t)"), kS, EI, ALU.mult, y)
                for m in range(2):
                    k = 2 * j + m
                    sl = slice(m * 256, m * 256 + 256)
                    yp = V.stt(rS[:, sl], rS[:, sl], vec('r_k', k), kS[:, sl], ALU.mult, ALU.mult, y, gr)
                prev = fr['end', j] = [V.last, gk]
                yps.append(yp)
            for o_, i_, b, t in mem_ev:
                bank_free[b] = S.act(o_, i_, ACT.Copy, t)
            t = bonus(3)
            st.hold = True
            fenced = fence()
            pg2 = load((lambda r: r[:, 0:1024], a['g2'][0:128, :]), (lambda r: r[0:32, 1024:2048], a['g2'][128:160, :]), early=True)
            tb = load((lambda r: r[:, 0:1024], a['gn_g'].broadcast_to([128, 1024])),
                      (lambda r: r[:, 1024:2048], a['gn_b'].broadcast_to([128, 1024])), early=True)
            o = 0
            AT = take(8192).rearrange("p (i s t) -> p i s t", i=16, s=4)
            BT = take(512).rearrange("p (m n) -> p m n", m=4)
            KTt = take(512).rearrange("p (m n) -> p m n", m=4)
            RR = take(512).rearrange("p (g n) -> p g n", g=2)
            SA = take(1024).rearrange("p (g n) -> p g n", g=4)
            SS = take(512).rearrange("p (m e n) -> p m e n", m=4, e=2)
            ss0 = G.op(lambda e: e.memset(SS, 0.0), ())
            assert o <= NLOW - 2048
            Xi = Hb[:, :].rearrange("p (g n) -> p g n", g=4)
            Zi = Sb[:, :].rearrange("p (g n) -> p g n", g=4)
            Wi = Xb[:, :].rearrange("p (g n) -> p g n", g=4)
            i4 = ident.unsqueeze(1).broadcast_to([128, 4, 128])

            def lvl(l):
                off = CST['lvl'][0] + 128 * l
                return CB[:, off:off + 128].unsqueeze(1).broadcast_to([128, 4, 128])
            m0t = cst('m0t').unsqueeze(1).broadcast_to([128, 4, 128])
            VT = vv_t[-1]
            at_t, xz, wt, y_mm, sa_t, rr_t = ([None] * 4 for _ in range(6))
            bt = {}
            turn = [0]

            def prob(half, g, n):
                h = 8 * half + 4 * (g % 2) + n
                return g // 2, h, h // 2, slice(64 * (h % 2), 64 * (h % 2) + 64)

            def form(half, g, banks):
                for n in range(4):
                    c, h, m, pp = prob(half, g, n)
                    i = 4 * g + n
                    b = banks[n % len(banks)]
                    rhs = AR[pp, m, c, :, :].rearrange("p s t -> p (s t)")
                    E.mm(PS[b][:, 0:256], BE[pp, m, c * 128:c * 128 + 128], rhs, True, True, bank_free[b])
                    t = E.mm(PS[b][:, 256:512], KA[pp, m, c * 128:c * 128 + 128], rhs, True, True, sig=True)
                    bank_free[b] = V.tt(AT[:, i, :, :].rearrange("p s t -> p (s t)"), PS[b][:, :], cst('atm'), ALU.mult, t,
                                        y_mm[g])
                at_t[g] = bank_free[b]

            def turned(half, banks):
                for src, dst, b in ((BE, BT, banks[0]), (KA, KTt, banks[1])):
                    for m in range(4):
                        t = E.tr(PS[b][:, m * 128:m * 128 + 128], src[:, 4 * half + m, 0:128], ident, bank_free[b],
                                 sig=(m == 3))
                    bt[half] = S.act(dst.rearrange("p m n -> p (m n)"), PS[b][:, :], ACT.Copy, t, bt.get('used'))
                    bank_free[b] = bt[half]

            def invert_w(l, g):
                b = g
                for n in range(4):
                    rhs = ident if l == 0 else Zi[:, g, n * 128:n * 128 + 128]
                    t = E.mm(PS[b][:, n * 128:n * 128 + 128], AT[:, 4 * g + n, 0, :], rhs, True, True,
                             at_t[g], xz[g] if l else None, bank_free[b], sig=(n == 3))
                wv = v3((Zi if l == 0 else Wi)[:, g, :], 128)
                e = V.tt(wv, v3(PS[b][:, :], 128), lvl(l), ALU.mult, t, sa_t[g])
                bank_free[b] = e
                wt[g] = V.tt(wv, wv, i4, ALU.add, e)
                if l == 0:
                    e = V.tt(v3(Xi[:, g, :], 128), AT[:, 4 * g:4 * g + 4, 0, :], m0t, ALU.mult, at_t[g])
                    xz[g] = V.tt(v3(Xi[:, g, :], 128), v3(Xi[:, g, :], 128), i4, ALU.add, e)

            def invert_xz(l, g):
                bx, bz = 4 + (2 * g) % 4, 5 + (2 * g) % 4
                for n in range(4):
                    ns = slice(n * 128, n * 128 + 128)
                    t = E.mm(PS[bx][:, ns], Wi[:, g, ns], Xi[:, g, ns], True, True, wt[g], bank_free[bx], sig=(n == 3))
                if l < 6:
                    for n in range(4):
                        ns = slice(n * 128, n * 128 + 128)
                        t2 = E.mm(PS[bz][:, ns], Xi[:, g, ns], Wi[:, g, ns], True, True, bank_free[bz], sig=(n == 3))
                    t = t2
                e = S.act(Xi[:, g, :], PS[bx][:, :], ACT.Copy, t)
                bank_free[bx] = e
                if l < 6:
                    e = S.act(Zi[:, g, :], PS[bz][:, :], ACT.Copy, t)
                    bank_free[bz] = e
                xz[g] = e

            def own(ap):
                q = ap.rearrange("p (q e x) -> p q e x", q=2, e=2)
                return [q[:, :, e_, 64 * e_:64 * e_ + 64] for e_ in range(2)]

            def by_head(ap):
                q = ap.rearrange("p (q e x) -> p q e x", q=2, e=2)
                return [q[:, :, e_, :] for e_ in range(2)]


            def rhs_of(half, g, st_t):
                b = g
                for n in range(4):
                    c, h, m, pp = prob(half, g, n)
                    ns = slice(n * 128, n * 128 + 128)
                    t = E.mm(PS[b][:, ns], AT[:, 4 * g + n, 2, :], VV[:, c, m * 128:m * 128 + 128], True, c == 0,
                             bank_free[b], at_t[g], VT, sig=(n == 3))
                    if c == 1:
                        t = E.mm(PS[b][:, ns], AR[:, m, 1, 0, :], SS[:, m - 4 * half, :, :].rearrange("p e n -> p (e n)"),
                                 False, True, st_t, sig=(n == 3))
                for o_, i_ in zip(by_head(RR[:, g % 2, :]), own(PS[b][:, :])):
                    rr_t[g] = S.act(o_, i_, ACT.Copy, t)
                bank_free[b] = rr_t[g]

            def solve(half, g):
                b = 4 + g
                for n in range(4):
                    q = 128 * (n // 2)
                    t = E.mm(PS[b][:, n * 128:n * 128 + 128], Xi[:, g, n * 128:n * 128 + 128],
                             RR[:, g % 2, q:q + 128], True, True, rr_t[g], xz[g], bank_free[b], sig=(n == 3))
                for o_, i_ in zip(by_head(SA[:, g, :]), own(PS[b][:, :])):
                    sa_t[g] = S.act(o_, i_, ACT.Copy, t, y_mm[g])
                bank_free[b] = sa_t[g]

            def state(half):
                for m in range(4):
                    for e_ in range(2):
                        h = 8 * half + 2 * m + e_
                        g, n = (h % 8) // 4, h % 4
                        pp = slice(64 * e_, 64 * e_ + 64)
                        E.mm(PS[6][pp, m * 64:m * 64 + 64], KTt[:, m, pp], VV[:, 0, h * 64:h * 64 + 64], True, False,
                             bank_free[6], bt[half])
                        t = E.mm(PS[6][pp, m * 64:m * 64 + 64], BT[:, m, pp], SA[:, g, n * 64:n * 64 + 64],
                                 False, True, sa_t[g], sig=True)
                bt['used'] = t
                for m in range(4):
                    for e_ in range(2):
                        pp = slice(64 * e_, 64 * e_ + 64)
                        s_ = V.ts(SS[pp, m, e_, :], PS[6][pp, m * 64:m * 64 + 64],
                                  DX[pp, 4 * half + m:4 * half + m + 1], None, ALU.mult, None, t, ss0, y_mm[3])
                bank_free[6] = s_
                return s_

            def outputs(half, c):
                for gg in range(2):
                    g = 2 * c + gg
                    b = 2 + gg
                    for n in range(4):
                        _, h, m, pp = prob(half, g, n)
                        i = 4 * g + n
                        ns = slice(n * 128, n * 128 + 128)
                        q = 128 * (n // 2)
                        E.mm(PS[b][:, ns], AT[:, i, 3, :], VV[:, c, m * 128:m * 128 + 128], True, False, bank_free[b])
                        t = E.mm(PS[b][:, ns], AT[:, i, 1, :], SA[:, g, q:q + 128], False, c == 0, sa_t[g], sig=(n == 3))
                        if c == 1:
                            t = E.mm(PS[b][:, ns], AR[:, m, 1, 1, :], SS[:, m - 4 * half, :, :].rearrange("p e n -> p (e n)"),
                                     False, True, sig=(n == 3))
                    y_mm[g] = t
                    c0 = half * 512 + gg * 256
                    for o_, i_ in zip(by_head(YY[:, c, c0:c0 + 256]), own(PS[b][:, :])):
                        x = S.act(o_, i_, ACT.Copy, t)
                    bank_free[b] = x
                return x

            GT_ = PA[:, 12288:14336].rearrange("p (t c) -> p t c", t=2)
            SQ = AR[:, 0, :, :, :].rearrange("p c s t -> p (c s t)")
            gate_t = []

            def gates():
                for tt in range(2):
                    for h in range(2):
                        b = 4 + 2 * tt + h
                        E.mm(PS[b][:, :], SG[:, 0, tt * 128:tt * 128 + 128], pg2.ap[:, h * 512:h * 512 + 512], True, False,
                             pg2.tok, sgt, bank_free[b])
                        t = E.mm(PS[b][:, :], SG[0:32, 1, tt * 128:tt * 128 + 128],
                                 pg2.ap[0:32, 1024 + h * 512:1536 + h * 512], False, True, sig=True)
                        bank_free[b] = S.act(GT_[:, tt, h * 512:h * 512 + 512], PS[b][:, :], ACT.Copy, t)
                free(pg2, t)
                g_, b_ = (tb.ap[:, i * 1024:i * 1024 + 1024].unsqueeze(1).broadcast_to([128, 2, 1024]) for i in range(2))
                x = G.tt(BV, BV, b_, ALU.add, tb.tok, fenced)
                x = G.tt(BV, BV, GT_, ALU.mult, x, bank_free[7])
                x = G.tt(GT_, GT_, g_, ALU.mult, x)
                free(tb, x)
                gate_t.append(x)

            def group_norm(c, half, ready):
                Y = YY[:, c, half * 512:half * 512 + 512]
                Y3 = v3(Y, 64)
                o_ = 128 + 16 * (2 * c + half)
                mu_, va_ = ST[:, o_:o_ + 8], ST[:, o_ + 8:o_ + 16]
                x = V.op(lambda e: e.tensor_reduce(mu_, Y3, AX, ALU.add), (ready,))
                yield
                x = V.ts(mu_, mu_, 1.0 / 64, None, ALU.mult, None, x)
                x = V.tt(Y3, Y3, mu_.unsqueeze(2).broadcast_to([128, 8, 64]), ALU.subtract, x)
                yield
                x = S.act(SQ, Y, ACT.Square, x, gn_free[0])
                yield
                x = V.op(lambda e: e.tensor_reduce(va_, v3(SQ, 64), AX, ALU.add), (x,))
                gn_free[0] = x
                x = V.ts(va_, va_, 1.0 / 64, GN_EPS, ALU.mult, ALU.add, x)
                yield
                x = S.act(va_, va_, ACT.Sqrt, x)
                yield
                x = V.op(lambda e: e.reciprocal(va_, va_), (x,))
                x = V.tt(Y3, Y3, va_.unsqueeze(2).broadcast_to([128, 8, 64]), ALU.mult, x)
                yield
                x = V.tt(Y, Y, GT_[:, c, half * 512:half * 512 + 512], ALU.mult, x, gate_t[0])
                yield
                yn[c, half] = V.tt(Y, Y, BV[:, c, half * 512:half * 512 + 512], ALU.add, x)
                yield
            gn_free, yn, norms = [None], {}, []

            def norm_step():
                while norms:
                    try:
                        next(norms[0])
                        return
                    except StopIteration:
                        norms.pop(0)

            for half in range(2):
                if half == 0:
                    for g in range(4):
                        if g == 2:
                            gates()
                        form(0, g, [0, 1, 2, 3, 4, 5, 6, 7] if g % 2 == 0 else [4, 5, 6, 7])
                    turned(0, [0, 1])
                for l in range(7):
                    for g in range(4):
                        invert_w(l, g)
                        norm_step()
                    if l:
                        for g in range(4):
                            invert_xz(l, g)
                rhs_of(half, 0, None)
                rhs_of(half, 1, None)
                solve(half, 0)
                solve(half, 1)
                ss_t = state(half)
                norms.append(group_norm(0, half, outputs(half, 0)))
                if half == 1:
                    S.act(ST[:, 4:5], cst('ones')[:, 0:1], ACT.Sqrt)
                if half == 0:
                    form(1, 0, [0, 1, 5])
                rhs_of(half, 2, ss_t)
                rhs_of(half, 3, ss_t)
                if half == 1:
                    norm_step(), norm_step()
                if half == 0:
                    form(1, 1, [0, 1, 4, 5])
                solve(half, 2)
                solve(half, 3)
                if half == 1:
                    for _ in range(3):
                        norm_step()
                if half == 0:
                    turned(1, [0, 1])
                norms.append(group_norm(1, half, outputs(half, 1)))
                if half == 0:
                    gn_free[0] = E.last
                if half == 0:
                    form(1, 2, [0, 1, 4, 5])
                    form(1, 3, [6, 7, 2, 3])

            while len(norms) > 1:
                norm_step()
            toks = [V.last, S.last, G.last, E.last]
            for q in (V, S, G):
                q.wait(toks)
            st.hold, st.low = False, G
            if st.plan is not None:
                pump(st.at - 2)
            st.low = V
            while norms:
                norm_step()
            thx = s_io.dma(D, H, a['x'].rearrange("(t p) c -> p t c", p=128), toks)
            yt = to_chan(YY, XT, PerT([[yn[tt, 0], yn[tt, 1]] for tt in range(2)]), [0, 1, 2, 3])
            toks = []

            def ev_keep(h, tt, b, t):
                toks.append(t)
                return None
            mode_a(a['w_o'], 0, 2, ev_keep, [4, 6, 5, 7], yt, tail=True)
            toks = [toks[0], toks[2], toks[1], toks[3]]
            x1 = residual_ln([4, 5, 6, 7], toks, a['lnmg'][0:1, :], a['lnmb'][0:1, :], 'mixg0', 'mixb0', True, thx)
            t = ffn(a['ffn_w_in'][0], a['ffn_w_down'][0], 11, True, x1)
            x1 = residual_ln([4, 5, 6, 7], t, a['lnfg'][0:1, :], a['lnfb'][0:1, :], 'ffng0', 'ffnb0')

            area = PH
            o = 0
            QQ = take(2048).rearrange("p (k t) -> p k t", k=8)
            KK = take(2048).rearrange("p (k t) -> p k t", k=8)
            VV = take(2048).rearrange("p (t c) -> p t c", t=2)
            OT = take(2048).rearrange("p (k t) -> p k t", k=8)
            raw = [take(512) for _ in range(2)]
            rc = [take(512) for _ in range(2)]
            TMP = take(3072)
            W = a['moba_w_qkv']
            cosb = cst('cos').unsqueeze(1).broadcast_to([128, 2, 256])
            sinb = cst('sin').unsqueeze(1).broadcast_to([128, 2, 256])
            rope_t, raw_free, pend = {}, [None, None], []

            def rope(dst, name, j):
                n_ = 2 * j + (name == 'k')

                def ev(_, b, t):
                    bk = 4 + n_ % 4
                    u = n_ % 2
                    x = S.act(raw[u].rearrange("p (m t) -> p m t", m=2), b, ACT.Copy, t, raw_free[u])
                    g = G.tt(rc[u].rearrange("p (m t) -> p m t", m=2), raw[u].rearrange("p (m t) -> p m t", m=2),
                             cosb, ALU.mult, x, raw_free[u])

                    def turn_():
                        t2 = E.mm(PS[bk][:, :], cst('perm'), raw[u], True, True, x, sig=True)
                        d = dst[:, 2 * j:2 * j + 2, :]
                        y = V.tt(d, PS[bk][:, :].rearrange("p (m t) -> p m t", m=2), sinb, ALU.mult, t2)
                        bank_free[bk] = y
                        y = V.tt(d, d, rc[u].rearrange("p (m t) -> p m t", m=2), ALU.add, y, g)
                        raw_free[u] = [y, t2]
                        rope_t[name, j] = y
                    if pend:
                        pend.pop()()
                    pend.append(turn_)
                    return x
                return ev
            vt = {}

            def ev_v2(h):
                def ev(_, tt, b, t):
                    vt[h] = S.act(VV[:, tt, h * 512:h * 512 + 512], b, ACT.Copy, t)
                    return vt[h]
                return ev

            def hp(h):
                return slice(64 * (h % 2), 64 * (h % 2) + 64)
            outs = []
            steps = attention(16, lambda h: QQ[hp(h), h // 2, :], lambda h: KK[hp(h), h // 2, :],
                              lambda h, s: VV[:, s, h * 64:h * 64 + 64],
                              lambda h: (hp(h), OT[:, h // 2, :], h % 2 == 1), 2, 0.125, True, TMP,
                              lambda h: [rope_t['q', h // 4], rope_t['k', h // 4]], lambda h: vt[h // 8], outs,
                              mask=cst('cmask'), banks=(0, 1, 2, 2, 3, 3))

            def step():
                next(steps)

            mode_a(W, 2048, 1, ev_v2(0), [0, 1], x1)
            one = [step]
            st.hooks = [[]] * 6 + [one] * 8 + [[], [lambda: pend.pop()()]] + [one] * 4
            for j in range(4):
                if j == 3:
                    mode_a(W, 2560, 1, ev_v2(1), [6, 7], x1)
                mode_b(W, 256 * j, 1, rope(QQ, 'q', j), [4 + 2 * j % 4], x1)
                mode_b(W, 1024 + 256 * j, 1, rope(KK, 'k', j), [5 + 2 * j % 4], x1)
            pend.pop()()
            sa = PerK()
            OTf = OT.rearrange("p k t -> p (k t)")

            def split_heads(c):
                sl = slice(c * 512, c * 512 + 512)
                x = S.act(AH[:, sl], OTf[:, sl], ACT.Copy, outs, e_done)
                sa.append(V.tt(AL[:, sl], OTf[:, sl], AH[:, sl].bitcast(F32), ALU.subtract, x))
            e_done = E.last
            split_heads(0)
            split_heads(1)
            toks = [None] * 4
            st.hooks = [one] * 4
            for kp in range(2):
                for h in range(2):
                    pc = load(wcols(a['moba_w_o'], 512 * h, 512, 4 * kp, 4), split=True, tail=h == 1)
                    for tt in range(2):
                        if tt:
                            hook()
                        b = 4 + 2 * tt + h
                        for k in range(4):
                            kk_ = 4 * kp + k
                            t = mm3(PS[b][:, :], act_kt(kk_, tt), wsl(pc, 512, k, 0, 512), kk_ == 0, kk_ == 7,
                                    pc.tok, bank_free[b], rk(sa, kk_), sig=(k == 3))
                        toks[2 * tt + h] = t
                    free(pc, t)
                if kp == 0:
                    step(), step(), step()
                    split_heads(2)
                    split_heads(3)
            x1 = residual_ln([4, 5, 6, 7], toks, a['lnmg'][1:2, :], a['lnmb'][1:2, :], 'mixg1', 'mixb1', True)
            t = ffn(a['ffn_w_in'][1], a['ffn_w_down'][1], 11, True, x1)
            hx = residual_ln([4, 5, 6, 7], t, a['lnfg'][1:2, :], a['lnfb'][1:2, :], 'ffng1', 'ffnb1', last=True)

            nrm = rms_scale(H)
            fence()
            xt = to_chan(S1, XT, nrm, [0, 1, 2, 3], 'nmix')
            o = 0
            UB = take(8 * 286).rearrange("p (k t) -> p k t", k=8)
            CV = take(2048).rearrange("p (k t) -> p k t", k=8)
            QQ = take(2048).rearrange("p (k t) -> p k t", k=8)
            KK = take(2048).rearrange("p (k t) -> p k t", k=8)
            VV = take(2048).rearrange("p (t c) -> p t c", t=2)
            GC = take(2048).rearrange("p (k t) -> p k t", k=8)
            GA = take(2048).rearrange("p (k t) -> p k t", k=8)
            OT = QQ
            TMP = take(3072)
            WI = take(16)
            SC = take(384)
            sgb = [TMP[:, i * 512:(i + 1) * 512] for i in range(2)]
            QI = TMP[:, 1024:2048].rearrange("p (k t) -> p k t", k=4)
            KI = TMP[:, 2048:2304]
            RL = [TMP[:, 2304:2688], TMP[:, 2688:3072]]
            W = a['w_in2']
            z = G.op(lambda e: e.memset(UB[:, :, 0:30], 0.0), ())
            conv_t = []
            st.rate = 6
            conv_done = []

            def conv(k):
                tok = [conv_t[k // 2], z]

                def tap(i):
                    def f():
                        if i == 30:
                            tok[:] = [V.ts(CV[:, k, :], UB[:, k, 30:286], vec('cw30', k), vec('conv_b', k), ALU.mult, ALU.add, *tok)]
                        else:
                            tok[:] = [V.stt(CV[:, k, :], UB[:, k, i:i + 256], vec(f'cw{i}', k), CV[:, k, :],
                                            ALU.mult, ALU.add, *tok)]
                        conv_done[:] = tok
                    return f
                return [tap(i) for i in [30] + list(range(30))]

            def conv_pool(k, buf):
                y = G.ts(CV[:, k, :], UB[:, k, 30:286], vec('cw30', k), vec('conv_b', k), ALU.mult, ALU.add, conv_t[k // 2], z)
                for i in range(30):
                    x = G.ts(buf, UB[:, k, i:i + 256], vec(f'cw{i}', k), 0.0, ALU.mult, ALU.add, y)
                    y = G.tt(CV[:, k, :], CV[:, k, :], buf, ALU.add, x)
                return y

            sg_free = [None, None]
            cp = []
            for j in range(4):
                bs = []
                for u in range(2):
                    pc = load(wcols(W, 1024 * u + 256 * j, 256), split=True)
                    b = 2 * (j % 2) + u
                    for m in range(2):
                        for k in range(KT):
                            t = mm3(PS[b][:, m * 256:m * 256 + 256], wsl(pc, 256, k, m * 128, m * 128 + 128), act_k(k),
                                    k == 0, k == 7, pc.tok, bank_free[b], rk(xt, k), sig=(m == 1 and k == 7))
                    free(pc, t)
                    bs.append((b, t))
                (ba, ta), (bg, tg) = bs
                x = S.act(sgb[j % 2], PS[bg][:, :], ACT.Sigmoid, tg, sg_free[j % 2])
                bank_free[bg] = x
                y = V.tt(UB[:, 2 * j:2 * j + 2, 30:286], PS[ba][:, :].rearrange("p (m t) -> p m t", m=2),
                         sgb[j % 2].rearrange("p (m t) -> p m t", m=2), ALU.mult, x, ta)
                bank_free[ba] = y
                sg_free[j % 2] = y
                conv_t.append(y)
                if j < 2:
                    st.beside += [f for k in (2 * j, 2 * j + 1) for f in conv(k)]
                else:
                    cp += [conv_pool(2 * j, Sb[:, 0:256]), conv_pool(2 * j + 1, Sb[:, 0:256])]

            q_t = []

            def ev_to(dst):
                def ev(j, b, t):
                    q_t.append(S.act(dst[:, 2 * j:2 * j + 2, :], b, ACT.Copy, t))
                    return q_t[-1]
                return ev
            mode_b(W, 5120, 2, ev_to(QI), [0, 1], xt)
            src = W[:, 5632:5704].rearrange("(k p) n -> p k n", p=128)
            pc = load((lambda r: v3(r[:, 0:1088], 136)[:, :, 0:64], src[:, :, 0:64]),
                      (lambda r: v3(r[:, 0:1088], 136)[:, :, 64:136], src[:, :, 0:72]))
            kw = v3(pc.ap[:, 0:1088], 136)
            for k in range(KT):
                t = E.mm(PS[2][:, 0:256], kw[:, k, 0:128], XT[:, k, :], k == 0, k == 7, pc.tok,
                         bank_free[2], sig=(k == 7))
            for tt in range(2):
                for k in range(KT):
                    t = E.mm(PS[2][:, 256 + 128 * tt:384 + 128 * tt], XT[:, k, tt * 128:tt * 128 + 128], kw[:, k, 8:136],
                             k == 0, k == 7, sig=(k == 7))
            free(pc, t)
            S.act(KI, PS[2][:, 0:256], ACT.Copy, t)
            x = S.act(WI.rearrange("p (t n) -> p t n", t=2), v3(PS[2][:, 256:512], 128)[:, :, 120:128], ACT.Copy, scale=8 ** -0.5)
            bank_free[2] = x
            ki_t = x
            sp = [(0, 128), (128, 384)]
            y = None
            rl_free = [None, None]
            for h in range(8):
                b = 4 + h % 2
                for tt in range(2):
                    lo, hi = sp[tt]
                    t = E.mm(PS[b][:, lo:hi], QI[hp(h), h // 2, tt * 128:tt * 128 + 128], KI[hp(h), 0:hi - lo], True, True,
                             ki_t, q_t[-1], bank_free[b], sig=(tt == 1))
                x = S.act(RL[h % 2], PS[b][:, 0:384], ACT.Relu, t, rl_free[h % 2], scale=0.125)
                bank_free[b] = x
                for tt in range(2):
                    lo, hi = sp[tt]
                    wi = WI[:, 8 * tt + h:8 * tt + h + 1]
                    if h == 0:
                        e = V.ts(SC[:, lo:hi], RL[0][:, lo:hi], wi, None, ALU.mult, None, x)
                    else:
                        e = V.stt(SC[:, lo:hi], RL[h % 2][:, lo:hi], wi, SC[:, lo:hi], ALU.mult, ALU.add, x, y)
                y = e
                rl_free[h % 2] = e
            y = V.tt(SC, SC, cst('cmask'), ALU.add, y)
            sel = [y]

            def later(f):
                def g_():
                    sel[0] = f(sel[0])
                    sel.append(None)
                return g_
            ops = []
            for tt in range(2):
                lo, hi = sp[tt]
                m8 = ST[:, 200 + 8 * tt:208 + 8 * tt]
                for r in range(8):
                    ops.append(later(lambda y, o_=m8, i_=SC[:, lo:hi]: V.op(lambda e: e.max(o_, i_), (y,))))
                    ops.append(later(lambda y, o_=SC[:, lo:hi], m_=m8: V.op(lambda e: e.match_replace(o_, m_, o_, TAKEN), (y,))))
            ops.append(later(lambda y: V.ts(SC, SC, TAKEN, None, ALU.is_equal, None, y)))
            ops.append(later(lambda y: V.tt(SC, SC, cst('c01'), ALU.mult, y)))
            ops.append(later(lambda y: V.ts(SC, SC, -1.0, -NEG, ALU.add, ALU.mult, y)))
            st.beside[:] = ops + st.beside

            mode_b(W, 2048, 4, ev_to(QQ), [0, 1], xt)
            mode_b(W, 3072, 4, ev_to(KK), [2, 3], xt)
            qk_t = q_t[-1]

            def ev_v3(h, tt, b, t):
                q_t.append(S.act(VV[:, tt, h * 512:h * 512 + 512], b, ACT.Copy, t))
                return q_t[-1]
            mode_a(W, 4096, 1, ev_v3, [4, 5], xt)
            while len(sel) <= len(ops):
                background(1)
            sel_t, v_t = sel[0], {0: q_t[-1]}
            outs = []
            steps = attention(8, lambda h: QQ[:, h, :], lambda h: KK[:, h, :], lambda h, s: VV[:, s, h * 128:h * 128 + 128],
                              lambda h: (slice(0, 128), OT[:, h, :], True), 1, 128 ** -0.5, True, TMP,
                              lambda h: qk_t, lambda h: v_t[h // 4], outs, mask=SC, mask_tok=lambda: sel_t,
                              banks=(0, 1, 2, 2, 3, 3))
            st.hooks = [[lambda: next(steps)], []] * 9 + [[lambda: next(steps)]] * 2

            def ev_v4(h, tt, b, t):
                v_t[1] = S.act(VV[:, tt, 512:1024], b, ACT.Copy, t)
                return v_t[1]
            mode_a(W, 4608, 1, ev_v4, [6, 7], xt)

            def ev_gate(dst, hv):
                def ev(j, b, t):
                    for m in range(2):
                        k = 2 * j + m
                        q_t.append(S.act(dst[:, k, :], b[:, m, :], ACT.Tanh, t, scale=0.5, bias=HV[:, hv + k:hv + k + 1]))
                    return q_t[-1]
                return ev
            mode_b(W, 5704, 4, ev_gate(GC, 16), [4, 5, 6, 7], xt)
            mode_b(W, 6728, 4, ev_gate(GA, 24), [4, 5, 6, 7], xt, tail=True)
            sa_ = split_act(OT.rearrange("p k t -> p (k t)"), outs)
            CVf = CV.rearrange("p k t -> p (k t)")
            mean, rst, SQC = KK[:, 0, :], KK[:, 1, :], Sb[:, :]
            cl = {}

            def conv_mean():
                while st.beside:
                    background(1)
                cv = conv_done + cp
                for k in range(KT):
                    t = E.mm(PS[4][:, 0:256], cst('ones'), CV[:, k, :], k == 0, k == 7, cv, bank_free[4], sig=(k == 7))
                x = V.ts(mean, PS[4][:, 0:256], 1.0 / C, None, ALU.mult, None, t, outs)
                bank_free[4] = x
                y = V.tt(CV, CV, mean.unsqueeze(1).broadcast_to([128, 8, 256]), ALU.subtract, x)
                cl['x'] = S.act(SQC, CVf, ACT.Square, y)

            def conv_var():
                for k in range(KT):
                    t = E.mm(PS[5][:, 0:256], cst('ones'), SQC[:, k * 256:k * 256 + 256], k == 0, k == 7, cl['x'],
                             bank_free[5], sig=(k == 7))
                y = V.ts(rst, PS[5][:, 0:256], 1.0 / C, EPS, ALU.mult, ALU.add, t)
                bank_free[5] = y
                y = S.act(rst, rst, ACT.Sqrt, y)
                y = V.op(lambda e: e.reciprocal(rst, rst), (y,))
                y = V.tt(CV, CV, rst.unsqueeze(1).broadcast_to([128, 8, 256]), ALU.mult, y)
                for k in range(KT):
                    cl['cv'] = S.act(CV[:, k, :], CV[:, k, :], ACT.Silu, y, scale=vec('cln_g', k), bias=vec('cln_b', k))
            gm = []

            def ev_mul(dst):
                def ev(j, b, t):
                    d = dst[:, 2 * j:2 * j + 2, :]
                    gm.append(V.stt(d, d, 1.0, b, ALU.add, ALU.mult, t))
                    return gm[-1]
                return ev
            st.hooks = [[], [], [conv_mean], [], [conv_var]]
            mode_b(a['w_attn_out'], 0, 4, ev_mul(GA), [0, 1], sa_, tail=True)
            sa_ = split_act(CVf, cl['cv'])

            def ev_sum(j, b, t):
                d = GC[:, 2 * j:2 * j + 2, :]
                x = V.stt(d, d, 1.0, b, ALU.add, ALU.mult, t)
                d2 = GA[:, 2 * j:2 * j + 2, :]
                gm.append(V.tt(d2, d2, d, ALU.add, x))
                return x
            mode_b(a['w_conv_out'], 0, 4, ev_sum, [2, 3], sa_, tail=True)
            sa_ = split_act(GA.rearrange("p k t -> p (k t)"), gm[-1], 0.5)

            def add_h(h, tt, b, t):
                hs = H[:, tt, h * 512:h * 512 + 512]
                hx.append(V.tt(hs, hs, b, ALU.add, t))
                hsum[0](tt, h, hx[-1])
                return hx[-1]
            hx = []
            hsum = [rms_sums(H)]
            mode_a(a['w_mix_out'], 0, 2, add_h, [4, 6, 5, 7], sa_, tail=True)

            nrm = rms_scale(H)
            xt = to_chan(S1, XT, nrm, [0, 1, 2, 3], 'nx')
            QX = QQ
            outs, qx_t = [], []

            def ev_qx(j, b, t):
                qx_t.append(S.act(QX[:, 2 * j:2 * j + 2, :], b, ACT.Copy, t))
                return qx_t[-1]
            cross = attention(4, lambda h: QX[:, h, :], lambda h: KX[:, h, :], lambda h, s: VX[:, s, h * 128:h * 128 + 128],
                              lambda h: (slice(0, 128), OT[:, h, :], True), 1, 128 ** -0.5, False, TMP,
                              lambda h: qx_t[h // 2], lambda h: None, outs)
            st.hooks = [[], [], [], [lambda: next(cross)]]
            mode_b(a['wx_q'], 0, 2, ev_qx, [6, 7], xt, tail=True)
            for _ in cross:
                pass
            sa_ = split_act(OT.rearrange("p k t -> p (k t)"), outs, n=2)
            hsum[0] = rms_sums(H)
            mode_a(a['wx_o'], 0, 2, add_h, [4, 6, 5, 7], sa_, nk=4, tail=True)
            nrm = rms_scale(H)
            x1 = to_chan(S1, XT, nrm, [0, 1, 2, 3], 'nffn')
            t = ffn(a['w_ff1'], a['w_ff2'], 16, False, x1)
            pc = load((lambda r: r[:, 0:1024], a['nfin'].broadcast_to([128, 1024])), tail=True)
            hx = []
            hsum[0] = rms_sums(H)
            for tt in range(2):
                for h in range(2):
                    add_h(h, tt, PS[4 + 2 * tt + h][:, :], t[2 * tt + h])
            nrm = rms_scale(H)
            for tt in range(2):
                for h in range(2):
                    sl = slice(h * 512, h * 512 + 512)
                    q = G if (tt, h) == (1, 1) else V
                    fin = q.tt(S1[:, tt, sl], S1[:, tt, sl], pc.ap[:, sl], ALU.mult, nrm, pc.tok)
                    s_out.dma(D, out[0, tt * 128:tt * 128 + 128, sl], S1[:, tt, sl], fin)
            D.wait((s_out.sem, s_out.v))

        for dry in (True, False):
            st.hooks, st.limit, st.hold, st.low = [], 10 ** 6, False, V
            run()
            if dry:
                st.plan = st.spec
                st.at = 0
                for q in (V, S, G, E, D):
                    q.reset()
                for c in (s_c, s_v, s_m, s_x, s_io, s_out):
                    c.v = 0
                bank_free[:] = [None] * 8

        block = ctx.enter_context(nc.Block())

        @block.vector
        def _(e):
            for f in V.items:
                f(e)

        @block.scalar
        def _(e):
            for f in S.items:
                f(e)

        @block.gpsimd
        def _(e):
            for f in G.items:
                f(e)

        @block.tensor
        def _(e):
            for f in E.items:
                f(e)

        @block.sync
        def _(e):
            for f in D.items:
                f(e)


def vectors(i):
    g = {'w0h': i['rwkv_w0'][0], 'a0h': i['rwkv_a0'][0], 'k_k': i['rwkv_k_k'][0], 'k_a': i['rwkv_k_a'][0],
         'r_k': i['rwkv_r_k'][0].reshape(-1), 'conv_b': i['conv_b_2'][0], 'cln_g': i['conv_ln_g_2'][0],
         'cln_b': i['conv_ln_b_2'][0], 'nmix': i['norm_mix_g_2'][0], 'nx': i['norm_x_g_2'][0],
         'nmem': i['norm_mem_g_2'][0], 'nffn': i['norm_ffn_g_2'][0], 'bgc': i['b_gate_2'][0, 0:C],
         'bga': i['b_gate_2'][0, C:2 * C]}
    for n in range(6):
        g[f'mu{n}'] = i['rwkv_mu'][0, n]
    for n in range(31):
        g[f'cw{n}'] = i['conv_w_2'][0, n]
    for l in range(2):
        g[f'mixg{l}'], g[f'mixb{l}'] = i['ln_mix_g'][l], i['ln_mix_b'][l]
        g[f'ffng{l}'], g[f'ffnb{l}'] = i['ln_ffn_g'][l], i['ln_ffn_b'][l]
    return np.ascontiguousarray(np.concatenate([g[n].reshape(8, 128).T for n in VECS], 1))


def kernel(**inputs):
    import numpy as _np
    import concourse.bacc as _bacc
    from concourse import mybir as _mybir
    from concourse.bass_utils import run_bass_kernel_spmd as _run

    i = {k: _np.asarray(v) for k, v in inputs.items()}
    arrays = {
        'cst': constants(), 'vec': vectors(i), 'xT': i['x'][0].T, 'x': i['x'][0], 'mem': i['mem_2'][0],
        'w_rkv': i['rwkv_w_rkv'][0], 'w1': i['rwkv_w1'][0], 'a1': i['rwkv_a1'][0], 'g1': i['rwkv_g1'][0],
        'w2': i['rwkv_w2'][0], 'a2': i['rwkv_a2'][0], 'g2': i['rwkv_g2'][0], 'gn_g': i['rwkv_gn_g'],
        'gn_b': i['rwkv_gn_b'], 'w_o': i['rwkv_w_o'][0], 'moba_w_qkv': i['moba_w_qkv'][0],
        'moba_w_o': i['moba_w_o'][0], 'ffn_w_in': i['ffn_w_in'], 'ffn_w_down': i['ffn_w_down'],
        'lnmg': i['ln_mix_g'], 'lnmb': i['ln_mix_b'], 'lnfg': i['ln_ffn_g'], 'lnfb': i['ln_ffn_b'],
        'w_in2': i['w_in_2'][0], 'w_conv_out': i['w_conv_out_2'][0], 'w_attn_out': i['w_attn_out_2'][0],
        'w_mix_out': i['w_mix_out_2'][0], 'wx_q': i['wx_q_2'][0], 'wx_kv': i['wx_kv_2'][0], 'wx_o': i['wx_o_2'][0],
        'w_ff1': i['w_ff1_2'][0], 'w_ff2': i['w_ff2_2'][0], 'nfin': i['norm_final_g_2'].reshape(1, C),
    }
    nc = _bacc.Bacc("TRN2", target_bir_lowering=False, num_devices=1)
    feed, aps = {}, {}
    for name, v in arrays.items():
        v = _np.ascontiguousarray(v)
        feed[f"in_{name}"] = v
        aps[name] = nc.dram_tensor(f"in_{name}", v.shape, _mybir.dt.from_np(v.dtype), kind="ExternalInput").ap()
    out = nc.dram_tensor("out_y", (1, T, C), F32, kind="ExternalOutput").ap()
    build(nc, aps, out)
    r = _run(nc, [feed], core_ids=[0])
    return r.results[0]["out_y"]
```
